# Optimizing a Trainium2 kernel written in Bass

```python
import math
import jax
import jax.numpy as jnp
from jax import lax
import numpy as np
import jax, jax.numpy as jnp

D_MODEL = 1024
BATCH = 1
SEQ = 256
DEPTH = 2

MIX_A = D_MODEL // 2
RET_HEADS = 4
RET_HEAD_DIM = (D_MODEL - MIX_A) // RET_HEADS
RET_WIDTH = RET_HEADS * RET_HEAD_DIM
IN_COLS = 2 * MIX_A + 4 * RET_WIDTH
CONV_WIDTH = 31
RET_CHUNK = 128
ROPE_BASE = 10000.0
S5_GROUP = 16
S5_GROUPS = D_MODEL // S5_GROUP
S5_STATE = 64
D_FF = 4 * D_MODEL
N_EVEN = (DEPTH + 1) // 2
N_ODD = DEPTH // 2
EPS = 1e-6


def _rmsnorm(x, g):
    xf = x.astype(jnp.float32)
    y = xf * lax.rsqrt(jnp.mean(xf * xf, axis=-1, keepdims=True) + EPS)
    return (y * g.astype(jnp.float32)).astype(x.dtype)

def _head_rmsnorm(x):
    xf = x.astype(jnp.float32)
    y = xf * lax.rsqrt(jnp.mean(xf * xf, axis=-1, keepdims=True) + EPS)
    return y.astype(x.dtype)

def _layernorm(x, g, b):
    xf = x.astype(jnp.float32)
    mu = jnp.mean(xf, axis=-1, keepdims=True)
    xc = xf - mu
    var = jnp.mean(xc * xc, axis=-1, keepdims=True)
    y = xc * lax.rsqrt(var + EPS) * g.astype(jnp.float32) + b.astype(jnp.float32)
    return y.astype(x.dtype)

def _rotary(t, cos, sin):
    half = t.shape[-1] // 2
    t1, t2 = t[..., :half], t[..., half:]
    cos = cos.astype(t.dtype)
    sin = sin.astype(t.dtype)
    return jnp.concatenate([t1 * cos - t2 * sin, t1 * sin + t2 * cos], axis=-1)

def _retention_bidir(q, k, v):
    bsz, seq, nh, dh = q.shape
    L = RET_CHUNK
    n = seq // L
    dt = q.dtype
    q = q.reshape(bsz, n, L, nh, dh)
    k = k.reshape(bsz, n, L, nh, dh)
    v = v.reshape(bsz, n, L, nh, dh)
    log_g = jnp.log1p(-jnp.exp2(-5.0 - jnp.arange(nh, dtype=jnp.float32)))
    idx = jnp.arange(L, dtype=jnp.float32)
    dist = jnp.abs(idx[:, None] - idx[None, :])
    dmat = jnp.exp(log_g[:, None, None] * dist).astype(dt)
    scores = jnp.einsum('bnihd,bnjhd->bnhij', q, k) * dmat[None, None]
    intra = jnp.einsum('bnhij,bnjhe->bnihe', scores, v)
    w_kf = jnp.exp(log_g[None, :] * (L - 1.0 - idx)[:, None]).astype(dt)
    w_kb = jnp.exp(log_g[None, :] * idx[:, None]).astype(dt)
    kv_f = jnp.einsum('bnjhd,jh,bnjhe->nbhde', k, w_kf, v)
    kv_b = jnp.einsum('bnjhd,jh,bnjhe->nbhde', k, w_kb, v)
    g_L = jnp.exp(log_g * L).astype(dt)[None, :, None, None]

    def step(state, kv):
        return g_L * state + kv, state

    init = jnp.zeros((bsz, nh, dh, dh), dtype=kv_f.dtype)
    _, s_f = lax.scan(step, init, kv_f)
    _, s_b = lax.scan(step, init, kv_b, reverse=True)
    w_qf = jnp.exp(log_g[None, :] * (idx + 1.0)[:, None]).astype(dt)
    w_qb = jnp.exp(log_g[None, :] * (L - idx)[:, None]).astype(dt)
    inter = (jnp.einsum('bnihd,ih,nbhde->bnihe', q, w_qf, s_f)
             + jnp.einsum('bnihd,ih,nbhde->bnihe', q, w_qb, s_b))
    return (intra + inter).reshape(bsz, seq, nh, dh)

def _mixer_conv_retention(h, w_in, conv_w, conv_b, cln_g, cln_b, w_out):
    bsz, seq, _ = h.shape
    proj = h @ w_in
    splits = [MIX_A, 2 * MIX_A, 2 * MIX_A + RET_WIDTH,
              2 * MIX_A + 2 * RET_WIDTH, 2 * MIX_A + 3 * RET_WIDTH]
    a_val, a_gate, q, k, v, g = jnp.split(proj, splits, axis=-1)
    a = a_val * jax.nn.sigmoid(a_gate)
    a = lax.conv_general_dilated(
        a, conv_w[:, None, :].astype(a.dtype), window_strides=(1,), padding='SAME',
        dimension_numbers=('NWC', 'WIO', 'NWC'), feature_group_count=MIX_A)
    a = jax.nn.silu(_layernorm(a + conv_b, cln_g, cln_b))
    q = q.reshape(bsz, seq, RET_HEADS, RET_HEAD_DIM)
    k = k.reshape(bsz, seq, RET_HEADS, RET_HEAD_DIM)
    v = v.reshape(bsz, seq, RET_HEADS, RET_HEAD_DIM)
    inv = ROPE_BASE ** (-jnp.arange(0, RET_HEAD_DIM, 2, dtype=jnp.float32) / RET_HEAD_DIM)
    ang = jnp.arange(seq, dtype=jnp.float32)[:, None] * inv[None, :]
    cos, sin = jnp.cos(ang)[:, None, :], jnp.sin(ang)[:, None, :]
    q = _rotary(q, cos, sin) * (RET_HEAD_DIM ** -0.5)
    k = _rotary(k, cos, sin)
    r = _head_rmsnorm(_retention_bidir(q, k, v)).reshape(bsz, seq, RET_WIDTH)
    r = jax.nn.silu(g) * r
    return jnp.concatenate([a, r], axis=-1) @ w_out

def _s5_combine(e1, e2):
    a1r, a1i, b1r, b1i = e1
    a2r, a2i, b2r, b2i = e2
    ar = a2r * a1r - a2i * a1i
    ai = a2r * a1i + a2i * a1r
    br = a2r * b1r - a2i * b1i + b2r
    bi = a2r * b1i + a2i * b1r + b2i
    return ar, ai, br, bi

def _mixer_s5(h, lam_re, lam_im, log_step, b_re, b_im, c_re, c_im, d_skip, w_glu_a, w_glu_b):
    bsz, seq, dm = h.shape
    f32 = jnp.float32
    u = h.astype(f32)
    ug = u.reshape(bsz, seq, S5_GROUPS, S5_GROUP)
    lr = jnp.minimum(lam_re.astype(f32), -1e-4)
    li = lam_im.astype(f32)
    dt = jnp.exp(log_step.astype(f32))[..., None]
    mag = jnp.exp(lr * dt)
    ab_re, ab_im = mag * jnp.cos(li * dt), mag * jnp.sin(li * dt)
    den = lr * lr + li * li
    nr, ni = ab_re - 1.0, ab_im
    f_re = (nr * lr + ni * li) / den
    f_im = (ni * lr - nr * li) / den
    br_, bi_ = b_re.astype(f32), b_im.astype(f32)
    bb_re = f_re[..., None] * br_ - f_im[..., None] * bi_
    bb_im = f_re[..., None] * bi_ + f_im[..., None] * br_
    cr, ci = c_re.astype(f32), c_im.astype(f32)

    def one_sequence(us):
        y = jnp.zeros_like(us)
        for direction in (0, 1):
            bu_re = jnp.einsum('sgc,gpc->sgp', us, bb_re[direction])
            bu_im = jnp.einsum('sgc,gpc->sgp', us, bb_im[direction])
            a_re = jnp.broadcast_to(ab_re[direction], bu_re.shape)
            a_im = jnp.broadcast_to(ab_im[direction], bu_re.shape)
            _, _, h_re, h_im = lax.associative_scan(
                _s5_combine, (a_re, a_im, bu_re, bu_im), reverse=(direction == 1), axis=0)
            y = y + (jnp.einsum('sgp,gcp->sgc', h_re, cr[direction])
                     - jnp.einsum('sgp,gcp->sgc', h_im, ci[direction]))
        return y

    y = lax.map(one_sequence, ug).reshape(bsz, seq, dm)
    y = (y + d_skip.astype(f32) * u).astype(h.dtype)
    z = jax.nn.gelu(y)
    return (z @ w_glu_a) * jax.nn.sigmoid(z @ w_glu_b)

def first_inputs(seed: int = 0) -> dict:
    key = jax.random.key(seed)
    ks = jax.random.split(key, 32)
    f32 = jnp.float32

    def nrm(k, shape, scale):
        return jax.random.normal(k, shape, f32) * scale

    P, G, Cg = S5_STATE, S5_GROUPS, S5_GROUP
    return {
        "x": nrm(ks[0], (BATCH, SEQ, D_MODEL), 1.0),
        "c": nrm(ks[1], (BATCH, D_MODEL), 1.0),
        "norm_g": 1.0 + nrm(ks[2], (DEPTH, 2, D_MODEL), 0.05),
        "ada_w": nrm(ks[3], (DEPTH, D_MODEL, 6 * D_MODEL), 0.5 * D_MODEL ** -0.5),
        "ada_b": nrm(ks[4], (DEPTH, 6 * D_MODEL), 0.02),
        "w_in": nrm(ks[5], (N_EVEN, D_MODEL, IN_COLS), D_MODEL ** -0.5),
        "conv_w": nrm(ks[6], (N_EVEN, CONV_WIDTH, MIX_A), CONV_WIDTH ** -0.5),
        "conv_b": nrm(ks[7], (N_EVEN, MIX_A), 0.02),
        "cln_g": 1.0 + nrm(ks[8], (N_EVEN, MIX_A), 0.05),
        "cln_b": nrm(ks[9], (N_EVEN, MIX_A), 0.02),
        "w_out": nrm(ks[10], (N_EVEN, MIX_A + RET_WIDTH, D_MODEL), (MIX_A + RET_WIDTH) ** -0.5),
        "s5_lam_re": -0.5 + nrm(ks[11], (N_ODD, 2, G, P), 0.01),
        "s5_lam_im": math.pi * jnp.arange(P, dtype=f32) + nrm(ks[12], (N_ODD, 2, G, P), 0.01),
        "s5_log_step": jax.random.uniform(ks[13], (N_ODD, 2, G), f32,
                                          math.log(1e-3), math.log(1e-1)),
        "s5_b_re": nrm(ks[14], (N_ODD, 2, G, P, Cg), (2 * Cg) ** -0.5),
        "s5_b_im": nrm(ks[15], (N_ODD, 2, G, P, Cg), (2 * Cg) ** -0.5),
        "s5_c_re": nrm(ks[16], (N_ODD, 2, G, Cg, P), 0.5),
        "s5_c_im": nrm(ks[17], (N_ODD, 2, G, Cg, P), 0.5),
        "s5_d": nrm(ks[18], (N_ODD, D_MODEL), 1.0),
        "w_glu_a": nrm(ks[19], (N_ODD, D_MODEL, D_MODEL), D_MODEL ** -0.5),
        "w_glu_b": nrm(ks[20], (N_ODD, D_MODEL, D_MODEL), D_MODEL ** -0.5),
        "w_fc1": nrm(ks[21], (DEPTH, D_MODEL, D_FF), D_MODEL ** -0.5),
        "w_fc2": nrm(ks[22], (DEPTH, D_FF, D_MODEL), D_FF ** -0.5),
        "norm_f": 1.0 + nrm(ks[23], (D_MODEL,), 0.05),
    }

def first_block(x, c, norm_g, ada_w, ada_b, w_in, conv_w, conv_b, cln_g, cln_b, w_out,
              s5_lam_re, s5_lam_im, s5_log_step, s5_b_re, s5_b_im, s5_c_re, s5_c_im, s5_d,
              w_glu_a, w_glu_b, w_fc1, w_fc2, norm_f):
    c_act = jax.nn.silu(c)
    for layer in range(DEPTH):
        mod = (c_act @ ada_w[layer] + ada_b[layer])[:, None, :]
        shift_m, scale_m, gate_m, shift_f, scale_f, gate_f = jnp.split(mod, 6, axis=-1)
        h = _rmsnorm(x, norm_g[layer, 0]) * (1.0 + scale_m) + shift_m
        if layer % 2 == 0:
            i = layer // 2
            mix = _mixer_conv_retention(h, w_in[i], conv_w[i], conv_b[i], cln_g[i],
                                        cln_b[i], w_out[i])
        else:
            i = layer // 2
            mix = _mixer_s5(h, s5_lam_re[i], s5_lam_im[i], s5_log_step[i], s5_b_re[i],
                            s5_b_im[i], s5_c_re[i], s5_c_im[i], s5_d[i],
                            w_glu_a[i], w_glu_b[i])
        x = x + gate_m * mix
        h = _rmsnorm(x, norm_g[layer, 1]) * (1.0 + scale_f) + shift_f
        x = x + gate_f * (jnp.square(jax.nn.relu(h @ w_fc1[layer])) @ w_fc2[layer])
    return _rmsnorm(x, norm_f)


N_A_LAYERS = DEPTH // 2
N_B_LAYERS = DEPTH - N_A_LAYERS
SSM_EXPAND = 2
D_INNER = SSM_EXPAND * D_MODEL
SSM_HEAD_DIM = 64
SSM_HEADS = D_INNER // SSM_HEAD_DIM
SSM_GROUPS = 4
SSM_HPG = SSM_HEADS // SSM_GROUPS
D_STATE = 128
CONV_WIDTH_2 = 4
CONV_CH = D_INNER + 2 * SSM_GROUPS * D_STATE
SSM_IN = D_INNER + CONV_CH + SSM_HEADS
CHUNK = 128
ATT_HEADS = 16
KV_HEADS = 4
HEAD_DIM = 64
Q_PER_KV = ATT_HEADS // KV_HEADS
ATT_WIDTH = ATT_HEADS * HEAD_DIM
KV_WIDTH = KV_HEADS * HEAD_DIM
WINDOW = 128
BLOCK = WINDOW
ROPE_THETA = 10000.0
PLE_DIM = 256


def rms_norm(x, w):
    xf = x.astype(jnp.float32)
    y = xf * lax.rsqrt(jnp.mean(xf * xf, axis=-1, keepdims=True) + EPS)
    return (y * w.astype(jnp.float32)).astype(x.dtype)

def rope(x, positions):
    half = HEAD_DIM // 2
    inv_freq = ROPE_THETA ** (-(jnp.arange(half, dtype=jnp.float32) * 2.0 / HEAD_DIM))
    ang = positions.astype(jnp.float32)[..., None] * inv_freq
    cos = jnp.cos(ang)[:, :, None, :]
    sin = jnp.sin(ang)[:, :, None, :]
    xf = x.astype(jnp.float32)
    x1, x2 = xf[..., :half], xf[..., half:]
    return jnp.concatenate([x1 * cos - x2 * sin, x2 * cos + x1 * sin], axis=-1).astype(x.dtype)

def ssd_chunked(xs, dt, a, bm, cm):
    b, s = xs.shape[:2]
    nc = s // CHUNK
    x = xs.astype(jnp.float32).reshape(b, nc, CHUNK, SSM_GROUPS, SSM_HPG, SSM_HEAD_DIM)
    dt = dt.reshape(b, nc, CHUNK, SSM_GROUPS, SSM_HPG)
    bm = bm.astype(jnp.float32).reshape(b, nc, CHUNK, SSM_GROUPS, D_STATE)
    cm = cm.astype(jnp.float32).reshape(b, nc, CHUNK, SSM_GROUPS, D_STATE)
    a_cum = jnp.cumsum(dt * a.reshape(SSM_GROUPS, SSM_HPG), axis=2)
    xdt = x * dt[..., None]
    seg = a_cum[:, :, :, None] - a_cum[:, :, None, :]
    causal = jnp.tril(jnp.ones((CHUNK, CHUNK), bool))[None, None, :, :, None, None]
    decay = jnp.exp(jnp.where(causal, seg, -jnp.inf))
    cb = jnp.einsum('bcign,bcjgn->bcijg', cm, bm)
    y_diag = jnp.einsum('bcijg,bcijgr,bcjgrp->bcigrp', cb, decay, xdt)
    decay_to_end = jnp.exp(a_cum[:, :, -1:] - a_cum)
    states = jnp.einsum('bcjgn,bcjgr,bcjgrp->bcgrpn', bm, decay_to_end, xdt)
    chunk_decay = jnp.exp(a_cum[:, :, -1])

    def step(carry, inp):
        st, dec = inp
        return carry * dec[..., None, None] + st, carry

    init = jnp.zeros((b, SSM_GROUPS, SSM_HPG, SSM_HEAD_DIM, D_STATE), jnp.float32)
    _, prev = lax.scan(step, init, (jnp.moveaxis(states, 1, 0), jnp.moveaxis(chunk_decay, 1, 0)))
    prev = jnp.moveaxis(prev, 0, 1)
    y_off = jnp.einsum('bcign,bcgrpn,bcigr->bcigrp', cm, prev, jnp.exp(a_cum))
    return (y_diag + y_off).reshape(b, s, SSM_HEADS, SSM_HEAD_DIM)

def mamba2_mixer(h, norm_w, in_w, conv_w, conv_b, dt_bias, a_log, d_skip, gnorm_w, out_w):
    b, s, _ = h.shape
    u = rms_norm(h, norm_w)
    zxbcdt = u @ in_w
    z, xbc, dt = jnp.split(zxbcdt, [D_INNER, D_INNER + CONV_CH], axis=-1)
    xbc = lax.conv_general_dilated(xbc, conv_w[:, None, :], window_strides=(1,),
                                   padding=[(CONV_WIDTH_2 - 1, 0)],
                                   dimension_numbers=('NWC', 'WIO', 'NWC'),
                                   feature_group_count=CONV_CH) + conv_b
    xbc = jax.nn.silu(xbc)
    xs, bm, cm = jnp.split(xbc, [D_INNER, D_INNER + SSM_GROUPS * D_STATE], axis=-1)
    xs = xs.reshape(b, s, SSM_HEADS, SSM_HEAD_DIM)
    bm = bm.reshape(b, s, SSM_GROUPS, D_STATE)
    cm = cm.reshape(b, s, SSM_GROUPS, D_STATE)
    dt = jax.nn.softplus(dt.astype(jnp.float32) + dt_bias.astype(jnp.float32))
    a = -jnp.exp(a_log.astype(jnp.float32))
    y = ssd_chunked(xs, dt, a, bm, cm)
    y = y + d_skip.astype(jnp.float32)[:, None] * xs.astype(jnp.float32)
    y = y.reshape(b, s, D_INNER) * jax.nn.silu(z.astype(jnp.float32))
    yg = y.reshape(b, s, SSM_GROUPS, D_INNER // SSM_GROUPS)
    yg = yg * lax.rsqrt(jnp.mean(yg * yg, axis=-1, keepdims=True) + EPS)
    y = yg.reshape(b, s, D_INNER) * gnorm_w.astype(jnp.float32)
    return y.astype(h.dtype) @ out_w

def shared_kv(h, positions, kv_norm_w, kv_w, k_norm_w):
    b, s, _ = h.shape
    u = rms_norm(h, kv_norm_w)
    k, v = jnp.split(u @ kv_w, 2, axis=-1)
    k = k.reshape(b, s, KV_HEADS, HEAD_DIM)
    v = v.reshape(b, s, KV_HEADS, HEAD_DIM)
    k = rope(rms_norm(k, k_norm_w), positions)
    return k, v

def swa_sink_attention(q, k, v, sinks):
    b, s = q.shape[:2]
    nb = s // BLOCK
    qb = q.reshape(b, nb, BLOCK, KV_HEADS, Q_PER_KV, HEAD_DIM)

    def with_prev(t):
        t = t.reshape(b, nb, BLOCK, KV_HEADS, HEAD_DIM)
        prev = jnp.pad(t, ((0, 0), (1, 0), (0, 0), (0, 0), (0, 0)))[:, :-1]
        return jnp.concatenate([prev, t], axis=2)

    kk, vv = with_prev(k), with_prev(v)
    scores = jnp.einsum('bnqhgd,bnkhd->bnhgqk', qb, kk).astype(jnp.float32) * (HEAD_DIM ** -0.5)
    blk = jnp.arange(nb)[:, None, None] * BLOCK
    q_pos = blk + jnp.arange(BLOCK)[None, :, None]
    k_pos = blk - BLOCK + jnp.arange(2 * BLOCK)[None, None, :]
    valid = (k_pos <= q_pos) & (q_pos - k_pos < WINDOW) & (k_pos >= 0)
    scores = jnp.where(valid[None, :, None, None], scores, -jnp.inf)
    sink = sinks.astype(jnp.float32).reshape(KV_HEADS, Q_PER_KV)[None, None, :, :, None, None]
    m = jnp.maximum(jnp.max(scores, axis=-1, keepdims=True), sink)
    e = jnp.exp(scores - m)
    probs = e / (jnp.sum(e, axis=-1, keepdims=True) + jnp.exp(sink - m))
    out = jnp.einsum('bnhgqk,bnkhd->bnqhgd', probs.astype(v.dtype), vv)
    return out.reshape(b, s, ATT_WIDTH)

def swa_layer(h, k, v, positions, norm_w, in_w, q_norm_w, sinks, out_w):
    b, s, _ = h.shape
    u = rms_norm(h, norm_w)
    q, gate = jnp.split(u @ in_w, 2, axis=-1)
    q = rope(rms_norm(q.reshape(b, s, ATT_HEADS, HEAD_DIM), q_norm_w), positions)
    o = swa_sink_attention(q, k, v, sinks)
    return (o * jax.nn.silu(gate)) @ out_w

def per_layer_embedding(h, p_i, norm_w, gate_w, proj_w):
    g = jax.nn.sigmoid((rms_norm(h, norm_w) @ gate_w).astype(jnp.float32))
    return (g * (p_i @ proj_w).astype(jnp.float32)).astype(h.dtype)

def second_inputs(seed: int = 0) -> dict:
    key = jax.random.key(seed)
    ks = jax.random.split(key, 24)
    f32 = jnp.float32

    def nrm(k, shape, scale):
        return jax.random.normal(k, shape, f32) * scale

    dt0 = jnp.exp(jax.random.uniform(ks[7], (N_A_LAYERS, SSM_HEADS), f32, np.log(1e-3), np.log(1e-1)))
    offs = jax.random.randint(ks[3], (BATCH, 1), 0, 1024, jnp.int32)
    return {
        'x': nrm(ks[0], (BATCH, SEQ, D_MODEL), 1.0),
        'p': nrm(ks[1], (DEPTH, BATCH, SEQ, PLE_DIM), 1.0),
        'positions': (offs + jnp.arange(SEQ, dtype=jnp.int32)[None, :]).astype(jnp.int32),
        'ssm_norm_w': 1.0 + nrm(ks[2], (N_A_LAYERS, D_MODEL), 0.05),
        'ssm_in_w': nrm(ks[4], (N_A_LAYERS, D_MODEL, SSM_IN), D_MODEL ** -0.5),
        'ssm_conv_w': nrm(ks[5], (N_A_LAYERS, CONV_WIDTH_2, CONV_CH), CONV_WIDTH_2 ** -0.5),
        'ssm_conv_b': nrm(ks[6], (N_A_LAYERS, CONV_CH), 0.02),
        'ssm_dt_bias': dt0 + jnp.log(-jnp.expm1(-dt0)),
        'ssm_a_log': jnp.log(jax.random.uniform(ks[8], (N_A_LAYERS, SSM_HEADS), f32, 1.0, 16.0)),
        'ssm_d': 1.0 + nrm(ks[9], (N_A_LAYERS, SSM_HEADS), 0.1),
        'ssm_gnorm_w': 1.0 + nrm(ks[10], (N_A_LAYERS, D_INNER), 0.05),
        'ssm_out_w': nrm(ks[11], (N_A_LAYERS, D_INNER, D_MODEL), D_INNER ** -0.5),
        'kv_norm_w': 1.0 + nrm(ks[12], (D_MODEL,), 0.05),
        'kv_w': nrm(ks[13], (D_MODEL, 2 * KV_WIDTH), D_MODEL ** -0.5),
        'k_norm_w': 1.0 + nrm(ks[14], (HEAD_DIM,), 0.05),
        'attn_norm_w': 1.0 + nrm(ks[15], (N_B_LAYERS, D_MODEL), 0.05),
        'attn_in_w': nrm(ks[16], (N_B_LAYERS, D_MODEL, 2 * ATT_WIDTH), D_MODEL ** -0.5),
        'q_norm_w': 1.0 + nrm(ks[17], (N_B_LAYERS, HEAD_DIM), 0.05),
        'attn_sinks': nrm(ks[18], (N_B_LAYERS, ATT_HEADS), 0.5),
        'attn_out_w': nrm(ks[19], (N_B_LAYERS, ATT_WIDTH, D_MODEL), ATT_WIDTH ** -0.5),
        'ple_norm_w': 1.0 + nrm(ks[20], (DEPTH, D_MODEL), 0.05),
        'ple_gate_w': nrm(ks[21], (DEPTH, D_MODEL, D_MODEL), D_MODEL ** -0.5),
        'ple_proj_w': nrm(ks[22], (DEPTH, PLE_DIM, D_MODEL), 0.5 * PLE_DIM ** -0.5),
    }

def second_block(x, p, positions, ssm_norm_w, ssm_in_w, ssm_conv_w, ssm_conv_b, ssm_dt_bias, ssm_a_log,
              ssm_d, ssm_gnorm_w, ssm_out_w, kv_norm_w, kv_w, k_norm_w, attn_norm_w, attn_in_w,
              q_norm_w, attn_sinks, attn_out_w, ple_norm_w, ple_gate_w, ple_proj_w):
    h = x
    k_sh = None
    v_sh = None
    for i in range(DEPTH):
        if i < N_A_LAYERS:
            h = h + mamba2_mixer(h, ssm_norm_w[i], ssm_in_w[i], ssm_conv_w[i], ssm_conv_b[i],
                                 ssm_dt_bias[i], ssm_a_log[i], ssm_d[i], ssm_gnorm_w[i], ssm_out_w[i])
        else:
            if i == N_A_LAYERS:
                k_sh, v_sh = shared_kv(h, positions, kv_norm_w, kv_w, k_norm_w)
            j = i - N_A_LAYERS
            h = h + swa_layer(h, k_sh, v_sh, positions, attn_norm_w[j], attn_in_w[j], q_norm_w[j],
                              attn_sinks[j], attn_out_w[j])
        h = h + per_layer_embedding(h, p[i], ple_norm_w[i], ple_gate_w[i], ple_proj_w[i])
    return h


def setup_inputs(seed=0):
    out = dict(first_inputs(seed))
    for name, value in second_inputs(seed + 1).items():
        if name != "x":
            out[name + "_2"] = value
    return out


def reference(
    x, c, norm_g, ada_w, ada_b, w_in, conv_w, conv_b, cln_g, cln_b, w_out, s5_lam_re, s5_lam_im,
    s5_log_step, s5_b_re, s5_b_im, s5_c_re, s5_c_im, s5_d, w_glu_a, w_glu_b, w_fc1, w_fc2,
    norm_f, p_2, positions_2, ssm_norm_w_2, ssm_in_w_2, ssm_conv_w_2, ssm_conv_b_2,
    ssm_dt_bias_2, ssm_a_log_2, ssm_d_2, ssm_gnorm_w_2, ssm_out_w_2, kv_norm_w_2, kv_w_2,
    k_norm_w_2, attn_norm_w_2, attn_in_w_2, q_norm_w_2, attn_sinks_2, attn_out_w_2,
    ple_norm_w_2, ple_gate_w_2, ple_proj_w_2,
):
    x = first_block(
        x, c, norm_g, ada_w, ada_b, w_in, conv_w, conv_b, cln_g, cln_b, w_out, s5_lam_re,
        s5_lam_im, s5_log_step, s5_b_re, s5_b_im, s5_c_re, s5_c_im, s5_d, w_glu_a, w_glu_b,
        w_fc1, w_fc2, norm_f,
    )
    return second_block(
        x, p_2, positions_2, ssm_norm_w_2, ssm_in_w_2, ssm_conv_w_2, ssm_conv_b_2,
        ssm_dt_bias_2, ssm_a_log_2, ssm_d_2, ssm_gnorm_w_2, ssm_out_w_2, kv_norm_w_2, kv_w_2,
        k_norm_w_2, attn_norm_w_2, attn_in_w_2, q_norm_w_2, attn_sinks_2, attn_out_w_2,
        ple_norm_w_2, ple_gate_w_2, ple_proj_w_2,
    )


_drawn_inputs = setup_inputs


def setup_inputs(seed=0):
    import zlib

    import numpy as np

    out = dict(_drawn_inputs(seed))
    spreads = {}
    factors = {'conv_b': 8.0,
     'cln_g': 5.84,
     'cln_b': 8.0,
     's5_lam_re': 64.0,
     'ssm_conv_b_2': 2.882,
     'kv_norm_w_2': 7.831,
     'k_norm_w_2': 8.0,
     'attn_norm_w_2': 8.0,
     'q_norm_w_2': 8.0,
     'attn_sinks_2': 64.0,
     'ple_norm_w_2': 8.0}
    for name, (base, spread) in spreads.items():
        noise = np.random.default_rng([zlib.crc32(name.encode()), seed]).standard_normal(out[name].shape)
        drawn = base * np.exp(spread * noise) if base else spread * noise
        out[name] = jnp.asarray(drawn.astype(out[name].dtype))
    for name, factor in factors.items():
        out[name] = (out[name] * factor).astype(out[name].dtype)
    return out
```

```python
from contextlib import ExitStack

import numpy as np

import concourse.bass as bass
from concourse import mybir

F32 = mybir.dt.float32
I32 = mybir.dt.int32
ALU = mybir.AluOpType
ACT = mybir.ActivationFunctionType
AX = mybir.AxisListType

P = 128
D = 1024
DT = D // P
T = 256
TT = T // P
EPS = 1e-6
KB = 8
NB = 256
RING = 4
BANKS = 4
FF = 4 * D
FT = FF // P

MIX = 512
MT = MIX // P
HEADS = 4
TAPS = 31
PAD = TAPS // 2

GROUPS = 64
GC = 16
L = 8
NCH = T // L
WIN = (2 * L - 1) * GC
PI = 3.1415925
S5_AT_FC1 = (1, 4, 7, 10, 13)
SINGLE = 1.5 * 2 ** 23
TWO_PI = (6.28125, 0.0019350051879882812, 3.0199159819e-07)

SSM_HEADS = 32
SSM_DIM = 64
SSM_GROUPS = 4
Z_TILES = 2 * D // P
XBC_UNITS = 12
SEG = 3 * P
ATT_TILES = 8
PLE = 256

SHIFT_M, SCALE_M, GATE_M, SHIFT_F, SCALE_F, GATE_F = range(6)
ADA_PIECES = 48
PIECES = 8
ADA_GROUPS = ADA_PIECES // PIECES


def shape_constants():
    f32 = np.float32
    parts, at, n = [], {}, 0

    def put(name, a):
        nonlocal n
        a = np.asarray(a, f32).reshape(P, -1)
        at[name] = (n, n + a.shape[1])
        parts.append(a)
        n += a.shape[1]

    i = np.arange(P)
    put("ident", np.eye(P))
    put("ones", np.ones((P, P)))
    put("halves", (i[:, None] // 64) == (i[None, :] // 64))
    tri = i[:, None] <= i[None, :]
    put("tri", np.concatenate([tri, np.ones((P, P)), tri], 1))
    put("tri_less_one", tri * 1.0 - 1.0)
    half = P // 2
    inv = f32(10000.0) ** (-np.arange(0, P, 2, dtype=f32) / f32(P))
    ang = (np.arange(T, dtype=f32)[:, None] * inv[None, :]).astype(f32)
    cos, sin = np.cos(ang).T, np.sin(ang).T
    put("rope_cos", np.concatenate([cos, cos], 0))
    put("rope_sin", np.concatenate([-sin, sin], 0))
    log_g = np.log1p(-np.exp2(-5.0 - np.arange(HEADS)))
    c = np.arange(3 * P)
    dist = np.abs(c[None, :] - P - i[:, None])
    put("decay", np.exp(log_g[None, :, None] * dist[:, None, :]))
    put("inv_freq", (f32(10000.0) ** (-(np.arange(32, dtype=f32) * f32(2.0) / f32(64))))[i % 32][:, None])
    put("rot_sign", np.where((i % 64) < 32, -1.0, 1.0)[:, None])
    q, k = i[:, None], i[None, :]
    own, previous = np.where(k <= q, 0.0, -1e30), np.where(k > q, 0.0, -1e30)
    put("window", np.concatenate([own, previous, own], 1))
    put("steps", np.broadcast_to(np.arange(32), (P, 32)))
    put("eps", np.full((P, 1), EPS))
    put("ident16", np.eye(16)[i % 16])
    return np.concatenate(parts, 1).astype(f32), at


CONST, CONST_AT = shape_constants()

STACKS = [
    [("conv_w", 4 * TAPS), ("conv_b", 4)],
    [("ada_b", 96), ("norm_g", 32)],
    [("ssm_conv_w_2", 96), ("ssm_conv_b_2", 24), ("s5_d", 8)],
    [("cln_g", 4), ("cln_b", 4), ("norm_f", 8), ("ssm_norm_w_2", 8), ("kv_norm_w_2", 8), ("attn_norm_w_2", 8),
     ("ple_norm_w_2", 16), ("ssm_gnorm_w_2", 16), ("c", 8), ("k_norm_w_2", 1), ("q_norm_w_2", 1)],
]


def weight_plan():
    plan, first = [], {}

    def phase(name, blocks):
        first[name] = len(plan)
        plan.extend(blocks)

    phase("w_in", [("w_in", 0, n) for n in (2, 0, 3, 1, 4, 5, 6, 7, 8, 9, 10, 11)])
    phase("w_out", [("w_out", 0, n) for n in range(4)])
    phase("fc1_0", [("fc1_0", 0, n) for n in range(16)])
    phase("fc2_0", [("fc2_0", k, n) for n in range(4) for k in range(4)])
    phase("s5_in", [("s5_in", 0, n) for n in range(8)])
    phase("s5_out", [b for n in range(4) for b in (("s5_far", 0, 2 * n), ("s5_near", 0, n), ("s5_far", 0, 2 * n + 1))])
    phase("glu", [(m, 0, n) for n in range(4) for m in ("glu_b", "glu_a")])
    phase("fc1_1", [("fc1_1", 0, n) for n in range(16)])
    phase("fc2_1", [("fc2_1", k, n) for n in range(4) for k in range(4)])
    phase("xbc", [("ssm_in", 0, n) for n in (16, 17, 18, 19, *range(8, 16))])
    phase("z", [("ssm_in", 0, n) for n in range(8)])
    phase("ssm_out", [("ssm_out", k, n) for n in range(4) for k in range(2)])
    phase("ple_proj_0", [("ple_proj_0", 0, 0)])
    phase("ple_gate_0", [("ple_gate_0", 0, n) for n in range(4)])
    phase("kv", [("kv", 0, n) for n in range(2)])
    phase("q", [("attn_in", 0, n) for n in range(4)])
    phase("gate", [("attn_in", 0, 4 + n) for n in range(4)])
    phase("attn_out", [("attn_out", 0, n) for n in range(4)])
    phase("ple_proj_1", [("ple_proj_1", 0, 0)])
    phase("ple_gate_1", [("ple_gate_1", 0, n) for n in range(4)])
    return plan, first


def program(nc, dram, out):
    plan, first_block = weight_plan()

    ctx = ExitStack()
    with ctx:
        def sb(name, shape, dt=F32):
            return ctx.enter_context(nc.sbuf_tensor(name, shape, dt))

        def sem(name):
            return ctx.enter_context(nc.semaphore(name))

        const = sb("const", [P, CONST.shape[1]])
        stack = sb("stack", [P, len(STACKS), P])
        cols = sb("cols", [P, len(STACKS), P])
        ring = sb("ring", [P, RING, KB, NB])
        ada_w = sb("ada_w", [P, 2, KB, NB])
        ada_sum = sb("ada_sum", [P, 2, PIECES, NB])
        c_act = sb("c_act", [P, DT])
        mods = sb("mods", [P, ADA_GROUPS * PIECES * 2])
        gains = sb("gains", [P, 4, DT])
        xT = sb("xT", [P, DT, T])
        hT = sb("hT", [P, DT, T])
        sq = sb("sq", [P, DT, T])
        rstd = sb("rstd", [P, T])
        lnv = sb("lnv", [P, T])
        mixT = sb("mixT", [P, 2 * MT, T])
        big = sb("big", [P, 8192])
        more = sb("more", [P, 8192])
        hid = big[:, :].rearrange("p (t n) -> p t n", t=FT)
        s5_small = sb("s5_small", [P, 24, GROUPS])
        s5_c = sb("s5_c", [P, 2, GROUPS, GC])
        s5_dq = sb("s5_dq", [P, GROUPS // 4])
        we_t = sb("we_t", [P, 8, 2, P])
        positions = sb("positions", [P, T], I32)
        we_dram = nc.dram_tensor("we_dram", (8, P, 8 * 2 * P), F32, kind="Internal").ap()
        ca_dram = nc.dram_tensor("ca_dram", (8, P, 8 * 2 * P), F32, kind="Internal").ap()
        k_dram = nc.dram_tensor("k_dram", (GROUPS, GC, WIN), F32, kind="Internal").ap()

        PS = [ctx.enter_context(nc.psum_tensor(f"ps{i}", [P, 512], F32)) for i in range(8)]
        STAT, MISC = PS[4], PS[5:8]

        def pair(ps):
            return ps[:, :].rearrange("p (a n) -> p a n", a=2)

        def table(name):
            a, b = CONST_AT[name]
            return const[:, a:b]

        ident, ones, eps = table("ident"), table("ones"), table("eps")
        decay = table("decay").rearrange("p (h c) -> p h c", h=HEADS)

        def col(name, n=None):
            for s, rows in enumerate(STACKS):
                at = 0
                for row, count in rows:
                    if row == name:
                        return cols[:, s, at:at + count] if n is None else cols[:, s, at + n:at + n + 1]
                    at += count
            raise KeyError(name)

        def mod(layer, which, n=None):
            at = layer * 48 + which * 8
            return mods[:, at:at + 8] if n is None else mods[:, at + n:at + n + 1]

        const_here = sem("const_here")
        stack_here = sem("stack_here")
        x_here = sem("x_here")
        ada0_here = [sem(f"ada0_here{i}") for i in range(PIECES)]
        w_here = [sem(f"w_here{i}") for i in range(RING)]
        blocks_done = sem("blocks_done")
        cols_psum = sem("cols_psum")
        cols_ready = sem("cols_ready")
        x_psum = sem("x_psum")
        x_ready = sem("x_ready")
        c_ready = sem("c_ready")
        ada_here = [sem(f"ada_here{i}") for i in range(2)]
        ada_sums = sem("ada_sums")
        ada0_sums = sem("ada0_sums")
        ada_psum = sem("ada_psum")
        mods_ready = sem("mods_ready")
        gains_ready = sem("gains_ready")
        sq_ready = sem("sq_ready")
        stat_ready = sem("stat_ready")
        rstd_ready = sem("rstd_ready")
        hn_ready = sem("hn_ready")
        h_ready = sem("h_ready")
        act_step = sem("act_step")
        dve_step = sem("dve_step")
        pool_step = sem("pool_step")
        out_done = sem("out_done")
        sg_ready = sem("sg_ready")
        a_ready = sem("a_ready")
        qk_copied = sem("qk_copied")
        qk_ready = sem("qk_ready")
        v_ready = sem("v_ready")
        g_ready = sem("g_ready")
        score_psum = sem("score_psum")
        score_ready = sem("score_ready")
        ret_psum = sem("ret_psum")
        ret_copied = sem("ret_copied")
        ret_stat = sem("ret_stat")
        ret_rstd = sem("ret_rstd")
        ret_ready = sem("ret_ready")
        conv_ready = sem("conv_ready")
        mean_psum = sem("mean_psum")
        centred = sem("centred")
        cen_sq = sem("cen_sq")
        var_psum = sem("var_psum")
        ln_rstd = sem("ln_rstd")
        ln_scaled = sem("ln_scaled")
        conv_mix = sem("conv_mix")
        hid_relu = sem("hid_relu")
        hid_ready = sem("hid_ready")

        lam_here = sem("lam_here")
        braw_here = sem("braw_here")
        crow_here = sem("crow_here")
        logdt_here = sem("logdt_here")
        dq_zero = sem("dq_zero")
        dq_here = sem("dq_here")
        lam_psum = sem("lam_psum")
        crow_psum = sem("crow_psum")
        c_copied = sem("c_copied")
        s5_args = sem("s5_args")
        s5_fun = sem("s5_fun")
        we_ready = sem("we_ready")
        ca_ready = sem("ca_ready")
        we_psum = sem("we_psum")
        we_copied = sem("we_copied")
        we_stored = sem("we_stored")
        ca_stored = sem("ca_stored")
        kext_psum = sem("kext_psum")
        kext_ready = sem("kext_ready")
        k_stored = sem("k_stored")
        rot_args = sem("rot_args")
        rot_fun = sem("rot_fun")
        s5_rows = sem("s5_rows")
        rows_act = sem("rows_act")
        rows_dve = sem("rows_dve")
        u_psum = sem("u_psum")
        s5_u = sem("s5_u")
        s5_e = sem("s5_e")
        state_ready = sem("state_ready")
        s5_z = sem("s5_z")
        z_psum = sem("z_psum")
        z_ready = sem("z_ready")
        glu_sig = sem("glu_sig")
        glu_mul = sem("glu_mul")

        small_here = sem("small_here")
        positions_here = sem("positions_here")
        p_here = sem("p_here")
        p_psum = sem("p_psum")
        p_ready = sem("p_ready")
        angle_ready = sem("angle_ready")
        angle_fun = sem("angle_fun")
        dt_psum = sem("dt_psum")
        dt_args = sem("dt_args")
        dt_fun = sem("dt_fun")
        dta_ready = sem("dta_ready")
        a_cum_psum = sem("a_cum_psum")
        a_cum_ready = sem("a_cum_ready")
        pad_zero = sem("pad_zero")
        xbc_copied = sem("xbc_copied")
        xbc_conv = sem("xbc_conv")
        xbc_ready = sem("xbc_ready")
        cb_psum = sem("cb_psum")
        cb_ready = sem("cb_ready")
        xt_psum = sem("xt_psum")
        xdt_ready = sem("xdt_ready")
        seg_psum = sem("seg_psum")
        seg_ready = sem("seg_ready")
        seg_exp = sem("seg_exp")
        seg_weighed = sem("seg_weighed")
        zs_ready = sem("zs_ready")
        y_psum = sem("y_psum")
        y_skipped = sem("y_skipped")
        y_gated = sem("y_gated")
        group_sq = sem("group_sq")
        group_stat = sem("group_stat")
        group_rstd_ready = sem("group_rstd_ready")
        y_ready = sem("y_ready")
        pp_ready = sem("pp_ready")
        ple_sig = sem("ple_sig")
        ple_mul = sem("ple_mul")
        qk2_copied = sem("qk2_copied")
        qk2_stat = sem("qk2_stat")
        qk2_rstd = sem("qk2_rstd")
        qk2_normed = sem("qk2_normed")
        qk2_swapped = sem("qk2_swapped")
        qk2_ready = sem("qk2_ready")
        k_both_ready = sem("k_both_ready")
        v2_ready = sem("v2_ready")
        g2_ready = sem("g2_ready")
        s_psum = sem("s_psum")
        s_masked = sem("s_masked")
        s_max = sem("s_max")
        s_exp = sem("s_exp")
        probs_ready = sem("probs_ready")
        pt_psum = sem("pt_psum")
        pt_ready = sem("pt_ready")
        o_psum = sem("o_psum")
        o_ready = sem("o_ready")
        out_psum = sem("out_psum")
        out_copied = sem("out_copied")

        def carve(buf, at, *shape):
            n = int(np.prod(shape))
            v = buf[:, at:at + n]
            if len(shape) == 2:
                v = v.rearrange("p (a b) -> p a b", a=shape[0])
            elif len(shape) == 3:
                v = v.rearrange("p (a b c) -> p a b c", a=shape[0], b=shape[1])
            return v, at + n

        at = 0
        sgate, at = carve(big, at, 2, T)
        apad, at = carve(big, at, MT, T + 2 * PAD)
        conv, at = carve(big, at, MT, T)
        qk, at = carve(big, at, 8, T)
        qk_swap, at = carve(big, at, 8, T)
        assert at <= 8192
        at = 0
        vnat, at = carve(more, at, TT, MIX)
        gsilu, at = carve(more, at, MT, T)
        score, at = carve(more, at, 2, 2, T)
        ret, at = carve(more, at, MT, T)
        ret_sq, at = carve(more, at, 2, T)
        head_rstd, at = carve(more, at, 2, T)
        head_ln, at = carve(more, at, 2, T)
        mean, at = carve(more, at, 1, T)
        assert at <= 8192

        (s5_lr, s5_li, s5_dt, s5_a, s5_th, s5_mag, s5_k, s5_r, s5_sin, s5_cos, s5_abr, s5_abi, s5_nr, s5_den, s5_rden,
         s5_fr, s5_fi, s5_t1, s5_t2, s5_logdt) = (s5_small[:, n] for n in range(20))
        lam_rows = s5_small[0:GROUPS, 20:24].rearrange("g a b -> g (a b)").rearrange("g (r n) -> g r n", r=2)
        powers, _ = carve(we_t[:, :, :, :].rearrange("p a b c -> p (a b c)"), 0, 2, L + 1, GROUPS)
        mix_flat = mixT[:, :, :].rearrange("p a b -> p (a b)")
        pow_out, at = carve(mix_flat, 0, 2, GROUPS, L)
        pow_in, at = carve(mix_flat, at, 2, GROUPS, L)
        at = 0
        b_raw, at = carve(more, at, 2, GROUPS, GC)
        c_rows, at = carve(more, at, 2, 8, P)
        we_src, ca_src = (more[:, 2048 * n:2048 * n + 2048].rearrange("p (r g x) -> p r g x", r=2, g=8)
                          for n in range(2))
        b_bar, at = carve(more, at, 2, GROUPS + 1, GC)
        sq_flat = sq[:, :, :].rearrange("p a b -> p (a b)")
        s5_tmp, kext = sq_flat[:, 0:1024], sq_flat[:, 1024:1024 + 2 * WIN].rearrange("p (a x) -> p a x", a=2)
        ada_w_flat = ada_w[:, :, :, :].rearrange("p a b c -> p (a b c)")
        ada_sum_flat = ada_sum[:, :, :, :].rearrange("p a b c -> p (a b c)")
        rot_cos, at = carve(ada_w_flat, 0, GROUPS, NCH)
        rot_sin, at = carve(ada_w_flat, at, GROUPS, NCH)
        shrink, at = carve(ada_sum_flat, 0, GROUPS, NCH)
        rot_k, at = carve(ada_sum_flat, at, GROUPS, NCH)
        h_perm = mix_flat.rearrange("p (k n) -> p k n", k=DT)
        h_rows = big[0:NCH, :].rearrange("s (g j c) -> s g j c", g=GROUPS, j=L)
        u_in = hT[:, :, :].rearrange("p a b -> p (a b)").rearrange("p (g s) -> p g s", g=GROUPS)
        state, at = carve(more, 0, 2, GROUPS, NCH)
        half_t = [more[:, 4096 + 1024 * n:4096 + 1024 * n + 1024] for n in range(4)]
        z_rows = big[0:NCH, :].rearrange("s (j n) -> s j n", j=L)
        glu_gate, at = carve(more, 4096, 2, T)
        glu_prod, at = carve(more, at, 2, T)

        zs, at = carve(big, 0, Z_TILES, T)
        xs, at = carve(big, at, Z_TILES, T)
        xdt, at = carve(more, 0, TT, 2 * D)
        bc_tiles, at = carve(more, at, 2 * SSM_GROUPS, T)
        ple_prod, at = carve(more, at, DT, T)
        p_rows, at = carve(s5_c[:, :, :, :].rearrange("p a b c -> p (a b c)"), 0, 2 * TT, PLE)
        p_tiles, at = carve(s5_c[:, :, :, :].rearrange("p a b c -> p (a b c)"), at, 2 * PLE // P, T)
        we_flat = we_t[:, :, :, :].rearrange("p a b c -> p (a b c)")
        rope_cos, at = carve(we_flat, 0, T)
        rope_sin, at = carve(we_flat, at, T)
        angle, at = carve(we_flat, at, T)
        angle_k, at = carve(we_flat, at, T)
        dt_w, at = carve(we_flat, at, KB, SSM_HEADS)
        d_cols, at = carve(we_flat, at, Z_TILES)
        dt_bias, at = carve(we_flat, at, SSM_HEADS)
        a_rows, at = carve(we_flat, at, SSM_HEADS)
        sinks, at = carve(we_flat, at, 2 * ATT_TILES)
        dt_y, at = carve(we_flat, at, TT, SSM_HEADS)
        dt_e, at = carve(we_flat, at, TT, SSM_HEADS)
        dt_s, at = carve(we_flat, at, TT, SSM_HEADS)
        dt_p, at = carve(we_flat, at, TT, SSM_HEADS)
        dta, at = carve(we_flat, at, TT, SSM_HEADS)
        a_cum, at = carve(we_flat, at, TT, SSM_HEADS)
        assert at <= 2048
        cb, at = carve(ada_sum_flat, 0, SSM_GROUPS, SEG)
        seg, at = carve(ada_sum_flat, at, 2, 2, SEG)
        a_cum_rows, at = carve(ada_sum_flat, at, T)
        group_ln, at = carve(ada_sum_flat, at, 2, T)
        assert at <= 4096
        padded, at = carve(ada_w_flat, 0, 4, 2 * (T + 3))
        convolved, at = carve(ada_w_flat, at, 2, 2 * T)
        group_rstd, at = carve(ada_w_flat, at, 2, T)
        assert at <= 4096
        qk2, at = carve(big, 0, 10, T)
        swap2, at = carve(big, at, 2, 2 * T)
        v2, at = carve(big, at, TT, 256)
        k_both, at = carve(big, at, 4, T)
        probs_t, at = carve(big, at, 2, 2, SEG)
        g2, at = carve(more, 0, ATT_TILES, T)
        probs, at = carve(more, at, 2, 2, SEG)
        out_rows, at = carve(big, 6144, TT, D)
        head_ln2, at = carve(ada_w_flat, 0, 2, 2 * T)
        head_rstd2, at = carve(ada_w_flat, at, 2, 2 * T)
        ple_gate, at = carve(ada_w_flat, at, 2, 2 * T)
        row_max, at = carve(ada_sum_flat, 0, ATT_TILES, 4)
        neg_max, at = carve(ada_sum_flat, at, ATT_TILES, 4)
        sink_arg, at = carve(ada_sum_flat, at, ATT_TILES, 4)
        sink_exp, at = carve(ada_sum_flat, at, ATT_TILES, 4)
        row_sum, at = carve(ada_sum_flat, at, ATT_TILES, 4)
        row_inv, at = carve(ada_sum_flat, at, ATT_TILES, 4)

        ready, left, first_unit = [], [], {}
        here = []
        for b, (name, _, _) in enumerate(plan):
            before = here[b - RING] if b >= RING else 0
            here.append(before + 16 * (L if name == "s5_near" else 1))

        def units(phase, blocks_each, leaves):
            first_unit[phase] = len(ready)
            for n, leave in enumerate(leaves):
                ready.append(first_block.get(phase, 0) + (n + 1) * blocks_each)
                left.append(leave)

        units("w_in", 1, [(sg_ready, 1), (a_ready, 1), (sg_ready, 2), (a_ready, 2)]
              + [(qk_copied, n + 1) for n in range(4)] + [(v_ready, 1), (v_ready, 2), (g_ready, 1), (g_ready, 2)])
        units("w_out", 1, [(x_ready, 4 + n + 1) for n in range(4)])
        units("fc1_0", 1, [(hid_relu, n + 1) for n in range(16)])
        units("fc2_0", 4, [(x_ready, 8 + n + 1) for n in range(4)])
        units("s5_in", 1, [(s5_e, n + 1) for n in range(8)])
        units("s5_out", 3, [(s5_z, n + 1) for n in range(4)])
        units("glu", 1, [x for n in range(4) for x in ((glu_sig, n + 1), (glu_mul, n + 1))])
        units("fc1_1", 1, [(hid_relu, 16 + n + 1) for n in range(16)])
        units("fc2_1", 4, [(x_ready, 16 + n + 1) for n in range(4)])
        units("xbc", 1, [(xbc_copied, n + 1) for n in range(XBC_UNITS)])
        units("z", 1, [(zs_ready, n + 1) for n in range(8)])
        units("ssm_out", 2, [(x_ready, 24 + n + 1) for n in range(4)])
        for layer, version in ((0, 7), (1, 9)):
            if layer == 1:
                units("kv", 1, [(qk2_copied, 1), (v2_ready, 1)])
                units("q", 1, [(qk2_copied, 2 + n) for n in range(4)])
                units("gate", 1, [(g2_ready, n + 1) for n in range(4)])
                units("attn_out", 1, [(x_ready, 32 + n + 1) for n in range(4)])
            units(f"ple_proj_{layer}", 0, [(pp_ready, 4 * layer + n + 1) for n in range(4)])
            for n in range(4):
                ready[first_unit[f"ple_proj_{layer}"] + n] = first_block[f"ple_proj_{layer}"] + 1
            units(f"ple_gate_{layer}", 1, [(ple_sig, 4 * layer + n + 1) for n in range(4)])
        units("final", 0, [(out_copied, n + 1) for n in range(4)])

        block = ctx.enter_context(nc.Block())

        @block.sync
        def _(sp):
            sp.dma_start(const[:, :], dram["const"]).then_inc(const_here, 16)
            sp.dma_start(mixT[:, :, :].rearrange("p (t a) n -> p t (a n)", t=TT),
                         dram["x"][0].rearrange("(t p) d -> p t d", p=P)).then_inc(x_here, 16)
            for n in range(PIECES):
                sp.dma_start((big, more)[n // 4][:, 2048 * (n % 4):2048 * (n % 4) + 2048]
                             .rearrange("p (k n) -> p k n", k=KB),
                             dram["ada_w"][0, :, n * NB:(n + 1) * NB].rearrange("(k p) n -> p k n", p=P))\
                    .then_inc(ada0_here[n], 16)
            for b, (name, kb, nb) in enumerate(plan):
                if b >= RING:
                    sp.wait_ge(blocks_done, b - RING + 1)
                if b == first_block["w_out"] + RING:
                    for ri, part in enumerate(("re", "im")):
                        for d in range(2):
                            sp.dma_start(lam_rows[:, ri, 64 * d:64 * d + 64], dram[f"s5_lam_{part}"][0, d])\
                                .then_inc(lam_here, 16)
                            sp.dma_start(c_rows[:, ri, :, 64 * d:64 * d + 64],
                                         dram[f"s5_c_{part}"][0, d].rearrange("(t g) c p -> (g c) t p", t=8))\
                                .then_inc(crow_here, 16)
                            sp.dma_start(b_raw[64 * d:64 * d + 64, ri],
                                         dram[f"s5_b_{part}"][0, d].rearrange("g p c -> p g c"))\
                                .then_inc(braw_here, 16)
                    for d in range(2):
                        sp.dma_start(s5_logdt[64 * d:64 * d + 64, :],
                                     dram["s5_log_step"][0, d:d + 1, :].partition_broadcast(64)).then_inc(logdt_here, 16)
                    sp.wait_ge(dq_zero, 1)
                    for q in range(4):
                        sp.dma_start(s5_dq[32 * q:32 * q + GC, :],
                                     dram["s5_d_flat"].rearrange("(a q c) -> q c a", q=4, c=GC)[q],
                                     allow_slow_non_contiguous=True).then_inc(dq_here, 16)
                if b == first_block["fc1_1"]:
                    sp.dma_start(dt_w, dram["ssm_in"][:, 5 * D:5 * D + SSM_HEADS].rearrange("(k p) n -> p k n", p=P))\
                        .then_inc(small_here, 16)
                    for dst, src in ((dt_bias, "ssm_dt_bias_2"), (a_rows, "ssm_a_log_2"), (sinks, "attn_sinks_2")):
                        sp.dma_start(dst, dram[src][0:1, :].partition_broadcast(P)).then_inc(small_here, 16)
                    for h in range(2):
                        sp.dma_start(d_cols[64 * h:64 * h + 64, :],
                                     dram["ssm_d_2"].rearrange("a (t h) -> a h t", h=2)[:, h].partition_broadcast(64),
                                     allow_slow_non_contiguous=True).then_inc(small_here, 16)
                    sp.dma_start(positions[:, :], dram["positions_2"][0:1, :].partition_broadcast(P))\
                        .then_inc(positions_here, 16)
                    sp.dma_start(p_rows, dram["p_2"].rearrange("l b (t p) n -> p (l b t) n", p=P)).then_inc(p_here, 16)
                if name.startswith("ple_proj"):
                    sp.dma_start(ring[:, b % RING].rearrange("p a b -> p (a b)").rearrange("p (k n) -> p k n", k=PLE // P),
                                 dram[name]).then_inc(w_here[b % RING], 16)
                    continue
                if name == "s5_in" and nb == 0:
                    sp.wait_ge(we_stored, 16 * 8)
                if name == "s5_far" and nb == 0:
                    sp.wait_ge(ca_stored, 16 * 8)
                    sp.wait_ge(k_stored, 64 * 8)
                if name == "s5_in":
                    sp.dma_start(ring[:, b % RING].rearrange("p a b -> p (a b)"), we_dram[nb])\
                        .then_inc(w_here[b % RING], 16)
                    continue
                if name == "s5_far":
                    sp.dma_start(ring[:, b % RING].rearrange("p a b -> p (a b)"), ca_dram[nb])\
                        .then_inc(w_here[b % RING], 16)
                    continue
                if name == "s5_near":
                    for j in range(L):
                        sp.dma_start(ring[GC * j:GC * j + GC, b % RING].rearrange("p a (b x) -> p (a b) x", x=P),
                                     k_dram[16 * nb:16 * nb + 16, :, (L - 1 - j) * GC:(L - 1 - j) * GC + P]
                                     .rearrange("g c x -> c g x")).then_inc(w_here[b % RING], 16)
                    continue
                sp.dma_start(ring[:, b % RING],
                             dram[name][kb * KB * P:(kb + 1) * KB * P, nb * NB:(nb + 1) * NB]
                             .rearrange("(k p) n -> p k n", p=P)).then_inc(w_here[b % RING], 16)
            for n in range(4):
                sp.wait_ge(out_copied, n + 1)
                sp.dma_start(out[0].rearrange("(t p) d -> p t d", p=P)[:, :, NB * n:NB * n + NB],
                             out_rows[:, :, NB * n:NB * n + NB]).then_inc(out_done, 16)
            sp.wait_ge(out_done, 16 * 4)

        @block.gpsimd
        def _(pool):
            steps = 0
            nc.gpsimd.memset(s5_dq[:, :], 0.0).then_inc(dq_zero, 1)

            def load_piece(n):
                layer, piece = divmod(n, ADA_PIECES // 2)
                pool.dma_start(ada_w[:, n % 2], dram["ada_w"][layer, :, piece * NB:(piece + 1) * NB]
                               .rearrange("(k p) n -> p k n", p=P)).then_inc(ada_here[n % 2], 16)

            load_piece(PIECES)
            load_piece(PIECES + 1)
            pool.wait_ge(c_ready, 1)
            for n in range(PIECES, ADA_PIECES):
                g, piece = divmod(n, PIECES)
                pool.wait_ge(ada_here[n % 2], 16 * ((n - PIECES) // 2 + 1))
                if piece == 0 and g >= 2:
                    pool.wait_ge(ada_psum, g - 1)
                w = ada_w[:, n % 2]
                nc.gpsimd.tensor_tensor(w, w, c_act[:, :].unsqueeze(2).to_broadcast([P, KB, NB]),
                                        ALU.mult).then_inc(pool_step, 1)
                steps += 1
                pool.wait_ge(pool_step, steps)
                for a in (4, 2):
                    nc.gpsimd.tensor_tensor(w[:, 0:a], w[:, 0:a], w[:, a:2 * a], ALU.add).then_inc(pool_step, 1)
                    steps += 1
                    pool.wait_ge(pool_step, steps)
                nc.gpsimd.tensor_tensor(ada_sum[:, g % 2, piece], w[:, 0], w[:, 1], ALU.add).then_inc(ada_sums, 1)
                pool.wait_ge(ada_sums, n - PIECES + 1)
                if n + 2 < ADA_PIECES:
                    load_piece(n + 2)

            def weigh(t):
                pool.wait_ge(seg_exp, t + 1)
                pool.wait_ge(cb_ready, SSM_GROUPS)
                s = seg[:, t % 2]
                nc.gpsimd.tensor_tensor(s, s, cb[:, t // 4].unsqueeze(1).to_broadcast([P, 2, SEG]), ALU.mult)\
                    .then_inc(seg_weighed, 1)

            weigh(0)
            weigh(1)
            for t in range(Z_TILES):
                pool.wait_ge(zs_ready, t // 2 + 1)
                pool.wait_ge(y_skipped, t + 1)
                nc.gpsimd.tensor_tensor(xs[:, t], xs[:, t], zs[:, t], ALU.mult).then_inc(y_gated, 1)
                if t + 2 < Z_TILES:
                    weigh(t + 2)

        @block.scalar
        def _(act):
            steps = [0]

            def link(ins):
                steps[0] += 1
                ins.then_inc(act_step, 1)
                act.wait_ge(act_step, steps[0])

            def unit(phase, n):
                u = first_unit[phase] + n
                act.wait_ge(blocks_done, ready[u])
                return pair(PS[u % BANKS])

            for s, rows in enumerate(STACKS):
                at = 0
                for name, count in rows:
                    a = dram[name]
                    if name in ("k_norm_w_2", "q_norm_w_2"):
                        for h in range(2):
                            act.dma_start(stack[at:at + 1, s, 64 * h:64 * h + 64], a).then_inc(stack_here, 16)
                    else:
                        act.dma_start(stack[at:at + count, s, :], a).then_inc(stack_here, 16)
                    at += count
            act.wait_ge(const_here, 16)
            act.wait_ge(cols_ready, 1)
            nc.scalar.activation(c_act[:, :], col("c"), ACT.Silu).then_inc(c_ready, 1)

            normed_before = (0, 8, 16, 24, 32, 32, 40, 48, 64)

            def norm_stats(i, version):
                for p in range(4):
                    act.wait_ge(x_ready, 4 * version + p + 1)
                    if p == 0 and i > 0:
                        act.wait_ge(stat_ready, i)
                    nc.scalar.activation(sq[:, 2 * p:2 * p + 2], xT[:, 2 * p:2 * p + 2], ACT.Square)\
                        .then_inc(sq_ready, 1)
                act.wait_ge(stat_ready, i + 1)
                if i > 0:
                    act.wait_ge(hn_ready, normed_before[i])
                link(nc.scalar.activation(lnv[:, :], STAT[:, 0:T], ACT.Ln, bias=eps, scale=1.0 / D))
                nc.scalar.activation(rstd[:, :], lnv[:, :], ACT.Exp, scale=-0.5).then_inc(rstd_ready, 1)

            def shift(i, layer, which):
                for k in range(DT):
                    act.wait_ge(hn_ready, 8 * i + k + 1)
                    dst, src = hT[:, k], hT[:, k]
                    if i == 2:
                        dst = h_perm[:, k].rearrange("p (j s) -> p s j", j=L)
                        src = src.rearrange("p (s j) -> p s j", j=L)
                    nc.scalar.activation(dst, src, ACT.Identity, bias=mod(layer, which, k), scale=1.0)\
                        .then_inc(h_ready, 1)

            norm_stats(0, 0)
            shift(0, 0, SHIFT_M)

            for j in range(2):
                ps = unit("w_in", 2 * j)
                if j:
                    act.wait_ge(a_ready, 1)
                nc.scalar.activation(sgate, ps, ACT.Sigmoid).then_inc(sg_ready, 1)
            for j in range(4):
                ps = unit("w_in", 4 + j)
                nc.scalar.activation(qk[:, 2 * j:2 * j + 2], ps, ACT.Copy)
                nc.scalar.activation(qk_swap[0:64, 2 * j:2 * j + 2], ps[64:128], ACT.Copy)
                nc.scalar.activation(qk_swap[64:128, 2 * j:2 * j + 2], ps[0:64], ACT.Copy).then_inc(qk_copied, 1)
            for j in range(2):
                ps = unit("w_in", 8 + j)
                nc.scalar.activation(vnat[:, :, NB * j:NB * j + NB], ps, ACT.Copy).then_inc(v_ready, 1)
            for j in range(2):
                ps = unit("w_in", 10 + j)
                nc.scalar.activation(gsilu[:, 2 * j:2 * j + 2], ps, ACT.Silu).then_inc(g_ready, 1)

            for h in range(HEADS):
                act.wait_ge(ret_psum, h + 1)
                nc.scalar.activation(ret[:, h], MISC[2][:, 0:T], ACT.Copy)
                nc.scalar.activation(ret_sq[:, h % 2], MISC[2][:, 0:T], ACT.Square).then_inc(ret_copied, 1)
                act.wait_ge(ret_stat, h + 1)
                if h >= 2:
                    act.wait_ge(ret_ready, h - 1)
                link(nc.scalar.activation(head_ln[:, h % 2], STAT[:, 0:T], ACT.Ln, bias=eps, scale=1.0 / P))
                nc.scalar.activation(head_rstd[:, h % 2], head_ln[:, h % 2], ACT.Exp, scale=-0.5)\
                    .then_inc(ret_rstd, 1)

            act.wait_ge(centred, 1)
            nc.scalar.activation(sq[:, 0:MT], conv, ACT.Square).then_inc(cen_sq, 1)
            act.wait_ge(var_psum, 1)
            link(nc.scalar.activation(lnv[:, :], STAT[:, 0:T], ACT.Ln, bias=eps, scale=1.0 / MIX))
            nc.scalar.activation(rstd[:, :], lnv[:, :], ACT.Exp, scale=-0.5).then_inc(ln_rstd, 1)
            for k in range(MT):
                act.wait_ge(ln_scaled, k + 1)
                nc.scalar.activation(mixT[:, k], conv[:, k], ACT.Silu, bias=col("cln_b", k), scale=1.0)\
                    .then_inc(conv_mix, 1)

            def relu_unit(phase, n):
                nc.scalar.activation(hid[:, 2 * n:2 * n + 2], unit(phase, n), ACT.Relu).then_inc(hid_relu, 1)

            def store_kernels(m):
                act.wait_ge(kext_ready, m + 1)
                for q in range(4):
                    act.dma_start(k_dram.rearrange("(a q) c x -> q c a x", q=4)[q, :, 2 * m:2 * m + 2, :],
                                  kext[32 * q:32 * q + GC, :, :]).then_inc(k_stored, 16)

            def s5_tile(m):
                if m > 0:
                    store_kernels(m - 1)
                    act.wait_ge(we_stored, 16 * m)
                for b in range(4):
                    act.wait_ge(we_psum, 4 * m + b + 1)
                    nc.scalar.activation(we_t[:, 2 * b:2 * b + 2].rearrange("p g r x -> p (g r x)"), MISC[b % 2][:, :],
                                         ACT.Copy).then_inc(we_copied, 1)
                act.wait_ge(we_copied, 4 * m + 4)
                act.dma_start(we_dram[m], we_t[:, :, :, :].rearrange("p g r x -> p (g r x)")).then_inc(we_stored, 16)
                act.wait_ge(ca_ready, m + 1)
                act.dma_start(ca_dram[m], more[:, 2048:4096]).then_inc(ca_stored, 16)

            norm_stats(1, 1)
            shift(1, 0, SHIFT_F)
            for n in range(16):
                relu_unit("fc1_0", n)
                if n == 0:
                    act.wait_ge(logdt_here, 32)
                    nc.scalar.activation(s5_dt, s5_logdt, ACT.Exp).then_inc(s5_fun, 1)
                    act.wait_ge(s5_args, 1)
                    nc.scalar.activation(s5_mag, s5_a, ACT.Exp).then_inc(s5_fun, 1)
                if n == 1:
                    act.wait_ge(s5_args, 2)
                    nc.scalar.activation(s5_sin, s5_r, ACT.Sin)
                    nc.scalar.activation(s5_cos, s5_r, ACT.Sin, scale=0.5).then_inc(s5_fun, 1)
                if n in (1, 2):
                    for b in range(2):
                        act.wait_ge(crow_psum, 2 * (n - 1) + b + 1)
                        nc.scalar.activation(s5_c[:, n - 1, 32 * b:32 * b + 32].rearrange("p g c -> p (g c)"),
                                             MISC[1 + b][:, :], ACT.Copy, scale=1.0 if n == 1 else -1.0)\
                            .then_inc(c_copied, 1)
                if n in S5_AT_FC1[1:]:
                    s5_tile(S5_AT_FC1.index(n) - 1)
            s5_tile(4)
            for m in range(5, 8):
                s5_tile(m)
            store_kernels(7)
            act.wait_ge(k_stored, 64 * 8)
            act.wait_ge(rot_args, 1)
            nc.scalar.activation(shrink[:, :, 1:NCH], s5_a.unsqueeze(2).to_broadcast([P, GROUPS, NCH - 1]), ACT.Exp,
                                 scale=float(L))
            nc.scalar.activation(rot_sin, rot_cos, ACT.Sin)
            nc.scalar.activation(rot_cos, rot_cos, ACT.Sin, scale=0.5).then_inc(rot_fun, 1)

            norm_stats(2, 2)
            shift(2, 1, SHIFT_M)
            for kh in range(2):
                act.wait_ge(s5_rows, 2 * kh + 1)
                for j in range(4):
                    ins = nc.scalar.activation(h_rows[:, 32 * kh:32 * kh + 32, j],
                                               PS[2 * kh][32 * j:32 * j + 32, :].rearrange("s (g c) -> s g c", c=GC),
                                               ACT.Copy)
                ins.then_inc(rows_act, 1)
            for n in range(8):
                ps = PS[(first_unit["s5_in"] + n) % BANKS]
                act.wait_ge(blocks_done, ready[first_unit["s5_in"] + n])
                v = ps[:, :].rearrange("p (r g s) -> p r g s", r=2, g=8)
                dst = state[:, :, 8 * n:8 * n + 8]
                nc.scalar.activation(dst[0:64], v[0:64], ACT.Copy)
                nc.scalar.activation(dst[64:128, :, :, ::-1], v[64:128], ACT.Copy).then_inc(s5_e, 1)
            for n in range(4):
                ps = PS[(first_unit["s5_out"] + n) % BANKS]
                act.wait_ge(blocks_done, ready[first_unit["s5_out"] + n])
                for q in range(4):
                    dst = z_rows.rearrange("s j (a q c) -> s q a j c", q=4, c=GC)[:, q, 4 * n:4 * n + 4]
                    ins = nc.scalar.activation(dst, ps[32 * q:32 * q + 32, :].rearrange("s (a j c) -> s a j c", a=4, j=L),
                                               ACT.Gelu_apprx_tanh)
                ins.then_inc(s5_z, 1)
            for n in range(4):
                ps = unit("glu", 2 * n)
                if n:
                    act.wait_ge(glu_mul, n)
                nc.scalar.activation(glu_gate, ps, ACT.Sigmoid).then_inc(glu_sig, 1)
            norm_stats(3, 3)
            shift(3, 1, SHIFT_F)
            for n in range(16):
                relu_unit("fc1_1", n)

            norm_stats(4, 4)
            act.wait_ge(angle_ready, 1)
            nc.scalar.activation(rope_sin, angle, ACT.Sin)
            nc.scalar.activation(rope_cos, angle, ACT.Sin, scale=0.5).then_inc(angle_fun, 1)

            norm_stats(5, 5)
            act.wait_ge(pad_zero, 1)
            for m in range(XBC_UNITS):
                ps = unit("xbc", m)
                if m >= 4:
                    act.wait_ge(xbc_conv, m - 3)
                nc.scalar.activation(padded[:, m % 4].rearrange("p (k n) -> p k n", k=2)[:, :, 3:3 + T], ps,
                                     ACT.Copy).then_inc(xbc_copied, 1)
                if m == 0:
                    act.wait_ge(small_here, 16 * 6)
                    nc.scalar.activation(a_rows, a_rows, ACT.Exp)
                    act.wait_ge(dt_args, 1)
                    nc.scalar.activation(dt_e, dt_s, ACT.Exp, scale=-1.0).then_inc(dt_fun, 1)

                def silu(m):
                    act.wait_ge(xbc_conv, m + 1)
                    for i in range(2):
                        tile = 16 + 2 * m + i if m < 4 else 2 * (m - 4) + i
                        dst = bc_tiles[:, 2 * m + i] if m < 4 else xs[:, tile]
                        ins = nc.scalar.activation(dst, convolved[:, m % 2, T * i:T * i + T], ACT.Silu,
                                                   bias=col("ssm_conv_b_2", tile), scale=1.0)
                    ins.then_inc(xbc_ready, 1)

                if m >= 1:
                    silu(m - 1)
            silu(XBC_UNITS - 1)

            def decays(t):
                act.wait_ge(seg_ready, t + 1)
                nc.scalar.activation(seg[:, t % 2], seg[:, t % 2], ACT.Exp).then_inc(seg_exp, 1)

            decays(0)
            decays(1)
            for n in range(8):
                ps = unit("z", n)
                nc.scalar.activation(zs[:, 2 * n:2 * n + 2], ps, ACT.Silu).then_inc(zs_ready, 1)
                if n < 7:
                    decays(2 * n + 2)
                    decays(2 * n + 3)
            for g in range(SSM_GROUPS):
                act.wait_ge(y_gated, 4 * g + 4)
                if g >= 2:
                    act.wait_ge(group_stat, g - 1)
                nc.scalar.activation(sq[:, 4 * (g % 2):4 * (g % 2) + 4], xs[:, 4 * g:4 * g + 4], ACT.Square)\
                    .then_inc(group_sq, 1)
                act.wait_ge(group_stat, g + 1)
                if g >= 2:
                    act.wait_ge(y_ready, 4 * (g - 1))
                link(nc.scalar.activation(group_ln[:, g % 2], MISC[g % 2][:, 0:T], ACT.Ln, bias=eps,
                                          scale=1.0 / (4 * P)))
                nc.scalar.activation(group_rstd[:, g % 2], group_ln[:, g % 2], ACT.Exp, scale=-0.5)\
                    .then_inc(group_rstd_ready, 1)

            def embedding(layer, norm, version):
                for n in range(4):
                    ps = unit(f"ple_proj_{layer}", n)
                    nc.scalar.activation(ple_prod[:, 2 * n:2 * n + 2], ps, ACT.Copy).then_inc(pp_ready, 1)
                norm_stats(norm, version)
                for n in range(4):
                    ps = unit(f"ple_gate_{layer}", n)
                    if n >= 2:
                        act.wait_ge(ple_mul, 4 * layer + n - 1)
                    nc.scalar.activation(ple_gate[:, n % 2].rearrange("p (k n) -> p k n", k=2), ps, ACT.Sigmoid)\
                        .then_inc(ple_sig, 1)

            embedding(0, 6, 6)

            norm_stats(7, 7)

            def head_norm(m):
                ps = unit("kv", 0) if m == 0 else unit("q", m - 1)
                if m >= 2:
                    act.wait_ge(qk2_stat, m - 1)
                nc.scalar.activation(sq[:, 2 * (m % 2):2 * (m % 2) + 2], ps, ACT.Square)
                nc.scalar.activation(qk2[:, 2 * m:2 * m + 2], ps, ACT.Copy).then_inc(qk2_copied, 1)
                if m == 0:
                    ps = unit("kv", 1)
                    nc.scalar.activation(v2, ps, ACT.Copy).then_inc(v2_ready, 1)
                act.wait_ge(qk2_stat, m + 1)
                if m >= 2:
                    act.wait_ge(qk2_normed, m - 1)
                link(nc.scalar.activation(head_ln2[:, m % 2], MISC[m % 2][:, :], ACT.Ln, bias=eps, scale=1.0 / 64))
                nc.scalar.activation(head_rstd2[:, m % 2], head_ln2[:, m % 2], ACT.Exp, scale=-0.5)\
                    .then_inc(qk2_rstd, 1)

            def swap_halves(m):
                act.wait_ge(qk2_normed, m + 1)
                if m >= 2:
                    act.wait_ge(qk2_ready, m - 1)
                src, dst = qk2[:, 2 * m:2 * m + 2], swap2[:, m % 2].rearrange("p (k n) -> p k n", k=2)
                for a in (0, 64):
                    nc.scalar.activation(dst[a:a + 32], src[a + 32:a + 64], ACT.Copy)
                    ins = nc.scalar.activation(dst[a + 32:a + 64], src[a:a + 32], ACT.Copy)
                ins.then_inc(qk2_swapped, 1)

            for m in range(5):
                head_norm(m)
                if m >= 1:
                    swap_halves(m - 1)
                if m == 2:
                    act.wait_ge(qk2_ready, 1)
                    for g in range(4):
                        lo = 64 * (g % 2)
                        nc.scalar.activation(k_both[0:64, g], qk2[lo:lo + 64, g // 2], ACT.Copy)
                        ins = nc.scalar.activation(k_both[64:128, g], qk2[lo:lo + 64, g // 2], ACT.Copy)
                    ins.then_inc(k_both_ready, 1)
            swap_halves(4)

            def exponents(t):
                act.wait_ge(s_max, t + 1)
                for h in range(2):
                    for b, (lo, hi) in enumerate(((0, P), (P, SEG))):
                        i = 2 * h + b
                        nc.scalar.activation(probs[:, t % 2, h, lo:hi], probs[:, t % 2, h, lo:hi], ACT.Exp,
                                             bias=neg_max[:, t, i:i + 1], scale=1.0,
                                             accum_out=row_sum[:, t, i:i + 1])
                nc.scalar.activation(sink_exp[:, t], sink_arg[:, t], ACT.Exp).then_inc(s_exp, 1)

            def copy_turned(t):
                for h in range(2):
                    act.wait_ge(pt_psum, 2 * t + h + 1)
                    if t >= 2 and h == 0:
                        act.wait_ge(o_psum, t - 1)
                    nc.scalar.activation(probs_t[:, t % 2, h], (MISC[2], STAT)[h][:, 0:SEG], ACT.Copy)\
                        .then_inc(pt_ready, 1)

            for n in range(4):
                nc.scalar.activation(g2[:, 2 * n:2 * n + 2], unit("gate", n), ACT.Silu).then_inc(g2_ready, 1)
            exponents(0)
            for t in range(ATT_TILES):
                if t + 1 < ATT_TILES:
                    exponents(t + 1)
                copy_turned(t)
            embedding(1, 8, 8)
            for n in range(4):
                act.wait_ge(out_psum, n + 1)
                nc.scalar.activation(out_rows[:, :, NB * n:NB * n + NB], pair(PS[(first_unit["final"] + n) % BANKS]),
                                     ACT.Copy).then_inc(out_copied, 1)

        @block.tensor
        def _(pe):
            def start_unit(phase, n):
                u = first_unit[phase] + n
                if u >= BANKS:
                    pe.wait_ge(*left[u - BANKS])
                return PS[u % BANKS]

            def start_block(phase, n):
                b = first_block[phase] + n
                pe.wait_ge(w_here[b % RING], here[b])
                return ring[:, b % RING]

            def project(phase, n, rhs, arrived=None):
                ps = pair(start_unit(phase, n))
                w = start_block(phase, n)
                for i in range(2):
                    for k in range(KB):
                        if i == 0 and arrived:
                            arrived(k)
                        last = nc.tensor.matmul(ps[:, i], w[:, k, P * i:P * i + P], rhs[:, k],
                                                start=(k == 0), stop=(k == KB - 1))
                last.then_inc(blocks_done, 1)

            def project_tokens(phase, n, lhs):
                ps = pair(start_unit(phase, n))
                w = start_block(phase, n)
                for i in range(TT):
                    for k in range(KB):
                        last = nc.tensor.matmul(ps[:, i], lhs[:, k, P * i:P * i + P], w[:, k],
                                                start=(k == 0), stop=(k == KB - 1))
                last.then_inc(blocks_done, 1)

            def project_deep(phase, n, kblocks, rhs, arrived=None):
                ps = pair(start_unit(phase, n))
                for kb in range(kblocks):
                    w = start_block(phase, n * kblocks + kb)
                    for k in range(KB):
                        if n == 0 and arrived:
                            arrived(kb * KB + k)
                        for i in range(2):
                            first = kb == 0 and k == 0
                            last = nc.tensor.matmul(ps[:, i], w[:, k, P * i:P * i + P], rhs[:, kb * KB + k],
                                                    start=(first and i == 0),
                                                    stop=(kb == kblocks - 1 and k == KB - 1),
                                                    skip_group_check=True)
                    last.then_inc(blocks_done, 1)

            def modulation(g):
                if g == 0:
                    pe.wait_ge(ada0_sums, 4)
                else:
                    pe.wait_ge(ada_sums, PIECES * g)
                    pe.wait_ge(mods_ready, g)
                for m in range(2 * PIECES):
                    last = nc.tensor.matmul(MISC[0][:, m:m + 1], ada_sum[:, g % 2, m // 2, P * (m % 2):P * (m % 2) + P],
                                            ones[:, 0:1], start=True, stop=True)
                last.then_inc(ada_psum, 1)

            def norm_stats(i):
                if i > 0:
                    pe.wait_ge(rstd_ready, i)
                for k in range(DT):
                    if k % 2 == 0:
                        pe.wait_ge(sq_ready, 4 * i + k // 2 + 1)
                    last = nc.tensor.matmul(STAT[:, 0:T], ones, sq[:, k], start=(k == 0), stop=(k == DT - 1))
                last.then_inc(stat_ready, 1)

            pe.wait_ge(const_here, 16)
            pe.wait_ge(stack_here, 16 * N_STACK_LOADS)
            for s in range(len(STACKS)):
                rows = sum(n for _, n in STACKS[s])
                last = nc.tensor.transpose(MISC[1][:, s * P:s * P + rows], stack[0:rows, s, :], ident[0:rows, 0:rows])
            last.then_inc(cols_psum, 1)
            pe.wait_ge(x_here, 16)
            for k in range(DT):
                for t in range(TT):
                    last = nc.tensor.transpose(PS[k // 2][:, (k % 2) * T + t * P:(k % 2) * T + t * P + P],
                                               mixT[:, :, :].rearrange("p (t a) n -> p t (a n)", t=TT)
                                               [:, t, k * P:k * P + P], ident)
                if k % 2:
                    last.then_inc(x_psum, 1)
            norm_stats(0)
            modulation(0)

            def h_arrived(i):
                return lambda k: pe.wait_ge(h_ready, 8 * i + k + 1)

            pe.wait_ge(x_ready, 4)
            for n in range(8):
                project("w_in", n, hT, h_arrived(0) if n == 0 else None)
            for n in range(8, 10):
                project_tokens("w_in", n, hT)
            for n in range(10, 12):
                project("w_in", n, hT)

            pe.wait_ge(mods_ready, 1)
            pe.wait_ge(rstd_ready, 1)
            pe.wait_ge(v_ready, 2)

            def scores(h):
                pe.wait_ge(qk_ready, 3 + h // 2)
                if h >= 2:
                    pe.wait_ge(score_ready, h - 1)
                for j in range(TT):
                    last = nc.tensor.matmul(MISC[h % 2][:, T * j:T * j + T], qk[:, 4 + h, P * j:P * j + P], qk[:, h],
                                            start=True, stop=True)
                last.then_inc(score_psum, 1)

            def values(h):
                pe.wait_ge(score_ready, h + 1)
                if h >= 1:
                    pe.wait_ge(ret_copied, h)
                for j in range(TT):
                    last = nc.tensor.matmul(MISC[2][:, 0:T], vnat[:, j, P * h:P * h + P], score[:, h % 2, j],
                                            start=(j == 0), stop=(j == TT - 1))
                last.then_inc(ret_psum, 1)

            def head_stats(h):
                pe.wait_ge(ret_copied, h + 1)
                if h >= 1:
                    pe.wait_ge(ret_rstd, h)
                nc.tensor.matmul(STAT[:, 0:T], ones, ret_sq[:, h % 2], start=True, stop=True).then_inc(ret_stat, 1)

            scores(0)
            for h in range(HEADS):
                if h + 1 < HEADS:
                    scores(h + 1)
                values(h)
                head_stats(h)

            pe.wait_ge(ret_rstd, HEADS)
            pe.wait_ge(conv_ready, 1)
            for k in range(MT):
                last = nc.tensor.matmul(STAT[:, 0:T], ones, conv[:, k], start=(k == 0), stop=(k == MT - 1))
            last.then_inc(mean_psum, 1)
            pe.wait_ge(cen_sq, 1)
            for k in range(MT):
                last = nc.tensor.matmul(STAT[:, 0:T], ones, sq[:, k], start=(k == 0), stop=(k == MT - 1))
            last.then_inc(var_psum, 1)
            modulation(1)

            def mix_arrived(k):
                if k < MT:
                    pe.wait_ge(conv_mix, k + 1)
                else:
                    pe.wait_ge(ret_ready, k - MT + 1)

            for n in range(4):
                project("w_out", n, mixT, mix_arrived if n == 0 else None)
            norm_stats(1)
            modulation(2)
            def s5_rows_turned(first, part, count):
                for b in range(2):
                    if part:
                        pe.wait_ge(c_copied, b + 1)
                    for t in range(4):
                        last = nc.tensor.transpose(MISC[1 + b][:, P * t:P * t + P], c_rows[:, part, 4 * b + t], ident)
                    last.then_inc(crow_psum, 1)

            def s5_tile(m):
                pe.wait_ge(we_ready, m + 1)
                for b in range(4):
                    if 4 * m + b >= 2:
                        pe.wait_ge(we_copied, 4 * m + b - 1)
                    for i in range(4):
                        last = nc.tensor.transpose(MISC[b % 2][:, P * i:P * i + P],
                                                   we_src[:, i % 2, 2 * b + i // 2], ident)
                    last.then_inc(we_psum, 1)
                pe.wait_ge(ca_ready, m + 1)
                if m > 0:
                    pe.wait_ge(kext_ready, m)
                edge = (L - 1) * GC
                for a in range(2):
                    for q in range(4):
                        g, gl = 8 * m + 4 * a + q, 4 * a + q
                        past = MISC[2][32 * q:32 * q + 32, P * a:P * a + P]
                        ahead = STAT[32 * q:32 * q + 32, P * a:P * a + edge]
                        for lo, dst, cols_in in ((64, ahead, slice(GC, P)), (0, past[:, GC:P], slice(0, edge))):
                            for ri in range(2):
                                b2 = b_bar[lo:lo + 64, ri, g:g + 2].rearrange("p g c -> p (g c)")
                                nc.tensor.matmul(dst, b2, ca_src[lo:lo + 64, ri, gl, cols_in],
                                                 start=(ri == 0), stop=(ri == 1))
                        for ri in range(2):
                            b2 = b_bar[:, ri, g:g + 2].rearrange("p g c -> p (g c)")
                            last = nc.tensor.matmul(past[:, 0:GC], b2, s5_c[:, ri, g], start=(ri == 0),
                                                    stop=(ri == 1))
                last.then_inc(kext_psum, 1)

            for n in range(16):
                project("fc1_0", n, hT, h_arrived(1) if n == 0 else None)
                if n == 0:
                    pe.wait_ge(lam_here, 64)
                    for ri in range(2):
                        last = nc.tensor.transpose(MISC[0][:, 64 * ri:64 * ri + 64], lam_rows[:, ri],
                                                   ident[0:64, 0:64])
                    last.then_inc(lam_psum, 1)
                    pe.wait_ge(crow_here, 64)
                    s5_rows_turned(0, 0, 2)
                if n == 1:
                    s5_rows_turned(0, 1, 2)
                if n in S5_AT_FC1[1:]:
                    s5_tile(S5_AT_FC1.index(n) - 1)
            s5_tile(4)
            for n in range(4):
                project_deep("fc2_0", n, 4, hid, lambda k: pe.wait_ge(hid_ready, k // 2 + 1) if k % 2 == 0 else None)
                if n < 3:
                    s5_tile(5 + n)
                if n == 2:
                    pe.wait_ge(we_copied, 32)
                    for g in range(3, 6):
                        modulation(g)

            norm_stats(2)
            for kh in range(2):
                for jq in range(2):
                    for i in range(4):
                        k = 4 * kh + i
                        if jq == 0:
                            pe.wait_ge(h_ready, 8 * 2 + k + 1)
                        last = nc.tensor.transpose(PS[2 * kh + jq][:, P * i:P * i + P],
                                                   h_perm[:, k, P * jq:P * jq + P], ident)
                    last.then_inc(s5_rows, 1)
            for b in range(4):
                if b % 2 == 0:
                    pe.wait_ge(rows_act, b // 2 + 1)
                    pe.wait_ge(rows_dve, b // 2 + 1)
                for i in range(16):
                    last = nc.tensor.transpose(PS[b][:, NCH * i:NCH * i + NCH],
                                               h_rows[:, 16 * b + i].rearrange("s j c -> s (j c)"),
                                               ident[0:NCH, 0:NCH])
                last.then_inc(u_psum, 1)
            for n in range(8):
                if n % 2 == 0:
                    pe.wait_ge(s5_u, n // 2 + 1)
                if n < 4:
                    pe.wait_ge(s5_u, 4)
                ps = start_unit("s5_in", n)
                w = start_block("s5_in", n).rearrange("p a b -> p (a b)").rearrange("p (g r x) -> p g r x", g=8, r=2)
                for ri in range(2):
                    for g in range(8):
                        last = nc.tensor.matmul(ps[:, 256 * ri + NCH * g:256 * ri + NCH * g + NCH], w[:, g, ri],
                                                u_in[:, 8 * n + g], start=True, stop=True)
                last.then_inc(blocks_done, 1)
            for n in range(4):
                ps = start_unit("s5_out", n)
                far0 = start_block("s5_out", 3 * n)
                near = start_block("s5_out", 3 * n + 1).rearrange("p a b -> p (a b)").rearrange("p (g x) -> p g x", g=16)
                for a in range(4):
                    if a == 0:
                        pe.wait_ge(state_ready, n // 2 + 1)
                    if a % 2 == 0:
                        far = (far0 if a == 0 else start_block("s5_out", 3 * n + 2)).rearrange("p a b -> p (a b)")\
                            .rearrange("p (r g x) -> p r g x", r=2, g=8)
                    for part in range(3):
                        for q in range(4):
                            g = 4 * a + q
                            if part == 0:
                                lhs, rhs = u_in[:, 16 * n + g], near[:, g]
                            else:
                                lhs, rhs = state[:, part - 1, 16 * n + g], far[:, part - 1, g % 8]
                            last = nc.tensor.matmul(ps[32 * q:32 * q + 32, P * a:P * a + P], lhs, rhs,
                                                    start=(part == 0), stop=(part == 2))
                    if a == 1:
                        last.then_inc(blocks_done, 1)
                last.then_inc(blocks_done, 2)
            for n in range(4):
                pe.wait_ge(s5_z, n + 1)
                if n >= 2:
                    pe.wait_ge(z_ready, n - 1)
                for i in range(2):
                    for j in range(L):
                        last = nc.tensor.transpose(MISC[n % 2][:, 256 * i + NCH * j:256 * i + NCH * j + NCH],
                                                   z_rows[:, j, P * (2 * n + i):P * (2 * n + i) + P],
                                                   ident[0:NCH, 0:NCH])
                last.then_inc(z_psum, 1)
            for n in range(8):
                project("glu", n, mixT, (lambda k: pe.wait_ge(z_ready, k // 2 + 1)) if n == 0 else None)
            norm_stats(3)
            for n in range(16):
                project("fc1_1", n, hT, h_arrived(3) if n == 0 else None)
            for n in range(4):
                project_deep("fc2_1", n, 4, hid,
                             lambda k: pe.wait_ge(hid_ready, 16 + k // 2 + 1) if k % 2 == 0 else None)

            def turn_p():
                pe.wait_ge(p_here, 16)
                for n in range(2):
                    pe.wait_ge(angle_ready, 1)
                    for i in range(4):
                        tile, t = 2 * n + i // 2, i % 2
                        last = nc.tensor.transpose(MISC[n][:, P * i:P * i + P],
                                                   p_rows[:, 2 * n + t, P * (tile % 2):P * (tile % 2) + P], ident)
                    last.then_inc(p_psum, 1)

            norm_stats(4)
            turn_p()
            norm_stats(5)

            def turn_x(n):
                pe.wait_ge(xbc_ready, 4 + n + 1)
                if n >= 2:
                    pe.wait_ge(xdt_ready, n - 1)
                for i in range(4):
                    last = nc.tensor.transpose((STAT, MISC[2])[n % 2][:, P * i:P * i + P],
                                               xs[:, 2 * n + i // 2, P * (i % 2):P * (i % 2) + P], ident)
                last.then_inc(xt_psum, 1)

            def spread(t):
                if t >= 2:
                    pe.wait_ge(seg_ready, t - 1)
                for h in range(2):
                    one_hot = ident[0:SSM_HEADS, 2 * t + h:2 * t + h + 1].to_broadcast([SSM_HEADS, P])
                    last = nc.tensor.matmul(MISC[t % 2][:, T * h:T * h + T], one_hot, a_cum_rows[0:SSM_HEADS, :],
                                            start=True, stop=True)
                last.then_inc(seg_psum, 1)

            def contract(t):
                pe.wait_ge(seg_weighed, t + 1)
                if t >= 2:
                    pe.wait_ge(y_skipped, t - 1)
                ps = (STAT, MISC[2])[t % 2]
                for h in range(2):
                    x = slice(SSM_DIM * (2 * t + h), SSM_DIM * (2 * t + h + 1))
                    rows = slice(SSM_DIM * h, SSM_DIM * h + SSM_DIM)
                    nc.tensor.matmul(ps[rows, 0:T], xdt[:, 0, x], seg[:, t % 2, h, 0:T], start=True, stop=False,
                                     skip_group_check=True)
                    last = nc.tensor.matmul(ps[rows, P:T], xdt[:, 1, x], seg[:, t % 2, h, T:SEG], start=False,
                                            stop=True, skip_group_check=True)
                last.then_inc(y_psum, 1)

            for m in range(XBC_UNITS):
                project("xbc", m, hT, (lambda k: pe.wait_ge(hn_ready, 32 + k + 1)) if m == 0 else None)
                if m == 0:
                    pe.wait_ge(small_here, 16 * 6)
                    pe.wait_ge(p_ready, 2)
                    for i in range(TT):
                        for k in range(KB):
                            last = nc.tensor.matmul(MISC[0][:, SSM_HEADS * i:SSM_HEADS * i + SSM_HEADS],
                                                    hT[:, k, P * i:P * i + P], dt_w[:, k], start=(k == 0),
                                                    stop=(k == KB - 1))
                    last.then_inc(dt_psum, 1)
                if m == 2:
                    pe.wait_ge(dta_ready, 1)
                    tri, less = table("tri")[:, 0:P], table("tri_less_one")
                    for i, w in enumerate((less, tri)):
                        nc.tensor.matmul(MISC[1][:, SSM_HEADS * i:SSM_HEADS * i + SSM_HEADS], w, dta[:, i], start=True,
                                         stop=True)
                    for i, w in enumerate((less, tri)):
                        last = nc.tensor.matmul(MISC[2][0:SSM_HEADS, P * i:P * i + P], dta[:, i], w, start=True,
                                                stop=True)
                    last.then_inc(a_cum_psum, 1)
                if m in (6, 7):
                    pe.wait_ge(xbc_ready, 4)
                    pe.wait_ge(a_cum_ready, 1)
                    for g in (2 * (m - 6), 2 * (m - 6) + 1):
                        if g >= 2:
                            pe.wait_ge(cb_ready, g - 1)
                        b, c = bc_tiles[:, g], bc_tiles[:, SSM_GROUPS + g]
                        nc.tensor.matmul(MISC[g % 2][:, 0:T], b[:, 0:P], c, start=True, stop=True)
                        nc.tensor.matmul(MISC[g % 2][:, T:SEG], b[:, P:T], c[:, P:T], start=True, stop=True)\
                            .then_inc(cb_psum, 1)
                if m >= 6:
                    turn_x(m - 6)
            pe.wait_ge(cb_ready, SSM_GROUPS)
            spread(0)
            spread(1)
            for n in range(8):
                project("z", n, hT)
                if n == 0:
                    turn_x(6)
                    turn_x(7)
                    pe.wait_ge(xdt_ready, 8)
                for t in (2 * n, 2 * n + 1):
                    contract(t)
                    if t + 2 < Z_TILES:
                        spread(t + 2)
            for g in range(SSM_GROUPS):
                pe.wait_ge(group_sq, g + 1)
                if g == 0:
                    pe.wait_ge(seg_ready, Z_TILES)
                if g >= 2:
                    pe.wait_ge(group_rstd_ready, g - 1)
                for k in range(4):
                    last = nc.tensor.matmul(MISC[g % 2][:, 0:T], ones, sq[:, 4 * (g % 2) + k], start=(k == 0),
                                            stop=(k == 3))
                last.then_inc(group_stat, 1)
            for n in range(4):
                project_deep("ssm_out", n, 2, xs, lambda k: pe.wait_ge(y_ready, k + 1))

            def embedding(layer, norm, base):
                w = start_block(f"ple_proj_{layer}", 0).rearrange("p a b -> p (a b)").rearrange(
                    "p (k n) -> p k n", k=PLE // P)
                pe.wait_ge(p_ready, 2)
                for n in range(4):
                    ps = pair(start_unit(f"ple_proj_{layer}", n))
                    for i in range(2):
                        for k in range(PLE // P):
                            last = nc.tensor.matmul(ps[:, i], w[:, k, P * (2 * n + i):P * (2 * n + i) + P],
                                                    p_tiles[:, 2 * layer + k], start=(k == 0), stop=(k == PLE // P - 1))
                last.then_inc(blocks_done, 1)
                norm_stats(norm)
                for n in range(4):
                    project(f"ple_gate_{layer}", n, hT,
                            (lambda k: pe.wait_ge(hn_ready, base + k + 1)) if n == 0 else None)

            embedding(0, 6, 40)

            norm_stats(7)

            def head_stats(m):
                pe.wait_ge(qk2_copied, m + 1)
                if m >= 2:
                    pe.wait_ge(qk2_rstd, m - 1)
                for i in range(2):
                    last = nc.tensor.matmul(MISC[m % 2][:, T * i:T * i + T], table("halves"), sq[:, 2 * (m % 2) + i],
                                            start=True, stop=True)
                last.then_inc(qk2_stat, 1)

            def scores(t):
                if t == 0:
                    pe.wait_ge(k_both_ready, 1)
                    pe.wait_ge(qk2_rstd, 5)
                else:
                    pe.wait_ge(s_masked, t)
                pe.wait_ge(qk2_ready, 2 + t // 2)
                for h in range(2):
                    lo = 64 * h
                    q, k = qk2[lo:lo + 64, 2 + t], k_both[lo:lo + 64, t // 2]
                    nc.tensor.matmul(MISC[h][:, 0:P], q[:, 0:P], k[:, 0:P], start=True, stop=True)
                    last = nc.tensor.matmul(MISC[h][:, P:SEG], q[:, P:T], k, start=True, stop=True)
                last.then_inc(s_psum, 1)

            def turn_probs(t):
                pe.wait_ge(probs_ready, t + 1)
                for h in range(2):
                    if t >= 1:
                        pe.wait_ge(pt_ready, 2 * t - 1 + h)
                    for i in range(3):
                        last = nc.tensor.transpose((MISC[2], STAT)[h][:, P * i:P * i + P],
                                                   probs[:, t % 2, h, P * i:P * i + P], ident)
                    last.then_inc(pt_psum, 1)

            def attend(t):
                ps = PS[t % 2]
                if t < 2:
                    pe.wait_ge(g2_ready, 4)
                else:
                    pe.wait_ge(o_ready, t - 1)
                for h in range(2):
                    pe.wait_ge(pt_ready, 2 * t + h + 1)
                    rows, v = slice(64 * h, 64 * h + 64), slice(64 * (t // 2), 64 * (t // 2) + 64)
                    p = probs_t[:, t % 2, h]
                    nc.tensor.matmul(ps[rows, 0:P], v2[:, 0, v], p[:, 0:P], start=True, stop=True)
                    nc.tensor.matmul(ps[rows, P:T], v2[:, 0, v], p[:, P:T], start=True, stop=False)
                    last = nc.tensor.matmul(ps[rows, P:T], v2[:, 1, v], p[:, T:SEG], start=False, stop=True)
                last.then_inc(o_psum, 1)

            project("kv", 0, mixT, lambda k: pe.wait_ge(hn_ready, 48 + k + 1))
            project_tokens("kv", 1, mixT)
            head_stats(0)
            for n in range(4):
                project("q", n, hT, (lambda k: pe.wait_ge(hn_ready, 56 + k + 1)) if n == 0 else None)
                head_stats(n + 1)
            for n in range(4):
                project("gate", n, hT)
            scores(0)
            scores(1)
            for t in range(ATT_TILES):
                turn_probs(t)
                if t + 2 < ATT_TILES:
                    scores(t + 2)
                attend(t)
            pe.wait_ge(o_ready, ATT_TILES)
            for n in range(4):
                project("attn_out", n, mixT)
            embedding(1, 8, 64)
            for n in range(4):
                ps = pair(start_unit("final", n))
                pe.wait_ge(x_ready, 4 * 9 + n + 1)
                for t in range(TT):
                    for i in range(2):
                        last = nc.tensor.transpose(ps[:, t, P * i:P * i + P], xT[:, 2 * n + i, P * t:P * t + P], ident)
                last.then_inc(out_psum, 1)

        @block.vector
        def _(dve):
            steps = [0]

            def step(ins):
                steps[0] += 1
                ins.then_inc(dve_step, 1)

            def link(ins):
                step(ins)
                dve.wait_ge(dve_step, steps[0])

            def behind(n):
                dve.wait_ge(dve_step, steps[0] - n)

            def unit(phase, n):
                u = first_unit[phase] + n
                dve.wait_ge(blocks_done, ready[u])
                return pair(PS[u % BANKS])

            dve.wait_ge(const_here, 16)
            dve.wait_ge(cols_psum, 1)
            for s in range(len(STACKS)):
                rows = sum(n for _, n in STACKS[s])
                last = nc.vector.tensor_copy(cols[:, s, 0:rows], MISC[1][:, s * P:s * P + rows])
            last.then_inc(cols_ready, 1)
            dve.wait_ge(cols_ready, 1)
            for p in range(4):
                dve.wait_ge(x_psum, p + 1)
                nc.vector.tensor_copy(xT[:, 2 * p:2 * p + 2], pair(PS[p])).then_inc(x_ready, 1)

            dve.wait_ge(c_ready, 1)
            for pp in range(PIECES // 2):
                for k in range(KB):
                    for n in (2 * pp, 2 * pp + 1):
                        w = (big, more)[n // 4][:, 2048 * (n % 4) + NB * k:2048 * (n % 4) + NB * k + NB]
                        if k == 0:
                            dve.wait_ge(ada0_here[n], 16)
                            step(nc.vector.tensor_scalar(ada_sum[:, 0, n], w, c_act[:, k:k + 1], None, ALU.mult))
                            continue
                        behind(1)
                        ins = nc.vector.scalar_tensor_tensor(out=ada_sum[:, 0, n], in0=w, scalar=c_act[:, k:k + 1],
                                                             in1=ada_sum[:, 0, n], op0=ALU.mult, op1=ALU.add)
                        if k == KB - 1 and n == 2 * pp + 1:
                            ins.then_inc(ada0_sums, 1)
                        else:
                            step(ins)

            def modulation(g):
                dve.wait_ge(ada_psum, g + 1)
                n = 2 * PIECES
                nc.vector.tensor_tensor(mods[:, g * n:g * n + n], MISC[0][:, 0:n], col("ada_b")[:, g * n:g * n + n],
                                        ALU.add).then_inc(mods_ready, 1)

            def gain(i):
                layer, which = i // 2, (SCALE_M, SCALE_F)[i % 2]
                dve.wait_ge(mods_ready, 3 * layer + (1, 3)[i % 2])
                link(nc.vector.scalar_tensor_tensor(out=gains[:, i], in0=mod(layer, which), scalar=1.0,
                                                    in1=col("norm_g")[:, 8 * i:8 * i + 8], op0=ALU.add, op1=ALU.mult))

            def normed(i, gain_col):
                dve.wait_ge(rstd_ready, i + 1)
                for k in range(DT):
                    nc.vector.scalar_tensor_tensor(out=hT[:, k], in0=xT[:, k], scalar=gain_col(k), in1=rstd[:, :],
                                                   op0=ALU.mult, op1=ALU.mult).then_inc(hn_ready, 1)

            def residual(phase, gate, first=0, last=4):
                for n in range(first, last):
                    ps = unit(phase, n)
                    for i in range(2):
                        k = 2 * n + i
                        ins = nc.vector.scalar_tensor_tensor(out=xT[:, k], in0=ps[:, i], scalar=gate(k), in1=xT[:, k],
                                                             op0=ALU.mult, op1=ALU.add)
                    ins.then_inc(x_ready, 1)

            modulation(0)
            gain(0)
            normed(0, lambda k: gains[:, 0, k:k + 1])

            nc.vector.memset(apad[:, :, 0:PAD], 0.0)
            nc.vector.memset(apad[:, :, PAD + T:], 0.0)
            for j in range(2):
                dve.wait_ge(sg_ready, j + 1)
                ps = unit("w_in", 2 * j + 1)
                nc.vector.tensor_tensor(apad[:, 2 * j:2 * j + 2, PAD:PAD + T], ps, sgate, ALU.mult).then_inc(a_ready, 1)
            dve.wait_ge(a_ready, 2)

            def taps(first, last):
                for tap in range(first, last):
                    for k in range(MT):
                        w = col("conv_w", 4 * tap + k)
                        if tap == 0:
                            step(nc.vector.tensor_scalar(conv[:, k], apad[:, k, 0:T], w, col("conv_b", k),
                                                         ALU.mult, ALU.add))
                            continue
                        behind(MT - 1)
                        ins = nc.vector.scalar_tensor_tensor(out=conv[:, k], in0=apad[:, k, tap:tap + T], scalar=w,
                                                             in1=conv[:, k], op0=ALU.mult, op1=ALU.add)
                        if tap == TAPS - 1 and k == MT - 1:
                            ins.then_inc(conv_ready, 1)
                        else:
                            step(ins)

            def rotate(j):
                dve.wait_ge(qk_copied, j + 1)
                a, b = qk[:, 2 * j:2 * j + 2], qk_swap[:, 2 * j:2 * j + 2]
                nc.vector.tensor_tensor(a, a, table("rope_cos").unsqueeze(1).to_broadcast([P, 2, T]), ALU.mult)
                link(nc.vector.tensor_tensor(b, b, table("rope_sin").unsqueeze(1).to_broadcast([P, 2, T]), ALU.mult))
                nc.vector.tensor_tensor(a, a, b, ALU.add).then_inc(qk_ready, 1)

            taps(0, 14)
            for j in range(4):
                rotate(j)
            taps(14, TAPS)

            def decayed(h):
                dve.wait_ge(score_psum, h + 1)
                if h >= 2:
                    dve.wait_ge(ret_psum, h - 1)
                for j in range(TT):
                    ins = nc.vector.scalar_tensor_tensor(out=score[:, h % 2, j], in0=MISC[h % 2][:, T * j:T * j + T],
                                                         scalar=float(P) ** -0.5,
                                                         in1=decay[:, h, P * (1 - j):P * (1 - j) + T],
                                                         op0=ALU.mult, op1=ALU.mult)
                ins.then_inc(score_ready, 1)

            def gated(h):
                dve.wait_ge(ret_rstd, h + 1)
                dve.wait_ge(g_ready, 2)
                link(nc.vector.tensor_tensor(ret[:, h], ret[:, h], head_rstd[:, h % 2], ALU.mult))
                nc.vector.tensor_tensor(mixT[:, MT + h], ret[:, h], gsilu[:, h], ALU.mult).then_inc(ret_ready, 1)

            for h in range(HEADS):
                decayed(h)
                if h >= 1:
                    gated(h - 1)
            gated(HEADS - 1)

            dve.wait_ge(conv_ready, 1)
            dve.wait_ge(mean_psum, 1)
            link(nc.vector.tensor_scalar(mean[:, 0], STAT[:, 0:T], 1.0 / MIX, None, ALU.mult))
            nc.vector.tensor_tensor(conv, conv, mean.to_broadcast([P, MT, T]), ALU.subtract).then_inc(centred, 1)
            dve.wait_ge(ln_rstd, 1)
            for k in range(MT):
                nc.vector.scalar_tensor_tensor(out=conv[:, k], in0=conv[:, k], scalar=col("cln_g", k), in1=rstd[:, :],
                                               op0=ALU.mult, op1=ALU.mult).then_inc(ln_scaled, 1)
            modulation(1)
            dve.wait_ge(mods_ready, 2)
            residual("w_out", lambda k: mod(0, GATE_M, k))
            modulation(2)
            gain(1)
            normed(1, lambda k: gains[:, 1, k:k + 1])

            def square_unit(base, n):
                dve.wait_ge(hid_relu, base + n + 1)
                a = hid[:, 2 * n:2 * n + 2]
                nc.vector.tensor_tensor(a, a, a, ALU.mult).then_inc(hid_ready, 1)

            def reduce_angle(dst, src, k):
                link(nc.vector.tensor_scalar(k, src, 0.5 / np.pi, SINGLE, ALU.mult, ALU.add))
                link(nc.vector.tensor_scalar(k, k, SINGLE, None, ALU.subtract))
                for n, part in enumerate(TWO_PI):
                    link(nc.vector.scalar_tensor_tensor(out=dst, in0=k, scalar=-part, in1=src if n == 0 else dst,
                                                        op0=ALU.mult, op1=ALU.add))
                return nc.vector.tensor_scalar(dst, dst, PI, -PI, ALU.min, ALU.max)

            def product(out_re, out_im, a, b, tmp, c=None):
                tt = nc.vector.tensor_tensor
                tt(out_re, a[0], b[0], ALU.mult)
                link(tt(tmp, a[1], b[1], ALU.mult))
                link(tt(out_re, out_re, tmp, ALU.subtract))
                tt(out_im, a[0], b[1], ALU.mult)
                link(tt(tmp, a[1], b[0], ALU.mult))
                return tt(out_im, out_im, tmp, ALU.add)

            def s5_steps():
                dve.wait_ge(lam_psum, 1)
                nc.vector.tensor_scalar(s5_lr, MISC[0][:, 0:64], -1e-4, None, ALU.min)
                dve.wait_ge(s5_fun, 1)
                link(nc.vector.tensor_copy(s5_li, MISC[0][:, 64:128]))
                nc.vector.tensor_tensor(s5_th, s5_li, s5_dt, ALU.mult)
                nc.vector.tensor_tensor(s5_a, s5_lr, s5_dt, ALU.mult).then_inc(s5_args, 1)
                dve.wait_ge(s5_args, 1)
                reduce_angle(s5_r, s5_th, s5_k).then_inc(s5_args, 1)

            def s5_discretize():
                tt, ts, stt = nc.vector.tensor_tensor, nc.vector.tensor_scalar, nc.vector.scalar_tensor_tensor
                dve.wait_ge(s5_fun, 3)
                link(tt(s5_cos, s5_cos, s5_cos, ALU.mult))
                link(ts(s5_cos, s5_cos, -2.0, 1.0, ALU.mult, ALU.add))
                tt(s5_abi, s5_mag, s5_sin, ALU.mult)
                link(tt(s5_abr, s5_mag, s5_cos, ALU.mult))
                ts(s5_nr, s5_abr, -1.0, None, ALU.add)
                tt(s5_den, s5_lr, s5_lr, ALU.mult)
                link(tt(s5_t1, s5_li, s5_li, ALU.mult))
                link(tt(s5_den, s5_den, s5_t1, ALU.add))
                nc.vector.reciprocal(s5_rden, s5_den)
                tt(s5_fr, s5_nr, s5_lr, ALU.mult)
                link(tt(s5_t1, s5_abi, s5_li, ALU.mult))
                link(tt(s5_fr, s5_fr, s5_t1, ALU.add))
                tt(s5_fi, s5_abi, s5_lr, ALU.mult)
                link(tt(s5_t2, s5_nr, s5_li, ALU.mult))
                link(tt(s5_fi, s5_fi, s5_t2, ALU.subtract))
                tt(s5_fr, s5_fr, s5_rden, ALU.mult)
                link(tt(s5_fi, s5_fi, s5_rden, ALU.mult))
                nc.vector.memset(powers[:, 0, 0], 1.0)
                nc.vector.memset(powers[:, 1, 0], 0.0)
                nc.vector.tensor_copy(powers[:, 0, 1], s5_abr)
                link(nc.vector.tensor_copy(powers[:, 1, 1], s5_abi))
                base = (s5_abr, s5_abi)
                for n in range(2, L + 1):
                    link(product(powers[:, 0, n], powers[:, 1, n], (powers[:, 0, n - 1], powers[:, 1, n - 1]), base,
                                 s5_t1))
                for ri in range(2):
                    nc.vector.tensor_copy(pow_in[0:64, ri], powers[0:64, ri, 0:L].rearrange("p n g -> p g n")[:, :, ::-1])
                    nc.vector.tensor_copy(pow_in[64:128, ri], powers[64:128, ri, 0:L].rearrange("p n g -> p g n"))
                    nc.vector.tensor_copy(pow_out[0:64, ri], powers[0:64, ri, 1:L + 1].rearrange("p n g -> p g n"))
                    link(nc.vector.tensor_copy(pow_out[64:128, ri],
                                               powers[64:128, ri, 1:L + 1].rearrange("p n g -> p g n")[:, :, ::-1]))
                dve.wait_ge(braw_here, 64)
                shape = [P, GROUPS, GC]
                f = tuple(x.unsqueeze(2).to_broadcast(shape) for x in (s5_fr, s5_fi))
                nc.vector.memset(b_bar[:, :, GROUPS], 0.0)
                link(product(b_bar[:, 0, 0:GROUPS], b_bar[:, 1, 0:GROUPS], f, (b_raw[:, 0], b_raw[:, 1]),
                             s5_tmp.rearrange("p (g c) -> p g c", g=GROUPS)))

            def s5_kernels(m):
                dve.wait_ge(kext_psum, m + 1)
                if m > 0:
                    dve.wait_ge(k_stored, 64 * m)
                else:
                    dve.wait_ge(dq_here, 64)
                edge = (L - 1) * GC
                nc.vector.tensor_copy(kext[:, :, 0:edge], STAT[:, 0:2 * P].rearrange("p (a x) -> p a x", a=2)[:, :, 0:edge])
                link(nc.vector.tensor_copy(kext[:, :, edge:WIN], MISC[2][:, 0:2 * P].rearrange("p (a x) -> p a x", a=2)))
                for a in range(2):
                    d = s5_dq[:, 2 * m + a:2 * m + a + 1]
                    mid = kext[:, a, edge:P]
                    ins = nc.vector.scalar_tensor_tensor(out=mid, in0=table("ident16"), scalar=d, in1=mid, op0=ALU.mult,
                                                         op1=ALU.add)
                ins.then_inc(kext_ready, 1)

            def s5_tile(m):
                if m > 0:
                    s5_kernels(m - 1)
                    dve.wait_ge(we_psum, 4 * m)
                    dve.wait_ge(ca_stored, 16 * m)
                else:
                    dve.wait_ge(crow_psum, 4)
                    dve.wait_ge(c_copied, 4)
                shape = [P, 8, L, GC]
                groups = slice(8 * m, 8 * m + 8)
                tmp = s5_tmp.rearrange("p (g j c) -> p g j c", g=8, j=L)

                def wide(x):
                    return x.rearrange("p g (j c) -> p g j c", j=L)

                p_in = [pow_in[:, ri, groups].unsqueeze(3).to_broadcast(shape) for ri in range(2)]
                b = [b_bar[:, ri, groups].unsqueeze(2).to_broadcast(shape) for ri in range(2)]
                product(wide(we_src[:, 0]), wide(we_src[:, 1]), p_in, b, tmp).then_inc(we_ready, 1)
                p_out = [pow_out[:, ri, groups].unsqueeze(3).to_broadcast(shape) for ri in range(2)]
                c, minus = [s5_c[:, ri, groups].unsqueeze(2).to_broadcast(shape) for ri in range(2)]
                tt = nc.vector.tensor_tensor
                re, im = wide(ca_src[:, 0]), wide(ca_src[:, 1])
                dve.wait_ge(we_ready, m + 1)
                tt(re, p_out[0], c, ALU.mult)
                link(tt(tmp, p_out[1], minus, ALU.mult))
                link(tt(re, re, tmp, ALU.add))
                tt(im, p_out[0], minus, ALU.mult)
                link(tt(tmp, p_out[1], c, ALU.mult))
                tt(im, im, tmp, ALU.subtract).then_inc(ca_ready, 1)

            for n in range(16):
                square_unit(0, n)
                if n == 0:
                    s5_steps()
                if n == 1:
                    s5_discretize()
                if n in S5_AT_FC1:
                    s5_tile(S5_AT_FC1.index(n))
            s5_tile(5)
            gate_f = lambda k: mod(0, GATE_F, k)
            residual("fc2_0", gate_f, 0, 1)
            s5_tile(6)
            residual("fc2_0", gate_f, 1, 2)
            s5_tile(7)
            residual("fc2_0", gate_f, 2, 3)
            s5_kernels(7)
            for g in range(3, 6):
                modulation(g)
            gain(2)
            gain(3)
            rshape = [P, GROUPS, NCH]
            link(nc.vector.tensor_scalar(s5_t1, s5_r, float(L), None, ALU.mult))
            link(reduce_angle(s5_t2, s5_t1, s5_k))
            nc.vector.memset(shrink[:, :, 0:1], 0.0)
            link(nc.vector.tensor_tensor(rot_cos, s5_t2.unsqueeze(2).to_broadcast(rshape),
                                         table("steps").unsqueeze(1).to_broadcast(rshape), ALU.mult))
            reduce_angle(rot_cos, rot_cos, rot_k).then_inc(rot_args, 1)
            dve.wait_ge(rot_fun, 1)
            link(nc.vector.tensor_tensor(rot_cos, rot_cos, rot_cos, ALU.mult))
            link(nc.vector.tensor_scalar(rot_cos, rot_cos, -2.0, 1.0, ALU.mult, ALU.add))
            residual("fc2_0", gate_f, 3, 4)

            normed(2, lambda k: gains[:, 2, k:k + 1])
            for kh in range(2):
                dve.wait_ge(s5_rows, 2 * kh + 2)
                for j in range(4):
                    ins = nc.vector.tensor_copy(h_rows[:, 32 * kh:32 * kh + 32, 4 + j],
                                                PS[2 * kh + 1][32 * j:32 * j + 32, :].rearrange("s (g c) -> s g c", c=GC))
                ins.then_inc(rows_dve, 1)
            for b in range(4):
                dve.wait_ge(u_psum, b + 1)
                if b == 0:
                    dve.wait_ge(h_ready, 8 * 3)
                nc.vector.tensor_copy(u_in[:, 16 * b:16 * b + 16].rearrange("p g s -> p (g s)"), PS[b][:, :])\
                    .then_inc(s5_u, 1)
            tt = nc.vector.tensor_tensor
            for hh in range(2):
                dve.wait_ge(s5_e, 4 * hh + 4)
                gs = slice(32 * hh, 32 * hh + 32)

                def flat(x):
                    return x.rearrange("p g s -> p (g s)")

                def by_group(x):
                    return x.rearrange("p (g s) -> p g s", g=32)

                cos, sin, keep = flat(rot_cos[:, gs]), flat(rot_sin[:, gs]), flat(shrink[:, gs])
                e_re, e_im = flat(state[:, 0, gs]), flat(state[:, 1, gs])
                t = half_t
                tt(t[0], cos, e_re, ALU.mult)
                link(tt(t[1], sin, e_im, ALU.mult))
                tt(t[0], t[0], t[1], ALU.add)
                tt(t[2], cos, e_im, ALU.mult)
                link(tt(t[3], sin, e_re, ALU.mult))
                link(tt(t[2], t[2], t[3], ALU.subtract))
                nc.vector.tensor_tensor_scan(out=t[1], data0=keep, data1=t[0], initial=0.0, op0=ALU.mult, op1=ALU.add)
                link(nc.vector.tensor_tensor_scan(out=t[3], data0=keep, data1=t[2], initial=0.0, op0=ALU.mult,
                                                  op1=ALU.add))
                for ri in range(2):
                    nc.vector.memset(state[0:64, ri, gs, 0:1], 0.0)
                    nc.vector.memset(state[64:128, ri, gs, NCH - 1:NCH], 0.0)
                    a, b = (t[1], t[3]) if ri == 0 else (t[3], t[1])
                    tt(t[0], cos, a, ALU.mult)
                    link(tt(t[2], sin, b, ALU.mult))
                    op = ALU.subtract if ri == 0 else ALU.add
                    x, y = by_group(t[0]), by_group(t[2])
                    tt(state[0:64, ri, gs, 1:NCH], x[0:64, :, 0:NCH - 1], y[0:64, :, 0:NCH - 1], op)
                    ins = tt(state[64:128, ri, gs, 0:NCH - 1][:, :, ::-1], x[64:128, :, 0:NCH - 1],
                             y[64:128, :, 0:NCH - 1], op)
                    if ri == 0:
                        link(ins)
                ins.then_inc(state_ready, 1)
                dve.wait_ge(state_ready, hh + 1)
            for n in range(4):
                dve.wait_ge(z_psum, n + 1)
                nc.vector.tensor_copy(mixT[:, 2 * n:2 * n + 2].rearrange("p k (s j) -> p k s j", j=L),
                                      MISC[n % 2][:, :].rearrange("p (k j s) -> p k s j", k=2, j=L)).then_inc(z_ready, 1)
            for n in range(4):
                dve.wait_ge(glu_sig, n + 1)
                ps = unit("glu", 2 * n + 1)
                if n >= 1:
                    dve.wait_ge(x_ready, 12 + n)
                tt(glu_prod, ps, glu_gate, ALU.mult).then_inc(glu_mul, 1)
                dve.wait_ge(glu_mul, n + 1)
                for i in range(2):
                    k = 2 * n + i
                    ins = nc.vector.scalar_tensor_tensor(out=xT[:, k], in0=glu_prod[:, i], scalar=mod(1, GATE_M, k),
                                                         in1=xT[:, k], op0=ALU.mult, op1=ALU.add)
                ins.then_inc(x_ready, 1)
            normed(3, lambda k: gains[:, 3, k:k + 1])
            for n in range(16):
                square_unit(16, n)
            residual("fc2_1", lambda k: mod(1, GATE_F, k))

            dve.wait_ge(positions_here, 16)
            link(nc.vector.tensor_copy(rope_cos, positions[:, :]))
            link(nc.vector.tensor_scalar(rope_cos, rope_cos, table("inv_freq"), None, ALU.mult))
            link(reduce_angle(angle, rope_cos, angle_k))
            nc.vector.tensor_copy(angle_k, angle).then_inc(angle_ready, 1)
            dve.wait_ge(rstd_ready, 5)
            for k in range(DT):
                ins = nc.vector.scalar_tensor_tensor(out=xT[:, k], in0=xT[:, k], scalar=col("norm_f", k), in1=rstd[:, :],
                                                     op0=ALU.mult, op1=ALU.mult)
                if k % 2:
                    ins.then_inc(x_ready, 1)
            for n in range(2):
                dve.wait_ge(p_psum, n + 1)
                nc.vector.tensor_copy(p_tiles[:, 2 * n:2 * n + 2], pair(MISC[n])).then_inc(p_ready, 1)
            dve.wait_ge(angle_fun, 1)
            nc.vector.tensor_scalar(rope_sin, rope_sin, table("rot_sign"), None, ALU.mult)
            link(nc.vector.tensor_tensor(rope_cos, rope_cos, rope_cos, ALU.mult))
            link(nc.vector.tensor_scalar(rope_cos, rope_cos, -2.0, 1.0, ALU.mult, ALU.add))

            def plain_norm(i, name, dst, first=0):
                dve.wait_ge(rstd_ready, i + 1)
                for k in range(DT):
                    nc.vector.scalar_tensor_tensor(out=dst[:, k], in0=xT[:, k], scalar=col(name, first + k),
                                                   in1=rstd[:, :], op0=ALU.mult, op1=ALU.mult).then_inc(hn_ready, 1)

            nc.vector.memset(padded.rearrange("p s (k n) -> p (s k) n", k=2)[:, :, 0:3], 0.0).then_inc(pad_zero, 1)
            plain_norm(5, "ssm_norm_w_2", hT)

            def convolve(m):
                dve.wait_ge(xbc_copied, m + 1)
                if m >= 2:
                    dve.wait_ge(xbc_ready, m - 1)
                src = padded[:, m % 4].rearrange("p (k n) -> p k n", k=2)
                for tap in range(4):
                    for i in range(2):
                        tile = 16 + 2 * m + i if m < 4 else 2 * (m - 4) + i
                        w = col("ssm_conv_w_2", 24 * tap + tile)
                        dst = convolved[:, m % 2, T * i:T * i + T]
                        if tap == 0:
                            step(nc.vector.tensor_scalar(dst, src[:, i, 0:T], w, None, ALU.mult))
                            continue
                        behind(1)
                        ins = nc.vector.scalar_tensor_tensor(out=dst, in0=src[:, i, tap:tap + T], scalar=w, in1=dst,
                                                             op0=ALU.mult, op1=ALU.add)
                        if tap == 3 and i == 1:
                            ins.then_inc(xbc_conv, 1)
                        else:
                            step(ins)

            def step_sizes():
                tt, ts, stt = nc.vector.tensor_tensor, nc.vector.tensor_scalar, nc.vector.scalar_tensor_tensor
                dve.wait_ge(dt_fun, 1)
                link(ts(dt_s, dt_e, 2.0, None, ALU.add))
                link(nc.vector.reciprocal(dt_s, dt_s))
                link(tt(dt_s, dt_s, dt_e, ALU.mult))
                link(tt(dt_e, dt_s, dt_s, ALU.mult))
                link(ts(dt_p, dt_e, 1.0 / 17, 1.0 / 15, ALU.mult, ALU.add))
                for n in (13, 11, 9, 7, 5, 3, 1):
                    link(tt(dt_p, dt_p, dt_e, ALU.mult))
                    link(ts(dt_p, dt_p, 1.0 / n, None, ALU.add))
                link(tt(dt_p, dt_p, dt_s, ALU.mult))
                link(ts(dt_y, dt_y, 0.0, None, ALU.max))
                for i in range(TT):
                    link(stt(out=dt_y[:, i], in0=dt_p[:, i], scalar=2.0, in1=dt_y[:, i], op0=ALU.mult, op1=ALU.add))
                    ins = stt(out=dta[:, i], in0=dt_y[:, i], scalar=-1.0, in1=a_rows, op0=ALU.mult, op1=ALU.mult)
                ins.then_inc(dta_ready, 1)

            def weigh_by_dt(n):
                dve.wait_ge(xt_psum, n + 1)
                ps = (STAT, MISC[2])[n % 2][:, :].rearrange("p (k t h c) -> p k t h c", k=2, t=TT, h=2)
                for i in range(2):
                    tile = 2 * n + i
                    ins = nc.vector.tensor_tensor(
                        xdt[:, :, P * tile:P * tile + P].rearrange("p t (h c) -> p t h c", h=2), ps[:, i],
                        dt_y[:, :, 2 * tile:2 * tile + 2].unsqueeze(3).to_broadcast([P, TT, 2, SSM_DIM]), ALU.mult)
                ins.then_inc(xdt_ready, 1)

            def segments(t):
                dve.wait_ge(seg_psum, t + 1)
                if t >= 2:
                    dve.wait_ge(y_psum, t - 1)
                for h in range(2):
                    rows = MISC[t % 2][:, T * h:T * h + T]
                    for i, (dst, src) in enumerate(((slice(0, T), slice(0, T)), (slice(T, SEG), slice(P, T)))):
                        ins = nc.vector.tensor_scalar(seg[:, t % 2, h, dst], rows[:, src],
                                                      a_cum[:, i, 2 * t + h:2 * t + h + 1], 0.0, ALU.subtract, ALU.min)
                ins.then_inc(seg_ready, 1)

            for m in range(XBC_UNITS):
                if m == 0:
                    dve.wait_ge(dt_psum, 1)
                    dve.wait_ge(small_here, 16 * 6)
                    ps = MISC[0][:, 0:TT * SSM_HEADS].rearrange("p (t h) -> p t h", t=TT)
                    link(nc.vector.tensor_tensor(dt_y, ps, dt_bias.unsqueeze(1).to_broadcast([P, TT, SSM_HEADS]), ALU.add))
                    link(nc.vector.tensor_scalar(dt_p, dt_y, -1.0, None, ALU.mult))
                    nc.vector.tensor_tensor(dt_s, dt_y, dt_p, ALU.max).then_inc(dt_args, 1)
                convolve(m)
                if m == 0:
                    step_sizes()
                if m == 2:
                    dve.wait_ge(a_cum_psum, 1)
                    nc.vector.tensor_copy(a_cum, MISC[1][:, 0:TT * SSM_HEADS].rearrange("p (t h) -> p t h", t=TT))
                    nc.vector.tensor_copy(a_cum_rows[0:SSM_HEADS, :], MISC[2][0:SSM_HEADS, 0:T]).then_inc(a_cum_ready, 1)
                    dve.wait_ge(a_cum_ready, 1)
                if m in (6, 7):
                    for g in (2 * (m - 6), 2 * (m - 6) + 1):
                        dve.wait_ge(cb_psum, g + 1)
                        nc.vector.tensor_tensor(cb[:, g], MISC[g % 2][:, 0:SEG], table("tri"), ALU.mult)\
                            .then_inc(cb_ready, 1)
                if m >= 6:
                    weigh_by_dt(m - 6)
            segments(0)
            segments(1)
            weigh_by_dt(6)
            weigh_by_dt(7)
            for t in range(Z_TILES):
                dve.wait_ge(y_psum, t + 1)
                nc.vector.scalar_tensor_tensor(out=xs[:, t], in0=xs[:, t], scalar=d_cols[:, t:t + 1],
                                               in1=(STAT, MISC[2])[t % 2][:, 0:T], op0=ALU.mult, op1=ALU.add)\
                    .then_inc(y_skipped, 1)
                if t + 2 < Z_TILES:
                    segments(t + 2)
            for t in range(Z_TILES):
                g = t // 4
                if t % 4 == 0:
                    dve.wait_ge(group_rstd_ready, g + 1)
                nc.vector.scalar_tensor_tensor(out=xs[:, t], in0=xs[:, t], scalar=col("ssm_gnorm_w_2", t),
                                               in1=group_rstd[:, g % 2], op0=ALU.mult, op1=ALU.mult).then_inc(y_ready, 1)

            def add_projection(phase):
                for n in range(4):
                    nc.vector.tensor_tensor(xT[:, 2 * n:2 * n + 2], xT[:, 2 * n:2 * n + 2], unit(phase, n), ALU.add)\
                        .then_inc(x_ready, 1)

            add_projection("ssm_out")

            def embedding(layer, norm):
                plain_norm(norm, "ple_norm_w_2", hT, 8 * layer)
                for n in range(4):
                    dve.wait_ge(ple_sig, 4 * layer + n + 1)
                    g = ple_gate[:, n % 2].rearrange("p (k n) -> p k n", k=2)
                    a = ple_prod[:, 2 * n:2 * n + 2]
                    nc.vector.tensor_tensor(a, a, g, ALU.mult).then_inc(ple_mul, 1)
                    dve.wait_ge(ple_mul, 4 * layer + n + 1)
                    nc.vector.tensor_tensor(xT[:, 2 * n:2 * n + 2], xT[:, 2 * n:2 * n + 2], a, ALU.add)\
                        .then_inc(x_ready, 1)

            embedding(0, 6)

            plain_norm(7, "kv_norm_w_2", mixT)
            plain_norm(7, "attn_norm_w_2", hT)

            def head_normed(m):
                dve.wait_ge(qk2_rstd, m + 1)
                for i in range(2):
                    a = qk2[:, 2 * m + i]
                    ins = nc.vector.scalar_tensor_tensor(out=a, in0=a, scalar=col("q_norm_w_2" if m else "k_norm_w_2", 0),
                                                         in1=head_rstd2[:, m % 2, T * i:T * i + T], op0=ALU.mult,
                                                         op1=ALU.mult)
                ins.then_inc(qk2_normed, 1)

            def rotate2(m):
                dve.wait_ge(qk2_swapped, m + 1)
                a, b = qk2[:, 2 * m:2 * m + 2], swap2[:, m % 2].rearrange("p (k n) -> p k n", k=2)
                nc.vector.tensor_tensor(a, a, rope_cos.unsqueeze(1).to_broadcast([P, 2, T]), ALU.mult)
                link(nc.vector.tensor_tensor(b, b, rope_sin.unsqueeze(1).to_broadcast([P, 2, T]), ALU.mult))
                nc.vector.tensor_tensor(a, a, b, ALU.add).then_inc(qk2_ready, 1)

            for m in range(5):
                head_normed(m)
                if m >= 1:
                    rotate2(m - 1)
            rotate2(4)

            def masked(t):
                dve.wait_ge(s_psum, t + 1)
                if t >= 2:
                    dve.wait_ge(pt_psum, 2 * (t - 1))
                for h in range(2):
                    ins = nc.vector.scalar_tensor_tensor(out=probs[:, t % 2, h], in0=MISC[h][:, 0:SEG], scalar=64 ** -0.5,
                                                         in1=table("window"), op0=ALU.mult, op1=ALU.add)
                ins.then_inc(s_masked, 1)
                dve.wait_ge(s_masked, t + 1)
                for h in range(2):
                    for b, (lo, hi) in enumerate(((0, P), (P, SEG))):
                        ins = nc.vector.tensor_reduce(row_max[:, t, 2 * h + b:2 * h + b + 1], probs[:, t % 2, h, lo:hi],
                                                      AX.X, ALU.max)
                link(ins)
                sink = sinks[:, 2 * t:2 * t + 2].unsqueeze(2).to_broadcast([P, 2, 2])

                def by_head(x):
                    return x[:, t].rearrange("p (h b) -> p h b", h=2)

                link(nc.vector.tensor_tensor(by_head(row_max), by_head(row_max), sink, ALU.max))
                nc.vector.tensor_scalar(neg_max[:, t], row_max[:, t], -1.0, None, ALU.mult)
                nc.vector.tensor_tensor(by_head(sink_arg), sink, by_head(row_max), ALU.subtract).then_inc(s_max, 1)

            def normalised(t):
                dve.wait_ge(s_exp, t + 1)
                link(nc.vector.tensor_tensor(row_sum[:, t], row_sum[:, t], sink_exp[:, t], ALU.add))
                link(nc.vector.reciprocal(row_inv[:, t], row_sum[:, t]))
                for h in range(2):
                    for b, (lo, hi) in enumerate(((0, P), (P, SEG))):
                        i = 2 * h + b
                        a = probs[:, t % 2, h, lo:hi]
                        ins = nc.vector.tensor_scalar(a, a, row_inv[:, t, i:i + 1], None, ALU.mult)
                ins.then_inc(probs_ready, 1)

            masked(0)
            for t in range(ATT_TILES):
                if t + 1 < ATT_TILES:
                    masked(t + 1)
                normalised(t)
                dve.wait_ge(o_psum, t + 1)
                dve.wait_ge(g2_ready, 4)
                nc.vector.tensor_tensor(mixT[:, t], PS[t % 2][:, 0:T], g2[:, t], ALU.mult).then_inc(o_ready, 1)
            add_projection("attn_out")
            embedding(1, 8)


N_STACK_LOADS = sum(2 if name in ("k_norm_w_2", "q_norm_w_2") else 1 for rows in STACKS for name, _ in rows)

INPUTS = [
    "x", "c", "norm_g", "ada_w", "ada_b", "w_in", "conv_w", "conv_b", "cln_g", "cln_b", "w_out", "s5_lam_re",
    "s5_lam_im", "s5_log_step", "s5_b_re", "s5_b_im", "s5_c_re", "s5_c_im", "s5_d", "w_glu_a", "w_glu_b", "w_fc1",
    "w_fc2", "norm_f", "p_2", "positions_2", "ssm_norm_w_2", "ssm_in_w_2", "ssm_conv_w_2", "ssm_conv_b_2",
    "ssm_dt_bias_2", "ssm_a_log_2", "ssm_d_2", "ssm_gnorm_w_2", "ssm_out_w_2", "kv_norm_w_2", "kv_w_2",
    "k_norm_w_2", "attn_norm_w_2", "attn_in_w_2", "q_norm_w_2", "attn_sinks_2", "attn_out_w_2", "ple_norm_w_2",
    "ple_gate_w_2", "ple_proj_w_2",
]


def build(nc, inputs):
    arrays, dram = {}, {}
    for name in INPUTS:
        a = np.ascontiguousarray(inputs[name])
        arrays[f"in_{name}"] = a
        dram[name] = nc.dram_tensor(f"in_{name}", a.shape, mybir.dt.from_np(a.dtype), kind="ExternalInput").ap()
    arrays["in_const"] = CONST
    dram["const"] = nc.dram_tensor("in_const", CONST.shape, F32, kind="ExternalInput").ap()
    dram["s5_d_flat"] = dram["s5_d"].rearrange("a n -> (a n)")
    for rows in STACKS:
        for name, count in rows:
            a = dram[name]
            if name in ("k_norm_w_2", "q_norm_w_2"):
                dram[name] = a if len(a.shape) == 2 else a.rearrange("(a n) -> a n", a=1)
                continue
            flat = a if len(a.shape) == 1 else a.rearrange(
                {2: "a b -> (a b)", 3: "a b c -> (a b c)"}[len(a.shape)])
            dram[name] = flat.rearrange("(r n) -> r n", n=P)
    dram["w_in"], dram["w_out"] = dram["w_in"][0], dram["w_out"][0]
    dram["glu_a"], dram["glu_b"] = dram["w_glu_a"][0], dram["w_glu_b"][0]
    for layer in range(2):
        dram[f"fc1_{layer}"], dram[f"fc2_{layer}"] = dram["w_fc1"][layer], dram["w_fc2"][layer]
        dram[f"ple_gate_{layer}"] = dram["ple_gate_w_2"][layer]
        dram[f"ple_proj_{layer}"] = dram["ple_proj_w_2"][layer].rearrange("(k p) n -> p k n", p=P)
    dram["ssm_in"], dram["ssm_out"], dram["kv"] = dram["ssm_in_w_2"][0], dram["ssm_out_w_2"][0], dram["kv_w_2"]
    dram["attn_in"], dram["attn_out"] = dram["attn_in_w_2"][0], dram["attn_out_w_2"][0]
    out = nc.dram_tensor("out", (1, T, D), F32, kind="ExternalOutput").ap()
    program(nc, dram, out)
    return arrays


def kernel(**inputs):
    import concourse.bacc as bacc
    from concourse.bass_utils import run_bass_kernel_spmd

    nc = bacc.Bacc("TRN2", target_bir_lowering=False, num_devices=1)
    arrays = build(nc, inputs)
    r = run_bass_kernel_spmd(nc, [arrays], core_ids=[0])
    return r.results[0]["out"]
```

```python
from contextlib import ExitStack

import numpy as np

import concourse.bass as bass
from concourse import mybir

F32 = mybir.dt.float32
F32R = mybir.dt.float32r
I32 = mybir.dt.int32
ALU = mybir.AluOpType
ACT = mybir.ActivationFunctionType
AX = mybir.AxisListType

P = 128
D = 1024
DT = D // P
T = 256
TT = T // P
EPS = 1e-6
KB = 8
NB = 256
RING = 4
BANKS = 4
FF = 4 * D
FT = FF // P

MIX = 512
MT = MIX // P
HEADS = 4
TAPS = 31
PAD = TAPS // 2

GROUPS = 64
GC = 16
L = 8
NCH = T // L
WIN = (2 * L - 1) * GC
PI = 3.1415925
S5_AT_FC1 = (1, 4, 7, 10, 13)
MODULATION_AT_FC1 = (7,)
SINGLE = 1.5 * 2 ** 23
TWO_PI = (6.28125, 0.0019350051879882812, 3.0199159819e-07)

SSM_HEADS = 32
SSM_DIM = 64
SSM_GROUPS = 4
Z_TILES = 2 * D // P
XBC_UNITS = 12
SEG = 3 * P
ATT_TILES = 8
Z_UNITS = [("z", 0), ("z", 1), ("z", 2), ("z", 3), ("z", 4), ("group", 0), ("z", 5), ("z", 6), ("group", 1), ("z", 7),
           ("group", 2), ("group", 3)]
ATT_UNITS = [("gate", 0), ("gate", 1), ("out", 0), ("out", 1), ("gate", 2), ("out", 2), ("out", 3), ("gate", 3),
             ("out", 4), ("out", 5), ("out", 6), ("out", 7)]
PLE = 256

SHIFT_M, SCALE_M, GATE_M, SHIFT_F, SCALE_F, GATE_F = range(6)
ADA_PIECES = 48
PIECES = 8
ADA0_ORDER = (0, 1, 7, 2, 3, 4, 6, 5)
ADA_GROUPS = ADA_PIECES // PIECES


def shape_constants():
    f32 = np.float32
    parts, at, n = [], {}, 0

    def put(name, a):
        nonlocal n
        a = np.asarray(a, f32).reshape(P, -1)
        at[name] = (n, n + a.shape[1])
        parts.append(a)
        n += a.shape[1]

    i = np.arange(P)
    put("ident", np.eye(P))
    put("ones", np.ones((P, P)))
    put("eps", np.full((P, 1), EPS))
    put("halves", (i[:, None] // 64) == (i[None, :] // 64))
    tri = i[:, None] <= i[None, :]
    put("tri", np.concatenate([tri, np.ones((P, P)), tri], 1))
    put("tri_less_one", tri * 1.0 - 1.0)
    put("inv_freq", (f32(10000.0) ** (-(np.arange(32, dtype=f32) * f32(2.0) / f32(64))))[i % 32][:, None])
    put("rot_sign", np.where((i % 64) < 32, -1.0, 1.0)[:, None])
    q, k = i[:, None], i[None, :]
    own, previous = np.where(k <= q, 0.0, -1e30), np.where(k > q, 0.0, -1e30)
    put("window", np.concatenate([own, previous, own], 1))
    put("steps", np.broadcast_to(np.arange(32), (P, 32)))
    put("ident16", np.eye(16)[i % 16])
    half = P // 2
    inv = f32(10000.0) ** (-np.arange(0, P, 2, dtype=f32) / f32(P))
    ang = (np.arange(T, dtype=f32)[:, None] * inv[None, :]).astype(f32)
    cos, sin = np.cos(ang).T, np.sin(ang).T
    put("rope_cos", np.concatenate([cos, cos], 0))
    put("rope_sin", np.concatenate([-sin, sin], 0))
    log_g = np.log1p(-np.exp2(-5.0 - np.arange(HEADS)))
    c = np.arange(3 * P)
    dist = np.abs(c[None, :] - P - i[:, None])
    put("decay", np.exp(log_g[None, :, None] * dist[:, None, :]))
    return np.concatenate(parts, 1).astype(f32), at


CONST, CONST_AT = shape_constants()
FIRST = CONST_AT["halves"][0]
KEPT = CONST_AT["rope_cos"][0]

STACKS = [
    [("conv_w", 4 * TAPS), ("conv_b", 4)],
    [("ada_b", 96), ("norm_g", 32)],
    [("ssm_conv_w_2", 96), ("ssm_conv_b_2", 24), ("s5_d", 8)],
    [("cln_g", 4), ("cln_b", 4), ("norm_f", 8), ("ssm_norm_w_2", 8), ("kv_norm_w_2", 8), ("attn_norm_w_2", 8),
     ("ple_norm_w_2", 16), ("ssm_gnorm_w_2", 16), ("c", 8), ("k_norm_w_2", 1), ("q_norm_w_2", 1)],
]


def weight_plan():
    plan, first = [], {}

    def phase(name, blocks):
        first[name] = len(plan)
        plan.extend(blocks)

    phase("w_in", [("w_in", 0, n) for n in (2, 0, 3, 1, 4, 5, 6, 7, 8, 9, 10, 11)])
    phase("w_out", [("w_out", 0, n) for n in range(4)])
    phase("fc1_0", [("fc1_0", 0, n) for n in range(16)])
    phase("fc2_0", [("fc2_0", k, n) for n in range(4) for k in range(4)])
    phase("s5_in", [("s5_in", 0, n) for n in range(8)])
    phase("s5_out", [b for n in range(4) for b in (("s5_far", 0, 2 * n), ("s5_near", 0, n), ("s5_far", 0, 2 * n + 1))])
    phase("glu", [(m, 0, n) for n in range(4) for m in ("glu_b", "glu_a")])
    phase("fc1_1", [("fc1_1", 0, n) for n in range(16)])
    phase("fc2_1", [("fc2_1", k, n) for n in range(4) for k in range(4)])
    phase("xbc", [("ssm_in", 0, n) for n in (16, 17, 18, 19, *range(8, 16))])
    phase("z", [("ssm_in", 0, n) for n in range(8)])
    phase("ssm_out", [("ssm_out", k, n) for n in range(4) for k in range(2)])
    phase("ple_proj_0", [("ple_proj_0", 0, 0)])
    phase("ple_gate_0", [("ple_gate_0", 0, n) for n in range(4)])
    phase("kv", [("kv", 0, n) for n in range(2)])
    phase("q", [("attn_in", 0, n) for n in range(4)])
    phase("gate", [("attn_in", 0, 4 + n) for n in range(4)])
    phase("attn_out", [("attn_out", 0, n) for n in range(4)])
    phase("ple_proj_1", [("ple_proj_1", 0, 0)])
    phase("ple_gate_1", [("ple_gate_1", 0, n) for n in range(4)])
    return plan, first

SPLIT_LO = {"glu": "vector", "fc1_1": "vector", "fc2_1": "vector", "xbc": "gpsimd", "z": "vector",
            "ssm_out": "vector", "ple_gate_0": "vector", "q": "vector", "gate": "vector",
            "attn_out": "vector", "ple_gate_1": "vector"}
SPLIT_SETS = (("glu", 4), ("fc1_1", 8), ("fc2_1", 16), ("xbc", 8), ("ssm_out", 16), ("ple_gate_0", 8), ("q", 8),
              ("attn_out", 8), ("ple_gate_1", 8))
SET_BASE = {name: sum(n for _, n in SPLIT_SETS[:i]) for i, (name, _) in enumerate(SPLIT_SETS)}


def split_plan(plan, first_block):
    order, place, low = [], {}, {}
    starts = sorted((b, name) for name, b in first_block.items())
    counts = {"vector": 0, "gpsimd": 0}
    for i, (start, name) in enumerate(starts):
        end = starts[i + 1][0] if i + 1 < len(starts) else len(plan)
        for b in range(start, end) if name in SPLIT_LO else ():
            place[b] = len(order)
            order.append(b)
            counts[SPLIT_LO[name]] += 1
            low[b] = (SPLIT_LO[name], counts[SPLIT_LO[name]])
    return order, place, low


def program(nc, dram, out):
    plan, first_block = weight_plan()
    split_order, split_place, split_low = split_plan(plan, first_block)

    ctx = ExitStack()
    with ctx:
        def sb(name, shape, dt=F32):
            return ctx.enter_context(nc.sbuf_tensor(name, shape, dt))

        twins = {}

        def sb_both(name, shape):
            offset = -(-nc.sbuf_base // 32) * 32
            tensor = sb(name, shape)
            twins[tensor.name] = nc.alloc_sbuf_tensor_at(f"{name}_rounded", shape, F32R, offset=offset)
            return tensor

        def sem(name):
            return ctx.enter_context(nc.semaphore(name))

        const = sb("const", [P, KEPT])
        cols = sb("cols", [P, len(STACKS), P])
        ring = sb_both("ring", [P, RING, KB, NB])
        w_high = sb("w_high", [P, 2, KB, NB], F32R)
        ada_w = sb("ada_w", [P, 2, KB, NB])
        ada_sum = sb("ada_sum", [P, 2, PIECES, NB])
        c_act = sb("c_act", [P, DT])
        mods = sb("mods", [P, ADA_GROUPS * PIECES * 2])
        gains = sb("gains", [P, 4, DT])
        xT = sb("xT", [P, DT, T])
        hT = sb_both("hT", [P, DT, T])
        stack = hT[:, 0:2].rearrange("p a n -> p (a n)").rearrange("p (s n) -> p s n", n=P)
        sq = sb_both("sq", [P, DT, T])
        rstd = sb("rstd", [P, T])
        lnv = sb("lnv", [P, T])
        mixT = sb_both("mixT", [P, 2 * MT, T])
        big = sb_both("big", [P, 8192])
        more = sb_both("more", [P, 8192])
        hid = big[:, :].rearrange("p (t n) -> p t n", t=FT)
        s5_small = sb("s5_small", [P, 24, GROUPS])
        s5_c = sb("s5_c", [P, 2, GROUPS, GC])
        s5_dq = sb("s5_dq", [P, GROUPS // 4])
        we_t = sb_both("we_t", [P, 8, 2, P])
        positions = s5_small[:, 0:4].rearrange("p a b -> p (a b)").bitcast(I32)
        we_dram = nc.dram_tensor("we_dram", (8, P, 8 * 2 * P), F32, kind="Internal").ap()
        ca_dram = nc.dram_tensor("ca_dram", (8, P, 8 * 2 * P), F32, kind="Internal").ap()
        k_dram = nc.dram_tensor("k_dram", (GROUPS, GC, WIN), F32, kind="Internal").ap()

        PS = [ctx.enter_context(nc.psum_tensor(f"ps{i}", [P, 512], F32)) for i in range(8)]
        STAT, MISC = PS[4], PS[5:8]

        def pair(ps):
            return ps[:, :].rearrange("p (a n) -> p a n", a=2)

        mixer_tables = we_t[:, :, :, :].rearrange("p a b c -> p (a b c)")[:, 0:CONST.shape[1] - KEPT]

        def table(name):
            a, b = CONST_AT[name]
            if a >= KEPT:
                return mixer_tables[:, a - KEPT:b - KEPT]
            return const[:, a:b]

        ident, ones, eps = table("ident"), table("ones"), table("eps")
        decay = table("decay").rearrange("p (h c) -> p h c", h=HEADS)

        def col(name, n=None):
            for s, rows in enumerate(STACKS):
                at = 0
                for row, count in rows:
                    if row == name:
                        return cols[:, s, at:at + count] if n is None else cols[:, s, at + n:at + n + 1]
                    at += count
            raise KeyError(name)

        def mod(layer, which, n=None):
            at = layer * 48 + which * 8
            return mods[:, at:at + 8] if n is None else mods[:, at + n:at + n + 1]

        def squares(i):
            return hid[:, 0:DT] if i in (3, 7) else sq

        def rounded(x):
            return bass.AP(tensor=twins[x.tensor.name], offset=x.offset, ap=x.ap)

        const_here = sem("const_here")
        tables_here = sem("tables_here")
        w_high_ready = sem("w_high_ready")
        w_low_vector = sem("w_low_vector")
        w_low_gpsimd = sem("w_low_gpsimd")
        a_high = sem("a_high")
        a_low = sem("a_low")
        stack_here = sem("stack_here")
        x_here = sem("x_here")
        ada0_here = [sem(f"ada0_here{i}") for i in range(PIECES)]
        w_here = [sem(f"w_here{i}") for i in range(RING)]
        blocks_done = sem("blocks_done")
        cols_psum = sem("cols_psum")
        cols_ready = sem("cols_ready")
        x_psum = sem("x_psum")
        x_ready = sem("x_ready")
        c_ready = sem("c_ready")
        ada_here = [sem(f"ada_here{i}") for i in range(2)]
        ada_sums = sem("ada_sums")
        ada0_sums = sem("ada0_sums")
        ada_psum = sem("ada_psum")
        mods_ready = sem("mods_ready")
        sq_ready = sem("sq_ready")
        stat_ready = sem("stat_ready")
        rstd_ready = sem("rstd_ready")
        hn_ready = sem("hn_ready")
        h_ready = sem("h_ready")
        act_step = sem("act_step")
        dve_step = sem("dve_step")
        pool_step = sem("pool_step")
        out_done = sem("out_done")
        sg_ready = sem("sg_ready")
        a_ready = sem("a_ready")
        qk_copied = sem("qk_copied")
        qk_ready = sem("qk_ready")
        v_ready = sem("v_ready")
        g_ready = sem("g_ready")
        score_psum = sem("score_psum")
        score_ready = sem("score_ready")
        ret_psum = sem("ret_psum")
        ret_copied = sem("ret_copied")
        ret_stat = sem("ret_stat")
        ret_rstd = sem("ret_rstd")
        ret_ready = sem("ret_ready")
        conv_ready = sem("conv_ready")
        ln_psum = sem("ln_psum")
        centred = sem("centred")
        cen_sq = sem("cen_sq")
        ln_rstd = sem("ln_rstd")
        ln_scaled = sem("ln_scaled")
        conv_mix = sem("conv_mix")
        hid_relu = sem("hid_relu")
        hid_ready = sem("hid_ready")

        lam_here = sem("lam_here")
        braw_here = sem("braw_here")
        crow_here = sem("crow_here")
        logdt_here = sem("logdt_here")
        dq_zero = sem("dq_zero")
        dq_here = sem("dq_here")
        lam_psum = sem("lam_psum")
        crow_psum = sem("crow_psum")
        c_copied = sem("c_copied")
        s5_args = sem("s5_args")
        s5_fun = sem("s5_fun")
        we_ready = sem("we_ready")
        ca_ready = sem("ca_ready")
        we_psum = sem("we_psum")
        we_copied = sem("we_copied")
        we_stored = sem("we_stored")
        ca_stored = sem("ca_stored")
        kext_psum = sem("kext_psum")
        kext_ready = sem("kext_ready")
        k_stored = sem("k_stored")
        rot_args = sem("rot_args")
        rot_fun = sem("rot_fun")
        s5_rows = sem("s5_rows")
        rows_act = sem("rows_act")
        rows_dve = sem("rows_dve")
        u_psum = sem("u_psum")
        s5_u = sem("s5_u")
        s5_e = sem("s5_e")
        state_ready = sem("state_ready")
        s5_z = sem("s5_z")
        z_psum = sem("z_psum")
        z_ready = sem("z_ready")
        glu_sig = sem("glu_sig")
        glu_mul = sem("glu_mul")

        small_here = sem("small_here")
        positions_here = sem("positions_here")
        p_here = sem("p_here")
        p_psum = sem("p_psum")
        p_ready = sem("p_ready")
        angle_ready = sem("angle_ready")
        angle_fun = sem("angle_fun")
        dt_psum = sem("dt_psum")
        dt_w_rounded = sem("dt_w_rounded")
        dt_w_low = sem("dt_w_low")
        dt_args = sem("dt_args")
        dt_fun = sem("dt_fun")
        dta_ready = sem("dta_ready")
        a_cum_psum = sem("a_cum_psum")
        a_cum_ready = sem("a_cum_ready")
        pad_zero = sem("pad_zero")
        xbc_copied = sem("xbc_copied")
        xbc_conv = sem("xbc_conv")
        xbc_ready = sem("xbc_ready")
        cb_psum = sem("cb_psum")
        cb_ready = sem("cb_ready")
        xt_psum = sem("xt_psum")
        xdt_ready = sem("xdt_ready")
        seg_psum = sem("seg_psum")
        seg_ready = sem("seg_ready")
        seg_exp = sem("seg_exp")
        seg_weighed = sem("seg_weighed")
        zs_ready = sem("zs_ready")
        y_psum = sem("y_psum")
        y_skipped = sem("y_skipped")
        y_gated = sem("y_gated")
        group_sq = sem("group_sq")
        group_stat = sem("group_stat")
        group_rstd_ready = sem("group_rstd_ready")
        y_ready = sem("y_ready")
        pp_ready = sem("pp_ready")
        ple_sig = sem("ple_sig")
        ple_mul = sem("ple_mul")
        qk2_copied = sem("qk2_copied")
        qk2_stat = sem("qk2_stat")
        qk2_rstd = sem("qk2_rstd")
        qk2_normed = sem("qk2_normed")
        qk2_swapped = sem("qk2_swapped")
        qk2_ready = sem("qk2_ready")
        k_both_ready = sem("k_both_ready")
        v2_ready = sem("v2_ready")
        g2_ready = sem("g2_ready")
        s_psum = sem("s_psum")
        s_masked = sem("s_masked")
        s_max = sem("s_max")
        s_exp = sem("s_exp")
        probs_ready = sem("probs_ready")
        pt_psum = sem("pt_psum")
        pt_ready = sem("pt_ready")
        o_psum = sem("o_psum")
        o_ready = sem("o_ready")
        out_copied = sem("out_copied")

        def carve(buf, at, *shape):
            n = int(np.prod(shape))
            v = buf[:, at:at + n]
            if len(shape) == 2:
                v = v.rearrange("p (a b) -> p a b", a=shape[0])
            elif len(shape) == 3:
                v = v.rearrange("p (a b c) -> p a b c", a=shape[0], b=shape[1])
            return v, at + n

        at = 0
        sgate, at = carve(big, at, 2, T)
        apad, at = carve(big, at, MT, T + 2 * PAD)
        conv, at = carve(big, at, MT, T)
        qk, at = carve(big, at, 8, T)
        qk_swap, at = carve(big, at, 8, T)
        assert at <= 8192
        at = 0
        vnat, at = carve(more, at, TT, MIX)
        gsilu, at = carve(more, at, MT, T)
        score, at = carve(more, at, 2, 2, T)
        ret, at = carve(more, at, MT, T)
        ret_sq, at = carve(more, at, 2, T)
        head_rstd, at = carve(more, at, 2, T)
        head_ln, at = carve(more, at, 2, T)
        mean, at = carve(more, at, 1, T)
        assert at <= 8192

        (s5_lr, s5_li, s5_dt, s5_a, s5_th, s5_mag, s5_k, s5_r, s5_sin, s5_cos, s5_abr, s5_abi, s5_nr, s5_den, s5_rden,
         s5_fr, s5_fi, s5_t1, s5_t2, s5_logdt) = (s5_small[:, n] for n in range(20))
        lam_rows = s5_small[0:GROUPS, 20:24].rearrange("g a b -> g (a b)").rearrange("g (r n) -> g r n", r=2)
        powers, _ = carve(we_t[:, :, :, :].rearrange("p a b c -> p (a b c)"), 0, 2, L + 1, GROUPS)
        mix_flat = mixT[:, :, :].rearrange("p a b -> p (a b)")
        pow_out, at = carve(mix_flat, 0, 2, GROUPS, L)
        pow_in, at = carve(mix_flat, at, 2, GROUPS, L)
        at = 0
        b_raw, at = carve(more, at, 2, GROUPS, GC)
        c_rows, at = carve(more, at, 2, 8, P)
        we_src, ca_src = (more[:, 2048 * n:2048 * n + 2048].rearrange("p (r g x) -> p r g x", r=2, g=8)
                          for n in range(2))
        b_bar, at = carve(more, at, 2, GROUPS + 1, GC)
        sq_flat = sq[:, :, :].rearrange("p a b -> p (a b)")
        s5_tmp, kext = sq_flat[:, 0:1024], sq_flat[:, 1024:1024 + 2 * WIN].rearrange("p (a x) -> p a x", a=2)
        ada_w_flat = ada_w[:, :, :, :].rearrange("p a b c -> p (a b c)")
        ada_sum_flat = ada_sum[:, :, :, :].rearrange("p a b c -> p (a b c)")
        rot_cos, at = carve(ada_w_flat, 0, GROUPS, NCH)
        rot_sin, at = carve(ada_w_flat, at, GROUPS, NCH)
        shrink, at = carve(ada_sum_flat, 0, GROUPS, NCH)
        rot_k, at = carve(ada_sum_flat, at, GROUPS, NCH)
        h_perm = mix_flat.rearrange("p (k n) -> p k n", k=DT)
        h_rows = big[0:NCH, :].rearrange("s (g j c) -> s g j c", g=GROUPS, j=L)
        u_in = hT[:, :, :].rearrange("p a b -> p (a b)").rearrange("p (g s) -> p g s", g=GROUPS)
        state, at = carve(more, 0, 2, GROUPS, NCH)
        part_t = [more[:, 4096 + 1024 * n:4096 + 1024 * n + 512] for n in range(4)]
        z_rows = big[0:NCH, :].rearrange("s (j n) -> s j n", j=L)
        glu_gate, at = carve(more, 4096, 2, T)
        glu_prod, at = carve(more, at, 2, T)

        zs, at = carve(big, 0, Z_TILES, T)
        xs, at = carve(big, at, Z_TILES, T)
        xdt, at = carve(more, 0, TT, 2 * D)
        bc_tiles, at = carve(more, at, 2 * SSM_GROUPS, T)
        ple_prod, at = carve(more, at, DT, T)
        p_rows, at = carve(s5_c[:, :, :, :].rearrange("p a b c -> p (a b c)"), 0, 2 * TT, PLE)
        p_tiles, at = carve(s5_c[:, :, :, :].rearrange("p a b c -> p (a b c)"), at, 2 * PLE // P, T)
        we_flat = we_t[:, :, :, :].rearrange("p a b c -> p (a b c)")
        rope_cos, at = carve(we_flat, 0, T)
        rope_sin, at = carve(we_flat, at, T)
        angle, at = carve(we_flat, at, T)
        angle_k, at = carve(we_flat, at, T)
        dt_w, at = carve(we_flat, at, KB, SSM_HEADS)
        dt_w_high, at = carve(we_flat, at, KB, SSM_HEADS)
        d_cols, at = carve(we_flat, at, Z_TILES)
        dt_bias, at = carve(we_flat, at, SSM_HEADS)
        a_rows, at = carve(we_flat, at, SSM_HEADS)
        sinks, at = carve(we_flat, at, 2 * ATT_TILES)
        dt_y, at = carve(we_flat, at, TT, SSM_HEADS)
        dt_e, at = carve(we_flat, at, TT, SSM_HEADS)
        dt_s, at = carve(we_flat, at, TT, SSM_HEADS)
        dt_p, at = carve(we_flat, at, TT, SSM_HEADS)
        dta, at = carve(we_flat, at, TT, SSM_HEADS)
        a_cum, at = carve(we_flat, at, TT, SSM_HEADS)
        assert at <= 2048
        cb, at = carve(ada_sum_flat, 0, SSM_GROUPS, SEG)
        seg, at = carve(ada_sum_flat, at, 2, 2, SEG)
        a_cum_rows, at = carve(ada_sum_flat, at, T)
        group_ln, at = carve(ada_sum_flat, at, 2, T)
        assert at <= 4096
        padded, at = carve(ada_w_flat, 0, 4, 2 * (T + 3))
        convolved, at = carve(ada_w_flat, at, 2, 2 * T)
        group_rstd, at = carve(ada_w_flat, at, 2, T)
        assert at <= 4096
        group_squares, _ = carve(ada_w_flat, 0, 2 * 4, T)
        qk2, at = carve(big, 0, 10, T)
        swap2, at = carve(big, at, 2, 2 * T)
        v2, at = carve(big, at, TT, 256)
        k_both, at = carve(big, at, 4, T)
        probs_t, at = carve(big, at, 2, 2, SEG)
        g2, at = carve(more, 0, ATT_TILES, T)
        probs, at = carve(more, at, 2, 2, SEG)
        out_rows, at = carve(big, 6144, TT, D)
        head_ln2, at = carve(ada_w_flat, 0, 2, 2 * T)
        head_rstd2, at = carve(ada_w_flat, at, 2, 2 * T)
        ple_gate, at = carve(ada_w_flat, at, 2, 2 * T)
        head_sq2, at = carve(ada_w_flat, at, 4, T)
        hid_high, _ = carve(more, 0, FT, T)
        y_high, _ = carve(more, 0, Z_TILES, T)
        att_high, _ = carve(more, 4096, ATT_TILES, T)
        row_max, at = carve(ada_sum_flat, 0, ATT_TILES, 4)
        neg_max, at = carve(ada_sum_flat, at, ATT_TILES, 4)
        sink_arg, at = carve(ada_sum_flat, at, ATT_TILES, 4)
        sink_exp, at = carve(ada_sum_flat, at, ATT_TILES, 4)
        row_sum, at = carve(ada_sum_flat, at, ATT_TILES, 4)
        row_inv, at = carve(ada_sum_flat, at, ATT_TILES, 4)

        ready, left, first_unit = [], [], {}
        here = []
        for b, (name, _, _) in enumerate(plan):
            before = here[b - RING] if b >= RING else 0
            here.append(before + 16 * (L if name == "s5_near" else 1))

        def units(phase, blocks_each, leaves):
            first_unit[phase] = len(ready)
            for n, leave in enumerate(leaves):
                ready.append(first_block.get(phase, 0) + (n + 1) * blocks_each)
                left.append(leave)

        units("w_in", 1, [(sg_ready, 1), (a_ready, 1), (sg_ready, 2), (a_ready, 2)]
              + [(qk_copied, n + 1) for n in range(4)] + [(v_ready, 1), (v_ready, 2), (g_ready, 1), (g_ready, 2)])
        units("w_out", 1, [(x_ready, 4 + n + 1) for n in range(4)])
        units("fc1_0", 1, [(hid_relu, n + 1) for n in range(16)])
        units("fc2_0", 4, [(x_ready, 8 + n + 1) for n in range(4)])
        units("s5_in", 1, [(s5_e, n + 1) for n in range(8)])
        units("s5_out", 3, [(s5_z, n + 1) for n in range(4)])
        units("glu", 1, [x for n in range(4) for x in ((glu_sig, n + 1), (glu_mul, n + 1))])
        units("fc1_1", 1, [(hid_relu, 16 + n + 1) for n in range(16)])
        units("fc2_1", 4, [(x_ready, 16 + n + 1) for n in range(4)])
        units("xbc", 1, [(xbc_copied, n + 1) for n in range(XBC_UNITS)])
        units("z", 1, [(zs_ready, n + 1) if kind == "z" else (group_rstd_ready, n + 1) for kind, n in Z_UNITS])
        for n in range(8):
            ready[first_unit["z"] + Z_UNITS.index(("z", n))] = first_block["z"] + n + 1
        units("ssm_out", 2, [(x_ready, 24 + n + 1) for n in range(4)])
        for layer, version in ((0, 7), (1, 9)):
            if layer == 1:
                units("kv", 1, [(qk2_copied, 1), (v2_ready, 1)])
                units("q", 1, [(qk2_copied, 2 + n) for n in range(4)])
                units("gate", 1, [(g2_ready, n + 1) if kind == "gate" else (o_ready, n + 1) for kind, n in ATT_UNITS])
                for n in range(4):
                    ready[first_unit["gate"] + ATT_UNITS.index(("gate", n))] = first_block["gate"] + n + 1
                units("attn_out", 1, [(x_ready, 32 + n + 1) for n in range(4)])
            units(f"ple_proj_{layer}", 0, [(pp_ready, 4 * layer + n + 1) for n in range(4)])
            for n in range(4):
                ready[first_unit[f"ple_proj_{layer}"] + n] = first_block[f"ple_proj_{layer}"] + 1
            units(f"ple_gate_{layer}", 1, [(ple_sig, 4 * layer + n + 1) for n in range(4)])
        units("final", 0, [(out_copied, n + 1) for n in range(4)])

        def load_stacks(engine, which):
            for s in which:
                at = 0
                for name, count in STACKS[s]:
                    a = dram[name]
                    if name in ("k_norm_w_2", "q_norm_w_2"):
                        for h in range(2):
                            engine.dma_start(stack[at:at + 1, s, 64 * h:64 * h + 64], a).then_inc(stack_here, 16)
                    else:
                        engine.dma_start(stack[at:at + count, s, :], a).then_inc(stack_here, 16)
                    at += count

        block = ctx.enter_context(nc.Block())

        @block.sync
        def _(sp):
            sp.dma_start(const[:, 0:FIRST], dram["const"][:, 0:FIRST]).then_inc(const_here, 16)
            load_stacks(sp, (3,))
            sp.dma_start(mixT[:, :, :].rearrange("p (t a) n -> p t (a n)", t=TT),
                         dram["x"][0].rearrange("(t p) d -> p t d", p=P)).then_inc(x_here, 16)
            for n in ADA0_ORDER:
                sp.dma_start((big, more)[n // 4][:, 2048 * (n % 4):2048 * (n % 4) + 2048]
                             .rearrange("p (k n) -> p k n", k=KB),
                             dram["ada_w"][0, :, n * NB:(n + 1) * NB].rearrange("(k p) n -> p k n", p=P))\
                    .then_inc(ada0_here[n], 16)
            for n in ADA0_ORDER[:6]:
                sp.wait_ge(ada0_here[n], 16)
            sp.dma_start(mixer_tables, dram["const"][:, KEPT:]).then_inc(tables_here, 16)
            sp.dma_start(const[:, FIRST:], dram["const"][:, FIRST:KEPT]).then_inc(tables_here, 16)
            for b, (name, kb, nb) in enumerate(plan):
                if b >= RING:
                    sp.wait_ge(blocks_done, b - RING + 1)
                if b == first_block["w_out"] + RING:
                    for ri, part in enumerate(("re", "im")):
                        for d in range(2):
                            sp.dma_start(lam_rows[:, ri, 64 * d:64 * d + 64], dram[f"s5_lam_{part}"][0, d])\
                                .then_inc(lam_here, 16)
                            sp.dma_start(c_rows[:, ri, :, 64 * d:64 * d + 64],
                                         dram[f"s5_c_{part}"][0, d].rearrange("(t g) c p -> (g c) t p", t=8))\
                                .then_inc(crow_here, 16)
                            sp.dma_start(b_raw[64 * d:64 * d + 64, ri],
                                         dram[f"s5_b_{part}"][0, d].rearrange("g p c -> p g c"))\
                                .then_inc(braw_here, 16)
                    for d in range(2):
                        sp.dma_start(s5_logdt[64 * d:64 * d + 64, :],
                                     dram["s5_log_step"][0, d:d + 1, :].partition_broadcast(64)).then_inc(logdt_here, 16)
                    sp.wait_ge(dq_zero, 1)
                    for q in range(4):
                        sp.dma_start(s5_dq[32 * q:32 * q + GC, :],
                                     dram["s5_d_flat"].rearrange("(a q c) -> q c a", q=4, c=GC)[q],
                                     allow_slow_non_contiguous=True).then_inc(dq_here, 16)
                if b == first_block["fc1_1"]:
                    sp.dma_start(dt_w, dram["ssm_in"][:, 5 * D:5 * D + SSM_HEADS].rearrange("(k p) n -> p k n", p=P))\
                        .then_inc(small_here, 16)
                    for dst, src in ((dt_bias, "ssm_dt_bias_2"), (a_rows, "ssm_a_log_2"), (sinks, "attn_sinks_2")):
                        sp.dma_start(dst, dram[src][0:1, :].partition_broadcast(P)).then_inc(small_here, 16)
                    for h in range(2):
                        sp.dma_start(d_cols[64 * h:64 * h + 64, :],
                                     dram["ssm_d_2"].rearrange("a (t h) -> a h t", h=2)[:, h].partition_broadcast(64),
                                     allow_slow_non_contiguous=True).then_inc(small_here, 16)
                    sp.dma_start(positions, dram["positions_2"][0:1, :].partition_broadcast(P))\
                        .then_inc(positions_here, 16)
                    sp.dma_start(p_rows, dram["p_2"].rearrange("l b (t p) n -> p (l b t) n", p=P)).then_inc(p_here, 16)
                if name.startswith("ple_proj"):
                    sp.dma_start(ring[:, b % RING].rearrange("p a b -> p (a b)").rearrange("p (k n) -> p k n", k=PLE // P),
                                 dram[name]).then_inc(w_here[b % RING], 16)
                    continue
                if name == "s5_in" and nb == 0:
                    sp.wait_ge(we_stored, 16 * 8)
                if name == "s5_far" and nb == 0:
                    sp.wait_ge(ca_stored, 16 * 8)
                    sp.wait_ge(k_stored, 64 * 8)
                if name == "s5_in":
                    sp.dma_start(ring[:, b % RING].rearrange("p a b -> p (a b)"), we_dram[nb])\
                        .then_inc(w_here[b % RING], 16)
                    continue
                if name == "s5_far":
                    sp.dma_start(ring[:, b % RING].rearrange("p a b -> p (a b)"), ca_dram[nb])\
                        .then_inc(w_here[b % RING], 16)
                    continue
                if name == "s5_near":
                    for j in range(L):
                        sp.dma_start(ring[GC * j:GC * j + GC, b % RING].rearrange("p a (b x) -> p (a b) x", x=P),
                                     k_dram[16 * nb:16 * nb + 16, :, (L - 1 - j) * GC:(L - 1 - j) * GC + P]
                                     .rearrange("g c x -> c g x")).then_inc(w_here[b % RING], 16)
                    continue
                sp.dma_start(ring[:, b % RING],
                             dram[name][kb * KB * P:(kb + 1) * KB * P, nb * NB:(nb + 1) * NB]
                             .rearrange("(k p) n -> p k n", p=P)).then_inc(w_here[b % RING], 16)
            for n in range(4):
                sp.wait_ge(out_copied, n + 1)
                sp.dma_start(out[0].rearrange("(t p) d -> p t d", p=P)[:, :, NB * n:NB * n + NB],
                             out_rows[:, :, NB * n:NB * n + NB]).then_inc(out_done, 16)
            sp.wait_ge(out_done, 16 * 4)

        @block.gpsimd
        def _(pool):
            steps = 0
            nc.gpsimd.memset(s5_dq[:, :], 0.0).then_inc(dq_zero, 1)

            def load_piece(n):
                layer, piece = divmod(n, ADA_PIECES // 2)
                pool.dma_start(ada_w[:, n % 2], dram["ada_w"][layer, :, piece * NB:(piece + 1) * NB]
                               .rearrange("(k p) n -> p k n", p=P)).then_inc(ada_here[n % 2], 16)

            for n in range(PIECES):
                pool.wait_ge(ada0_here[n], 16)
            load_piece(PIECES)
            load_piece(PIECES + 1)
            pool.wait_ge(c_ready, 1)
            for n in range(PIECES, ADA_PIECES):
                g, piece = divmod(n, PIECES)
                pool.wait_ge(ada_here[n % 2], 16 * ((n - PIECES) // 2 + 1))
                if piece == 0 and g >= 2:
                    pool.wait_ge(ada_psum, g - 1)
                w = ada_w[:, n % 2]
                nc.gpsimd.tensor_tensor(w, w, c_act[:, :].unsqueeze(2).to_broadcast([P, KB, NB]),
                                        ALU.mult).then_inc(pool_step, 1)
                steps += 1
                pool.wait_ge(pool_step, steps)
                for a in (4, 2):
                    nc.gpsimd.tensor_tensor(w[:, 0:a], w[:, 0:a], w[:, a:2 * a], ALU.add).then_inc(pool_step, 1)
                    steps += 1
                    pool.wait_ge(pool_step, steps)
                nc.gpsimd.tensor_tensor(ada_sum[:, g % 2, piece], w[:, 0], w[:, 1], ALU.add).then_inc(ada_sums, 1)
                pool.wait_ge(ada_sums, n - PIECES + 1)
                if n + 2 < ADA_PIECES:
                    load_piece(n + 2)

            for b in split_order:
                if split_low[b][0] == "gpsimd":
                    for half in range(2):
                        pool.wait_ge(w_high_ready, 2 * split_place[b] + half + 1)
                        ks = slice(4 * half, 4 * half + 4)
                        w = ring[:, b % RING, ks]
                        nc.gpsimd.tensor_tensor(rounded(w), w, w_high[:, split_place[b] % 2, ks],
                                                ALU.subtract).then_inc(w_low_gpsimd, 1)

            def weigh(t):
                pool.wait_ge(seg_exp, t + 1)
                pool.wait_ge(cb_ready, SSM_GROUPS)
                s = seg[:, t % 2]
                nc.gpsimd.tensor_tensor(s, s, cb[:, t // 4].unsqueeze(1).to_broadcast([P, 2, SEG]), ALU.mult)\
                    .then_inc(seg_weighed, 1)

            weigh(0)
            weigh(1)
            for t in range(Z_TILES):
                pool.wait_ge(zs_ready, t // 2 + 1)
                pool.wait_ge(y_skipped, t + 1)
                nc.gpsimd.tensor_tensor(xs[:, t], xs[:, t], zs[:, t], ALU.mult).then_inc(y_gated, 1)
                if t + 2 < Z_TILES:
                    weigh(t + 2)

            for m in range(5):
                pool.wait_ge(qk2_normed, m + 1)
                if m >= 2:
                    pool.wait_ge(qk2_ready, m - 1)
                src, dst = qk2[:, 2 * m:2 * m + 2], swap2[:, m % 2].rearrange("p (k n) -> p k n", k=2)
                for a in (0, 64):
                    nc.gpsimd.tensor_copy(dst[a:a + 32], src[a + 32:a + 64])
                    ins = nc.gpsimd.tensor_copy(dst[a + 32:a + 64], src[a:a + 32])
                ins.then_inc(qk2_swapped, 1)

        @block.scalar
        def _(act):
            steps = [0]

            def link(ins):
                steps[0] += 1
                ins.then_inc(act_step, 1)
                act.wait_ge(act_step, steps[0])

            split_next = [0]

            def round_to(end):
                while split_next[0] < len(split_order) and split_order[split_next[0]] < end:
                    c = split_next[0]
                    b = split_order[c]
                    act.wait_ge(w_here[b % RING], here[b])
                    if c >= 2:
                        act.wait_ge(blocks_done, split_order[c - 2] + 1)
                    for half in range(2):
                        ks = slice(4 * half, 4 * half + 4)
                        nc.scalar.activation(w_high[:, c % 2, ks], ring[:, b % RING, ks], ACT.Copy)\
                            .then_inc(w_high_ready, 1)
                    split_next[0] += 1

            def round_tiles(dst, src, bias=None):
                if bias is None:
                    ins = nc.scalar.activation(rounded(dst), src, ACT.Copy)
                else:
                    ins = nc.scalar.activation(rounded(dst), src, ACT.Identity, bias=bias, scale=1.0)
                ins.then_inc(a_high, 1)

            def round_normed(count):
                for k in range(DT):
                    act.wait_ge(hn_ready, count + k + 1)
                    round_tiles(sq[:, k], hT[:, k])

            def unit(phase, n):
                u = first_unit[phase] + n
                round_to(ready[u] + 1)
                act.wait_ge(blocks_done, ready[u])
                return pair(PS[u % BANKS])

            load_stacks(act, (0, 1, 2))
            act.wait_ge(const_here, 16)
            act.wait_ge(cols_ready, 1)
            nc.scalar.activation(c_act[:, :], col("c"), ACT.Silu).then_inc(c_ready, 1)

            normed_before = (0, 8, 16, 24, 32, 32, 40, 48, 64)

            def norm_squares(i, version):
                for p in range(4):
                    act.wait_ge(x_ready, 4 * version + p + 1)
                    if p == 0 and i > 0:
                        act.wait_ge(stat_ready, i)
                    nc.scalar.activation(squares(i)[:, 2 * p:2 * p + 2], xT[:, 2 * p:2 * p + 2], ACT.Square)\
                        .then_inc(sq_ready, 1)

            def norm_rstd(i):
                act.wait_ge(stat_ready, i + 1)
                if i > 0:
                    act.wait_ge(hn_ready, normed_before[i])
                link(nc.scalar.activation(lnv[:, :], STAT[:, 0:T], ACT.Ln, bias=eps, scale=1.0 / D))
                nc.scalar.activation(rstd[:, :], lnv[:, :], ACT.Exp, scale=-0.5).then_inc(rstd_ready, 1)

            def norm_stats(i, version):
                norm_squares(i, version)
                norm_rstd(i)

            def shift(i, layer, which):
                for k in range(DT):
                    act.wait_ge(hn_ready, 8 * i + k + 1)
                    dst, src = hT[:, k], hT[:, k]
                    if i == 2:
                        dst = h_perm[:, k].rearrange("p (j s) -> p s j", j=L)
                        src = src.rearrange("p (s j) -> p s j", j=L)
                    nc.scalar.activation(dst, src, ACT.Identity, bias=mod(layer, which, k), scale=1.0)\
                        .then_inc(h_ready, 1)

            norm_stats(0, 0)
            shift(0, 0, SHIFT_M)

            for j in range(2):
                ps = unit("w_in", 2 * j)
                if j:
                    act.wait_ge(a_ready, 1)
                nc.scalar.activation(sgate, ps, ACT.Sigmoid).then_inc(sg_ready, 1)
            for j in range(4):
                ps = unit("w_in", 4 + j)
                nc.scalar.activation(qk[:, 2 * j:2 * j + 2], ps, ACT.Copy)
                nc.scalar.activation(qk_swap[0:64, 2 * j:2 * j + 2], ps[64:128], ACT.Copy)
                nc.scalar.activation(qk_swap[64:128, 2 * j:2 * j + 2], ps[0:64], ACT.Copy).then_inc(qk_copied, 1)
            for j in range(2):
                ps = unit("w_in", 8 + j)
                nc.scalar.activation(vnat[:, :, NB * j:NB * j + NB], ps, ACT.Copy).then_inc(v_ready, 1)
            for j in range(2):
                ps = unit("w_in", 10 + j)
                nc.scalar.activation(gsilu[:, 2 * j:2 * j + 2], ps, ACT.Silu).then_inc(g_ready, 1)

            for h in range(HEADS):
                act.wait_ge(ret_psum, h + 1)
                nc.scalar.activation(ret[:, h], MISC[2][:, 0:T], ACT.Copy)
                nc.scalar.activation(ret_sq[:, h % 2], MISC[2][:, 0:T], ACT.Square).then_inc(ret_copied, 1)
                act.wait_ge(ret_stat, h + 1)
                if h >= 2:
                    act.wait_ge(ret_ready, h - 1)
                link(nc.scalar.activation(head_ln[:, h % 2], STAT[:, 0:T], ACT.Ln, bias=eps, scale=1.0 / P))
                nc.scalar.activation(head_rstd[:, h % 2], head_ln[:, h % 2], ACT.Exp, scale=-0.5)\
                    .then_inc(ret_rstd, 1)

            act.wait_ge(centred, 1)
            nc.scalar.activation(sq[:, 0:MT], conv, ACT.Square).then_inc(cen_sq, 1)
            act.wait_ge(ln_psum, 2)
            link(nc.scalar.activation(lnv[:, :], STAT[:, 0:T], ACT.Ln, bias=eps, scale=1.0 / MIX))
            nc.scalar.activation(rstd[:, :], lnv[:, :], ACT.Exp, scale=-0.5).then_inc(ln_rstd, 1)
            for k in range(MT):
                act.wait_ge(ln_scaled, k + 1)
                nc.scalar.activation(mixT[:, k], conv[:, k], ACT.Silu, bias=col("cln_b", k), scale=1.0)\
                    .then_inc(conv_mix, 1)

            def relu_unit(phase, n):
                nc.scalar.activation(hid[:, 2 * n:2 * n + 2], unit(phase, n), ACT.Relu).then_inc(hid_relu, 1)

            def store_kernels(m):
                act.wait_ge(kext_ready, m + 1)
                for q in range(4):
                    act.dma_start(k_dram.rearrange("(a q) c x -> q c a x", q=4)[q, :, 2 * m:2 * m + 2, :],
                                  kext[32 * q:32 * q + GC, :, :]).then_inc(k_stored, 16)

            def s5_tile(m):
                if m > 0:
                    store_kernels(m - 1)
                    act.wait_ge(we_stored, 16 * m)
                for b in range(4):
                    act.wait_ge(we_psum, 4 * m + b + 1)
                    nc.scalar.activation(we_t[:, 2 * b:2 * b + 2].rearrange("p g r x -> p (g r x)"), MISC[b % 2][:, :],
                                         ACT.Copy).then_inc(we_copied, 1)
                act.wait_ge(we_copied, 4 * m + 4)
                act.dma_start(we_dram[m], we_t[:, :, :, :].rearrange("p g r x -> p (g r x)")).then_inc(we_stored, 16)
                act.wait_ge(ca_ready, m + 1)
                act.dma_start(ca_dram[m], more[:, 2048:4096]).then_inc(ca_stored, 16)

            norm_stats(1, 1)
            shift(1, 0, SHIFT_F)
            for n in range(16):
                relu_unit("fc1_0", n)
                if n == 0:
                    act.wait_ge(logdt_here, 32)
                    nc.scalar.activation(s5_dt, s5_logdt, ACT.Exp).then_inc(s5_fun, 1)
                    act.wait_ge(s5_args, 1)
                    nc.scalar.activation(s5_mag, s5_a, ACT.Exp).then_inc(s5_fun, 1)
                if n == 1:
                    act.wait_ge(s5_args, 2)
                    nc.scalar.activation(s5_sin, s5_r, ACT.Sin)
                    nc.scalar.activation(s5_cos, s5_r, ACT.Sin, scale=0.5).then_inc(s5_fun, 1)
                if n in (1, 2):
                    for b in range(2):
                        act.wait_ge(crow_psum, 2 * (n - 1) + b + 1)
                        nc.scalar.activation(s5_c[:, n - 1, 32 * b:32 * b + 32].rearrange("p g c -> p (g c)"),
                                             MISC[1 + b][:, :], ACT.Copy, scale=1.0 if n == 1 else -1.0)\
                            .then_inc(c_copied, 1)
                if n in S5_AT_FC1[1:]:
                    s5_tile(S5_AT_FC1.index(n) - 1)
            s5_tile(4)
            for m in range(5, 8):
                s5_tile(m)
            store_kernels(7)
            act.wait_ge(k_stored, 64 * 8)
            act.wait_ge(rot_args, 1)
            nc.scalar.activation(shrink[:, :, 1:NCH], s5_a.unsqueeze(2).to_broadcast([P, GROUPS, NCH - 1]), ACT.Exp,
                                 scale=float(L))
            nc.scalar.activation(rot_sin, rot_cos, ACT.Sin)
            nc.scalar.activation(rot_cos, rot_cos, ACT.Sin, scale=0.5).then_inc(rot_fun, 1)

            norm_stats(2, 2)
            shift(2, 1, SHIFT_M)
            for kh in range(2):
                act.wait_ge(s5_rows, 2 * kh + 1)
                for j in range(4):
                    ins = nc.scalar.activation(h_rows[:, 32 * kh:32 * kh + 32, j],
                                               PS[2 * kh][32 * j:32 * j + 32, :].rearrange("s (g c) -> s g c", c=GC),
                                               ACT.Copy)
                ins.then_inc(rows_act, 1)
            for n in range(8):
                ps = PS[(first_unit["s5_in"] + n) % BANKS]
                act.wait_ge(blocks_done, ready[first_unit["s5_in"] + n])
                v = ps[:, :].rearrange("p (r g s) -> p r g s", r=2, g=8)
                dst = state[:, :, 8 * n:8 * n + 8]
                nc.scalar.activation(dst[0:64], v[0:64], ACT.Copy)
                nc.scalar.activation(dst[64:128, :, :, ::-1], v[64:128], ACT.Copy).then_inc(s5_e, 1)
            for n in range(4):
                ps = PS[(first_unit["s5_out"] + n) % BANKS]
                act.wait_ge(blocks_done, ready[first_unit["s5_out"] + n])
                for q in range(4):
                    dst = z_rows.rearrange("s j (a q c) -> s q a j c", q=4, c=GC)[:, q, 4 * n:4 * n + 4]
                    ins = nc.scalar.activation(dst, ps[32 * q:32 * q + 32, :].rearrange("s (a j c) -> s a j c", a=4, j=L),
                                               ACT.Gelu_apprx_tanh)
                ins.then_inc(s5_z, 1)
            round_to(first_block["glu"] + 1)
            for n in range(4):
                act.wait_ge(z_ready, n + 1)
                round_tiles(sq[:, 2 * n:2 * n + 2], mixT[:, 2 * n:2 * n + 2])
            for n in range(4):
                ps = unit("glu", 2 * n)
                if n:
                    act.wait_ge(glu_mul, n)
                nc.scalar.activation(glu_gate, ps, ACT.Sigmoid).then_inc(glu_sig, 1)
            round_to(first_block["fc1_1"] + 1)
            norm_stats(3, 3)
            for k in range(DT):
                act.wait_ge(hn_ready, 8 * 3 + k + 1)
                round_tiles(sq[:, k], hT[:, k], mod(1, SHIFT_F, k))
            for n in range(17):
                if n < 16:
                    relu_unit("fc1_1", n)
                if n >= 1:
                    act.wait_ge(hid_ready, 16 + n)
                    round_tiles(hid_high[:, 2 * n - 2:2 * n], hid[:, 2 * n - 2:2 * n])
            round_to(first_block["xbc"] + 1)

            act.wait_ge(small_here, 16 * 6)
            nc.scalar.activation(rounded(dt_w_high), dt_w, ACT.Copy).then_inc(dt_w_rounded, 1)
            norm_stats(4, 4)
            act.wait_ge(angle_ready, 1)
            nc.scalar.activation(rope_sin, angle, ACT.Sin)
            nc.scalar.activation(rope_cos, angle, ACT.Sin, scale=0.5).then_inc(angle_fun, 1)

            norm_stats(5, 5)
            round_normed(32)
            act.wait_ge(pad_zero, 1)
            for m in range(XBC_UNITS):
                ps = unit("xbc", m)
                if m >= 4:
                    act.wait_ge(xbc_conv, m - 3)
                nc.scalar.activation(padded[:, m % 4].rearrange("p (k n) -> p k n", k=2)[:, :, 3:3 + T], ps,
                                     ACT.Copy).then_inc(xbc_copied, 1)
                if m == 0:
                    act.wait_ge(small_here, 16 * 6)
                    nc.scalar.activation(a_rows, a_rows, ACT.Exp)
                    act.wait_ge(dt_args, 1)
                    nc.scalar.activation(dt_e, dt_s, ACT.Exp, scale=-1.0).then_inc(dt_fun, 1)

                def silu(m):
                    act.wait_ge(xbc_conv, m + 1)
                    for i in range(2):
                        tile = 16 + 2 * m + i if m < 4 else 2 * (m - 4) + i
                        dst = bc_tiles[:, 2 * m + i] if m < 4 else xs[:, tile]
                        ins = nc.scalar.activation(dst, convolved[:, m % 2, T * i:T * i + T], ACT.Silu,
                                                   bias=col("ssm_conv_b_2", tile), scale=1.0)
                    ins.then_inc(xbc_ready, 1)

                if m >= 1:
                    silu(m - 1)
            silu(XBC_UNITS - 1)

            def decays(t):
                act.wait_ge(seg_ready, t + 1)
                nc.scalar.activation(seg[:, t % 2], seg[:, t % 2], ACT.Exp).then_inc(seg_exp, 1)

            def group_norm(g):
                act.wait_ge(y_gated, 4 * g + 4)
                if g >= 2:
                    act.wait_ge(group_stat, g - 1)
                nc.scalar.activation(group_squares[:, 4 * (g % 2):4 * (g % 2) + 4], xs[:, 4 * g:4 * g + 4], ACT.Square)\
                    .then_inc(group_sq, 1)
                act.wait_ge(group_stat, g + 1)
                if g >= 2:
                    act.wait_ge(y_ready, 4 * (g - 1))
                ps = PS[(first_unit["z"] + Z_UNITS.index(("group", g))) % BANKS]
                link(nc.scalar.activation(group_ln[:, g % 2], ps[:, 0:T], ACT.Ln, bias=eps, scale=1.0 / (4 * P)))
                nc.scalar.activation(group_rstd[:, g % 2], group_ln[:, g % 2], ACT.Exp, scale=-0.5)\
                    .then_inc(group_rstd_ready, 1)

            decays(0)
            decays(1)
            for n in range(8):
                ps = unit("z", Z_UNITS.index(("z", n)))
                nc.scalar.activation(zs[:, 2 * n:2 * n + 2], ps, ACT.Silu).then_inc(zs_ready, 1)
                if n < 7:
                    decays(2 * n + 2)
                    decays(2 * n + 3)
                if n in (4, 6):
                    group_norm((n - 4) // 2)
            round_to(first_block["ssm_out"] + 2)
            group_norm(2)
            act.wait_ge(y_psum, Z_TILES)
            for t in range(Z_TILES):
                if t == 8:
                    group_norm(3)
                act.wait_ge(y_ready, t + 1)
                round_tiles(y_high[:, t], xs[:, t])

            def embedding(layer, norm, version):
                round_to(first_block[f"ple_gate_{layer}"] + 1)
                norm_squares(norm, version)
                for n in range(4):
                    ps = unit(f"ple_proj_{layer}", n)
                    nc.scalar.activation(ple_prod[:, 2 * n:2 * n + 2], ps, ACT.Copy).then_inc(pp_ready, 1)
                norm_rstd(norm)
                round_normed(normed_before[norm])
                for n in range(4):
                    ps = unit(f"ple_gate_{layer}", n)
                    if n >= 2:
                        act.wait_ge(ple_mul, 4 * layer + n - 1)
                    nc.scalar.activation(ple_gate[:, n % 2].rearrange("p (k n) -> p k n", k=2), ps, ACT.Sigmoid)\
                        .then_inc(ple_sig, 1)

            embedding(0, 6, 6)

            round_to(first_block["q"] + 1)
            norm_stats(7, 7)
            round_normed(56)

            def head_norm(m):
                ps = unit("kv", 0) if m == 0 else unit("q", m - 1)
                if m >= 2:
                    act.wait_ge(qk2_stat, m - 1)
                nc.scalar.activation(head_sq2[:, 2 * (m % 2):2 * (m % 2) + 2], ps, ACT.Square)
                nc.scalar.activation(qk2[:, 2 * m:2 * m + 2], ps, ACT.Copy).then_inc(qk2_copied, 1)
                if m == 0:
                    ps = unit("kv", 1)
                    nc.scalar.activation(v2, ps, ACT.Copy).then_inc(v2_ready, 1)
                act.wait_ge(qk2_stat, m + 1)
                if m >= 2:
                    act.wait_ge(qk2_normed, m - 1)
                link(nc.scalar.activation(head_ln2[:, m % 2], (MISC[2], STAT)[m % 2][:, :], ACT.Ln, bias=eps, scale=1.0 / 64))
                nc.scalar.activation(head_rstd2[:, m % 2], head_ln2[:, m % 2], ACT.Exp, scale=-0.5)\
                    .then_inc(qk2_rstd, 1)

            for m in range(5):
                head_norm(m)
                if m == 2:
                    act.wait_ge(qk2_ready, 1)
                    for g in range(4):
                        lo = 64 * (g % 2)
                        nc.scalar.activation(k_both[0:64, g], qk2[lo:lo + 64, g // 2], ACT.Copy)
                        ins = nc.scalar.activation(k_both[64:128, g], qk2[lo:lo + 64, g // 2], ACT.Copy)
                    ins.then_inc(k_both_ready, 1)

            def exponents(t):
                act.wait_ge(s_max, t + 1)
                for h in range(2):
                    for b, (lo, hi) in enumerate(((0, P), (P, SEG))):
                        i = 2 * h + b
                        nc.scalar.activation(probs[:, t % 2, h, lo:hi], probs[:, t % 2, h, lo:hi], ACT.Exp,
                                             bias=neg_max[:, t, i:i + 1], scale=1.0,
                                             accum_out=row_sum[:, t, i:i + 1])
                nc.scalar.activation(sink_exp[:, t], sink_arg[:, t], ACT.Exp).then_inc(s_exp, 1)

            def copy_turned(t):
                for h in range(2):
                    act.wait_ge(pt_psum, 2 * t + h + 1)
                    if t >= 2 and h == 0:
                        act.wait_ge(o_psum, t - 1)
                    nc.scalar.activation(probs_t[:, t % 2, h], (MISC[2], STAT)[h][:, 0:SEG], ACT.Copy)\
                        .then_inc(pt_ready, 1)

            def round_output(t):
                act.wait_ge(o_ready, t + 1)
                round_tiles(att_high[:, t], mixT[:, t])

            def gate_silu(n):
                nc.scalar.activation(g2[:, 2 * n:2 * n + 2], unit("gate", ATT_UNITS.index(("gate", n))), ACT.Silu)\
                    .then_inc(g2_ready, 1)

            exponents(0)
            gate_silu(0)
            for t in range(ATT_TILES):
                if t in (1, 3, 5):
                    gate_silu((t + 1) // 2)
                if t + 1 < ATT_TILES:
                    exponents(t + 1)
                copy_turned(t)
                if t >= 2:
                    round_output(t - 2)
            round_to(first_block["attn_out"] + 2)
            round_output(ATT_TILES - 2)
            round_output(ATT_TILES - 1)
            embedding(1, 8, 8)
            for n in range(4):
                act.wait_ge(x_psum, 4 + n + 1)
                nc.scalar.activation(out_rows[:, :, NB * n:NB * n + NB], pair(PS[(first_unit["final"] + n) % BANKS]),
                                     ACT.Copy).then_inc(out_copied, 1)

        @block.tensor
        def _(pe):
            def start_unit(phase, n):
                u = first_unit[phase] + n
                if u >= BANKS:
                    pe.wait_ge(*left[u - BANKS])
                return PS[u % BANKS]

            def start_block(phase, n):
                b = first_block[phase] + n
                pe.wait_ge(w_here[b % RING], here[b])
                return ring[:, b % RING]

            def block_products(phase, n, arrived, places):
                b = first_block[phase] + n
                split = phase in SPLIT_LO
                w = ring[:, b % RING]
                if split:
                    high, low = w_high[:, split_place[b] % 2], rounded(w)
                else:
                    pe.wait_ge(w_here[b % RING], here[b])
                waited = 0
                for k, out, columns, x, start, stop in places:
                    if split and k // 4 == waited:
                        engine, count = split_low[b]
                        pe.wait_ge(w_low_vector if engine == "vector" else w_low_gpsimd, 2 * count - 1 + waited)
                        waited += 1
                    if arrived and columns.start == 0:
                        arrived(k)
                    if split:
                        x_high, x_low = x
                        nc.tensor.matmul(out, high[:, k, columns], x_high, start=start, stop=False,
                                         skip_group_check=True)
                        nc.tensor.matmul(out, high[:, k, columns], x_low, start=False, stop=False,
                                         skip_group_check=True)
                        last = nc.tensor.matmul(out, low[:, k, columns], x_high, start=False, stop=stop,
                                                skip_group_check=True)
                    else:
                        last = nc.tensor.matmul(out, w[:, k, columns], x, start=start, stop=stop,
                                                skip_group_check=True)
                last.then_inc(blocks_done, 1)

            def at_tile(x, k):
                return (rounded(x[0][:, k]), rounded(x[1][:, k])) if len(x) == 2 else x[0][:, k]

            def project(phase, n, x, arrived=None, unit=None):
                ps = pair(start_unit(phase, n if unit is None else unit))
                block_products(phase, n, arrived,
                               [(k, ps[:, i], slice(P * i, P * i + P), at_tile(x, k), k == 0, k == KB - 1)
                                for i in range(2) for k in range(KB)])

            def project_tokens(phase, n, lhs):
                ps = pair(start_unit(phase, n))
                w = start_block(phase, n)
                for i in range(TT):
                    for k in range(KB):
                        last = nc.tensor.matmul(ps[:, i], lhs[:, k, P * i:P * i + P], w[:, k],
                                                start=(k == 0), stop=(k == KB - 1))
                last.then_inc(blocks_done, 1)

            def project_deep(phase, n, kblocks, x, arrived=None):
                ps = pair(start_unit(phase, n))
                for kb in range(kblocks):
                    block_products(phase, n * kblocks + kb,
                                   (lambda k: arrived(kb * KB + k)) if n == 0 and arrived else None,
                                   [(k, ps[:, i], slice(P * i, P * i + P), at_tile(x, kb * KB + k),
                                     kb == 0 and k == 0 and i == 0, kb == kblocks - 1 and k == KB - 1)
                                    for k in range(KB) for i in range(2)])

            def split_arrived(name, tiles=1):
                def arrived(k):
                    if k % tiles == 0:
                        pe.wait_ge(a_low, SET_BASE[name] + k // tiles + 1)
                return arrived

            def modulation(g):
                def over_partitions(pieces):
                    for n in pieces:
                        for m in (2 * n, 2 * n + 1):
                            last = nc.tensor.matmul(MISC[0][:, m:m + 1], ada_sum[:, g % 2, n, P * (m % 2):P * (m % 2) + P],
                                                    ones[:, 0:1], start=True, stop=True)
                    return last

                def from_weights(n):
                    pe.wait_ge(ada0_here[n], 16)
                    w = more[:, 2048 * (n - 4):2048 * (n - 4) + 2048].rearrange("p (k n) -> p k n", k=KB)
                    for m in (2 * n, 2 * n + 1):
                        for k in range(KB):
                            nc.tensor.matmul(MISC[0][:, m:m + 1], w[:, k, P * (m % 2):P * (m % 2) + P],
                                             c_act[:, k:k + 1], start=(k == 0), stop=(k == KB - 1))

                if g == 0:
                    pe.wait_ge(c_ready, 1)
                    from_weights(7)
                    pe.wait_ge(ada0_sums, 2)
                    over_partitions(range(4))
                    from_weights(6)
                    pe.wait_ge(ada0_sums, 4)
                    last = over_partitions((4, 5))
                else:
                    pe.wait_ge(ada_sums, PIECES * g)
                    pe.wait_ge(mods_ready, g)
                    last = over_partitions(range(PIECES))
                last.then_inc(ada_psum, 1)

            def norm_stats(i):
                if i > 0:
                    pe.wait_ge(rstd_ready, i)
                for k in range(DT):
                    if k % 2 == 0:
                        pe.wait_ge(sq_ready, 4 * i + k // 2 + 1)
                    last = nc.tensor.matmul(STAT[:, 0:T], ones, squares(i)[:, k], start=(k == 0), stop=(k == DT - 1))
                last.then_inc(stat_ready, 1)

            pe.wait_ge(const_here, 16)
            pe.wait_ge(stack_here, 16 * N_STACK_LOADS)
            for s in range(len(STACKS)):
                rows = sum(n for _, n in STACKS[s])
                last = nc.tensor.transpose(MISC[1][:, s * P:s * P + rows], stack[0:rows, s, :], ident[0:rows, 0:rows])
            last.then_inc(cols_psum, 1)
            pe.wait_ge(x_here, 16)
            for k in range(DT):
                for t in range(TT):
                    last = nc.tensor.transpose(PS[k // 2][:, (k % 2) * T + t * P:(k % 2) * T + t * P + P],
                                               mixT[:, :, :].rearrange("p (t a) n -> p t (a n)", t=TT)
                                               [:, t, k * P:k * P + P], ident)
                if k % 2:
                    last.then_inc(x_psum, 1)
            norm_stats(0)
            modulation(0)

            def h_arrived(i):
                return lambda k: pe.wait_ge(h_ready, 8 * i + k + 1)

            pe.wait_ge(x_ready, 4)
            pe.wait_ge(tables_here, 32)
            for n in range(8):
                project("w_in", n, (hT,), h_arrived(0) if n == 0 else None)
            for n in range(8, 10):
                project_tokens("w_in", n, hT)
            for n in range(10, 12):
                project("w_in", n, (hT,))

            pe.wait_ge(mods_ready, 1)
            pe.wait_ge(rstd_ready, 1)
            pe.wait_ge(v_ready, 2)

            def scores(h):
                pe.wait_ge(qk_ready, 3 + h // 2)
                if h >= 2:
                    pe.wait_ge(score_ready, h - 1)
                for j in range(TT):
                    last = nc.tensor.matmul(MISC[h % 2][:, T * j:T * j + T], qk[:, 4 + h, P * j:P * j + P], qk[:, h],
                                            start=True, stop=True)
                last.then_inc(score_psum, 1)

            def values(h):
                pe.wait_ge(score_ready, h + 1)
                if h >= 1:
                    pe.wait_ge(ret_copied, h)
                for j in range(TT):
                    last = nc.tensor.matmul(MISC[2][:, 0:T], vnat[:, j, P * h:P * h + P], score[:, h % 2, j],
                                            start=(j == 0), stop=(j == TT - 1))
                last.then_inc(ret_psum, 1)

            def head_stats(h):
                pe.wait_ge(ret_copied, h + 1)
                if h >= 1:
                    pe.wait_ge(ret_rstd, h)
                nc.tensor.matmul(STAT[:, 0:T], ones, ret_sq[:, h % 2], start=True, stop=True).then_inc(ret_stat, 1)

            scores(0)
            for h in range(HEADS):
                if h + 1 < HEADS:
                    scores(h + 1)
                values(h)
                head_stats(h)

            pe.wait_ge(ret_rstd, HEADS)
            pe.wait_ge(conv_ready, 1)
            for k in range(MT):
                last = nc.tensor.matmul(STAT[:, 0:T], ones, conv[:, k], start=(k == 0), stop=(k == MT - 1))
            last.then_inc(ln_psum, 1)
            pe.wait_ge(cen_sq, 1)
            for k in range(MT):
                last = nc.tensor.matmul(STAT[:, 0:T], ones, sq[:, k], start=(k == 0), stop=(k == MT - 1))
            last.then_inc(ln_psum, 1)
            modulation(1)

            def mix_arrived(k):
                if k < MT:
                    pe.wait_ge(conv_mix, k + 1)
                else:
                    pe.wait_ge(ret_ready, k - MT + 1)

            for n in range(4):
                project("w_out", n, (mixT,), mix_arrived if n == 0 else None)
            norm_stats(1)
            modulation(2)
            def s5_rows_turned(first, part, count):
                for b in range(2):
                    if part:
                        pe.wait_ge(c_copied, b + 1)
                    for t in range(4):
                        last = nc.tensor.transpose(MISC[1 + b][:, P * t:P * t + P], c_rows[:, part, 4 * b + t], ident)
                    last.then_inc(crow_psum, 1)

            def s5_tile(m):
                pe.wait_ge(we_ready, m + 1)
                pe.wait_ge(mods_ready, (3, 3, 4, 4, 4, 4, 5, 5)[m])
                def turned(banks):
                    for b in banks:
                        if 4 * m + b >= 2:
                            pe.wait_ge(we_copied, 4 * m + b - 1)
                        for i in range(4):
                            last = nc.tensor.transpose(MISC[b % 2][:, P * i:P * i + P],
                                                       we_src[:, i % 2, 2 * b + i // 2], ident)
                        last.then_inc(we_psum, 1)

                turned((0, 1))
                pe.wait_ge(ca_ready, m + 1)
                if m > 0:
                    pe.wait_ge(kext_ready, m)
                edge = (L - 1) * GC
                for a in range(2):
                    for q in range(4):
                        g, gl = 8 * m + 4 * a + q, 4 * a + q
                        past = MISC[2][32 * q:32 * q + 32, P * a:P * a + P]
                        ahead = STAT[32 * q:32 * q + 32, P * a:P * a + edge]
                        for lo, dst, cols_in in ((64, ahead, slice(GC, P)), (0, past[:, GC:P], slice(0, edge))):
                            for ri in range(2):
                                b2 = b_bar[lo:lo + 64, ri, g:g + 2].rearrange("p g c -> p (g c)")
                                nc.tensor.matmul(dst, b2, ca_src[lo:lo + 64, ri, gl, cols_in],
                                                 start=(ri == 0), stop=(ri == 1))
                        for ri in range(2):
                            b2 = b_bar[:, ri, g:g + 2].rearrange("p g c -> p (g c)")
                            last = nc.tensor.matmul(past[:, 0:GC], b2, s5_c[:, ri, g], start=(ri == 0),
                                                    stop=(ri == 1))
                last.then_inc(kext_psum, 1)
                turned((2, 3))

            for n in range(16):
                project("fc1_0", n, (hT,), h_arrived(1) if n == 0 else None)
                if n == 0:
                    pe.wait_ge(lam_here, 64)
                    for ri in range(2):
                        last = nc.tensor.transpose(MISC[0][:, 64 * ri:64 * ri + 64], lam_rows[:, ri],
                                                   ident[0:64, 0:64])
                    last.then_inc(lam_psum, 1)
                    pe.wait_ge(crow_here, 64)
                    s5_rows_turned(0, 0, 2)
                if n == 1:
                    s5_rows_turned(0, 1, 2)
                if n in S5_AT_FC1[1:]:
                    s5_tile(S5_AT_FC1.index(n) - 1)
                if n in MODULATION_AT_FC1:
                    m = MODULATION_AT_FC1.index(n)
                    if n > S5_AT_FC1[1]:
                        pe.wait_ge(we_copied, 4 * sum(n >= a for a in S5_AT_FC1[1:]))
                    modulation(3 + m)
            s5_tile(4)
            for n in range(4):
                project_deep("fc2_0", n, 4, (hid,), lambda k: pe.wait_ge(hid_ready, k // 2 + 1) if k % 2 == 0 else None)
                if n < 3:
                    s5_tile(5 + n)
                if n in (0, 2):
                    pe.wait_ge(we_copied, 4 * (6 + n))
                    modulation(4 + n // 2)

            norm_stats(2)
            for kh in range(2):
                for jq in range(2):
                    for i in range(4):
                        k = 4 * kh + i
                        if jq == 0:
                            pe.wait_ge(h_ready, 8 * 2 + k + 1)
                        last = nc.tensor.transpose(PS[2 * kh + jq][:, P * i:P * i + P],
                                                   h_perm[:, k, P * jq:P * jq + P], ident)
                    last.then_inc(s5_rows, 1)
            for b in range(4):
                if b % 2 == 0:
                    pe.wait_ge(rows_act, b // 2 + 1)
                    pe.wait_ge(rows_dve, b // 2 + 1)
                for i in range(16):
                    last = nc.tensor.transpose(PS[b][:, NCH * i:NCH * i + NCH],
                                               h_rows[:, 16 * b + i].rearrange("s j c -> s (j c)"),
                                               ident[0:NCH, 0:NCH])
                last.then_inc(u_psum, 1)
            for n in range(8):
                if n % 2 == 0:
                    pe.wait_ge(s5_u, n // 2 + 1)
                if n < 4:
                    pe.wait_ge(s5_u, 4)
                ps = start_unit("s5_in", n)
                w = start_block("s5_in", n).rearrange("p a b -> p (a b)").rearrange("p (g r x) -> p g r x", g=8, r=2)
                for ri in range(2):
                    for g in range(8):
                        last = nc.tensor.matmul(ps[:, 256 * ri + NCH * g:256 * ri + NCH * g + NCH], w[:, g, ri],
                                                u_in[:, 8 * n + g], start=True, stop=True)
                last.then_inc(blocks_done, 1)
            for n in range(4):
                ps = start_unit("s5_out", n)
                far0 = start_block("s5_out", 3 * n)
                near = start_block("s5_out", 3 * n + 1).rearrange("p a b -> p (a b)").rearrange("p (g x) -> p g x", g=16)
                for a in range(4):
                    if a == 0:
                        pe.wait_ge(state_ready, n + 1)
                    if a % 2 == 0:
                        far = (far0 if a == 0 else start_block("s5_out", 3 * n + 2)).rearrange("p a b -> p (a b)")\
                            .rearrange("p (r g x) -> p r g x", r=2, g=8)
                    for part in range(3):
                        for q in range(4):
                            g = 4 * a + q
                            if part == 0:
                                lhs, rhs = u_in[:, 16 * n + g], near[:, g]
                            else:
                                lhs, rhs = state[:, part - 1, 16 * n + g], far[:, part - 1, g % 8]
                            last = nc.tensor.matmul(ps[32 * q:32 * q + 32, P * a:P * a + P], lhs, rhs,
                                                    start=(part == 0), stop=(part == 2))
                    if a == 1:
                        last.then_inc(blocks_done, 1)
                last.then_inc(blocks_done, 2)
            for n in range(4):
                pe.wait_ge(s5_z, n + 1)
                if n >= 2:
                    pe.wait_ge(z_ready, n - 1)
                for i in range(2):
                    for j in range(L):
                        last = nc.tensor.transpose(MISC[n % 2][:, 256 * i + NCH * j:256 * i + NCH * j + NCH],
                                                   z_rows[:, j, P * (2 * n + i):P * (2 * n + i) + P],
                                                   ident[0:NCH, 0:NCH])
                last.then_inc(z_psum, 1)
            for n in range(8):
                project("glu", n, (sq, mixT), split_arrived("glu", 2) if n == 0 else None)
            norm_stats(3)
            for n in range(16):
                project("fc1_1", n, (sq, hT), split_arrived("fc1_1") if n == 0 else None)
            for n in range(4):
                project_deep("fc2_1", n, 4, (hid_high, hid), split_arrived("fc2_1", 2))

            def turn_p():
                pe.wait_ge(p_here, 16)
                for n in range(2):
                    pe.wait_ge(angle_ready, 1)
                    for i in range(4):
                        tile, t = 2 * n + i // 2, i % 2
                        last = nc.tensor.transpose(MISC[n][:, P * i:P * i + P],
                                                   p_rows[:, 2 * n + t, P * (tile % 2):P * (tile % 2) + P], ident)
                    last.then_inc(p_psum, 1)

            norm_stats(4)
            turn_p()
            norm_stats(5)

            def turn_x(n):
                pe.wait_ge(xbc_ready, 4 + n + 1)
                if n >= 2:
                    pe.wait_ge(xdt_ready, n - 1)
                for i in range(4):
                    last = nc.tensor.transpose((STAT, MISC[2])[n % 2][:, P * i:P * i + P],
                                               xs[:, 2 * n + i // 2, P * (i % 2):P * (i % 2) + P], ident)
                last.then_inc(xt_psum, 1)

            def spread(t):
                if t >= 2:
                    pe.wait_ge(seg_ready, t - 1)
                for h in range(2):
                    one_hot = ident[0:SSM_HEADS, 2 * t + h:2 * t + h + 1].to_broadcast([SSM_HEADS, P])
                    last = nc.tensor.matmul(MISC[t % 2][:, T * h:T * h + T], one_hot, a_cum_rows[0:SSM_HEADS, :],
                                            start=True, stop=True)
                last.then_inc(seg_psum, 1)

            def contract(t):
                pe.wait_ge(seg_weighed, t + 1)
                if t >= 2:
                    pe.wait_ge(y_skipped, t - 1)
                ps = (STAT, MISC[2])[t % 2]
                for h in range(2):
                    x = slice(SSM_DIM * (2 * t + h), SSM_DIM * (2 * t + h + 1))
                    rows = slice(SSM_DIM * h, SSM_DIM * h + SSM_DIM)
                    nc.tensor.matmul(ps[rows, 0:T], xdt[:, 0, x], seg[:, t % 2, h, 0:T], start=True, stop=False,
                                     skip_group_check=True)
                    last = nc.tensor.matmul(ps[rows, P:T], xdt[:, 1, x], seg[:, t % 2, h, T:SEG], start=False,
                                            stop=True, skip_group_check=True)
                last.then_inc(y_psum, 1)

            def group_stats(g):
                pe.wait_ge(group_sq, g + 1)
                ps = start_unit("z", Z_UNITS.index(("group", g)))
                for k in range(4):
                    last = nc.tensor.matmul(ps[:, 0:T], ones, group_squares[:, 4 * (g % 2) + k], start=(k == 0),
                                            stop=(k == 3))
                last.then_inc(group_stat, 1)

            for m in range(XBC_UNITS):
                project("xbc", m, (sq, hT), split_arrived("xbc") if m == 0 else None)
                if m == 0:
                    pe.wait_ge(small_here, 16 * 6)
                    pe.wait_ge(p_ready, 2)
                    pe.wait_ge(dt_w_low, 1)
                    for i in range(TT):
                        for k in range(KB):
                            for n, (x, w) in enumerate(((sq, dt_w_high), (hT, dt_w_high), (sq, dt_w))):
                                last = nc.tensor.matmul(MISC[0][:, SSM_HEADS * i:SSM_HEADS * i + SSM_HEADS],
                                                        rounded(x[:, k, P * i:P * i + P]), rounded(w[:, k]),
                                                        start=(k == 0 and n == 0), stop=(k == KB - 1 and n == 2))
                    last.then_inc(dt_psum, 1)
                if m == 2:
                    pe.wait_ge(dta_ready, 1)
                    tri, less = table("tri")[:, 0:P], table("tri_less_one")
                    for i, w in enumerate((less, tri)):
                        nc.tensor.matmul(MISC[1][:, SSM_HEADS * i:SSM_HEADS * i + SSM_HEADS], w, dta[:, i], start=True,
                                         stop=True)
                    for i, w in enumerate((less, tri)):
                        last = nc.tensor.matmul(MISC[2][0:SSM_HEADS, P * i:P * i + P], dta[:, i], w, start=True,
                                                stop=True)
                    last.then_inc(a_cum_psum, 1)
                if m in (6, 7):
                    pe.wait_ge(xbc_ready, 4)
                    pe.wait_ge(a_cum_ready, 1)
                    for g in (2 * (m - 6), 2 * (m - 6) + 1):
                        if g >= 2:
                            pe.wait_ge(cb_ready, g - 1)
                        b, c = bc_tiles[:, g], bc_tiles[:, SSM_GROUPS + g]
                        nc.tensor.matmul(MISC[g % 2][:, 0:T], b[:, 0:P], c, start=True, stop=True)
                        nc.tensor.matmul(MISC[g % 2][:, T:SEG], b[:, P:T], c[:, P:T], start=True, stop=True)\
                            .then_inc(cb_psum, 1)
                if m >= 6:
                    turn_x(m - 6)
            pe.wait_ge(cb_ready, SSM_GROUPS)
            spread(0)
            spread(1)
            for n in range(8):
                project("z", n, (sq, hT), unit=Z_UNITS.index(("z", n)))
                if n == 0:
                    turn_x(6)
                    turn_x(7)
                    pe.wait_ge(xdt_ready, 8)
                for t in (2 * n, 2 * n + 1):
                    contract(t)
                    if t + 2 < Z_TILES:
                        spread(t + 2)
                if n in (4, 6):
                    group_stats((n - 4) // 2)
            group_stats(2)
            group_stats(3)
            for n in range(4):
                project_deep("ssm_out", n, 2, (y_high, xs), split_arrived("ssm_out"))

            def embedding(layer, norm):
                w = start_block(f"ple_proj_{layer}", 0).rearrange("p a b -> p (a b)").rearrange(
                    "p (k n) -> p k n", k=PLE // P)
                pe.wait_ge(p_ready, 2)
                for n in range(4):
                    ps = pair(start_unit(f"ple_proj_{layer}", n))
                    for i in range(2):
                        for k in range(PLE // P):
                            last = nc.tensor.matmul(ps[:, i], w[:, k, P * (2 * n + i):P * (2 * n + i) + P],
                                                    p_tiles[:, 2 * layer + k], start=(k == 0), stop=(k == PLE // P - 1))
                last.then_inc(blocks_done, 1)
                norm_stats(norm)
                for n in range(4):
                    project(f"ple_gate_{layer}", n, (sq, hT),
                            split_arrived(f"ple_gate_{layer}") if n == 0 else None)

            embedding(0, 6)

            norm_stats(7)

            def head_stats(m):
                pe.wait_ge(qk2_copied, m + 1)
                if m >= 2:
                    pe.wait_ge(qk2_rstd, m - 1)
                for i in range(2):
                    last = nc.tensor.matmul((MISC[2], STAT)[m % 2][:, T * i:T * i + T], table("halves"), head_sq2[:, 2 * (m % 2) + i],
                                            start=True, stop=True)
                last.then_inc(qk2_stat, 1)

            def scores(t):
                if t == 0:
                    pe.wait_ge(k_both_ready, 1)
                else:
                    pe.wait_ge(s_masked, t)
                pe.wait_ge(qk2_ready, 2 + t // 2)
                for h in range(2):
                    lo = 64 * h
                    q, k = qk2[lo:lo + 64, 2 + t], k_both[lo:lo + 64, t // 2]
                    nc.tensor.matmul(MISC[h][:, 0:P], q[:, 0:P], k[:, 0:P], start=True, stop=True)
                    last = nc.tensor.matmul(MISC[h][:, P:SEG], q[:, P:T], k, start=True, stop=True)
                last.then_inc(s_psum, 1)

            def turn_probs(t):
                pe.wait_ge(probs_ready, t + 1)
                if t == 0:
                    pe.wait_ge(qk2_rstd, 5)
                for h in range(2):
                    if t >= 1:
                        pe.wait_ge(pt_ready, 2 * t - 1 + h)
                    for i in range(3):
                        last = nc.tensor.transpose((MISC[2], STAT)[h][:, P * i:P * i + P],
                                                   probs[:, t % 2, h, P * i:P * i + P], ident)
                    last.then_inc(pt_psum, 1)

            def attend(t):
                ps = start_unit("gate", ATT_UNITS.index(("out", t)))
                for h in range(2):
                    pe.wait_ge(pt_ready, 2 * t + h + 1)
                    rows, v = slice(64 * h, 64 * h + 64), slice(64 * (t // 2), 64 * (t // 2) + 64)
                    p = probs_t[:, t % 2, h]
                    nc.tensor.matmul(ps[rows, 0:P], v2[:, 0, v], p[:, 0:P], start=True, stop=True)
                    nc.tensor.matmul(ps[rows, P:T], v2[:, 0, v], p[:, P:T], start=True, stop=False)
                    last = nc.tensor.matmul(ps[rows, P:T], v2[:, 1, v], p[:, T:SEG], start=False, stop=True)
                last.then_inc(o_psum, 1)

            project("kv", 0, (mixT,), lambda k: pe.wait_ge(hn_ready, 48 + k + 1))
            project_tokens("kv", 1, mixT)
            head_stats(0)
            for n in range(4):
                project("q", n, (sq, hT), split_arrived("q") if n == 0 else None)
                head_stats(n + 1)
                if n == 2:
                    scores(0)
            def gate(n):
                project("gate", n, (sq, hT), unit=ATT_UNITS.index(("gate", n)))

            scores(1)
            gate(0)
            for t in range(ATT_TILES):
                if t in (1, 3, 5):
                    gate((t + 1) // 2)
                turn_probs(t)
                if t + 2 < ATT_TILES:
                    scores(t + 2)
                if t >= 1:
                    attend(t - 1)
            attend(ATT_TILES - 1)
            for n in range(4):
                project("attn_out", n, (att_high, mixT), split_arrived("attn_out") if n == 0 else None)
            embedding(1, 8)
            for n in range(4):
                ps = pair(start_unit("final", n))
                pe.wait_ge(x_ready, 4 * 9 + n + 1)
                for t in range(TT):
                    for i in range(2):
                        last = nc.tensor.transpose(ps[:, t, P * i:P * i + P], xT[:, 2 * n + i, P * t:P * t + P], ident)
                last.then_inc(x_psum, 1)

        @block.vector
        def _(dve):
            steps = [0]

            def step(ins):
                steps[0] += 1
                ins.then_inc(dve_step, 1)

            def link(ins):
                step(ins)
                dve.wait_ge(dve_step, steps[0])

            def behind(n):
                dve.wait_ge(dve_step, steps[0] - n)

            split_next = [0]

            def lower_to(end):
                while split_next[0] < len(split_order) and split_order[split_next[0]] < end:
                    c = split_next[0]
                    b = split_order[c]
                    for half in range(2) if split_low[b][0] == "vector" else ():
                        dve.wait_ge(w_high_ready, 2 * c + half + 1)
                        ks = slice(4 * half, 4 * half + 4)
                        w = ring[:, b % RING, ks]
                        nc.vector.tensor_tensor(rounded(w), w, w_high[:, c % 2, ks], ALU.subtract)\
                            .then_inc(w_low_vector, 1)
                    split_next[0] += 1

            def lower_tiles(name, n, full, high):
                dve.wait_ge(a_high, SET_BASE[name] + n + 1)
                nc.vector.tensor_tensor(rounded(full), full, rounded(high), ALU.subtract).then_inc(a_low, 1)

            def unit(phase, n):
                u = first_unit[phase] + n
                lower_to(ready[u] + 1)
                dve.wait_ge(blocks_done, ready[u])
                return pair(PS[u % BANKS])

            dve.wait_ge(const_here, 16)
            dve.wait_ge(cols_psum, 1)
            for s in range(len(STACKS)):
                rows = sum(n for _, n in STACKS[s])
                last = nc.vector.tensor_copy(cols[:, s, 0:rows], MISC[1][:, s * P:s * P + rows])
            last.then_inc(cols_ready, 1)
            dve.wait_ge(cols_ready, 1)
            for p in range(4):
                dve.wait_ge(x_psum, p + 1)
                nc.vector.tensor_copy(xT[:, 2 * p:2 * p + 2], pair(PS[p])).then_inc(x_ready, 1)

            dve.wait_ge(c_ready, 1)
            for pieces in ((0, 1), (2, 3), (4,), (5,)):
                for k in range(KB):
                    for n in pieces:
                        w = (big, more)[n // 4][:, 2048 * (n % 4) + NB * k:2048 * (n % 4) + NB * k + NB]
                        if k == 0:
                            dve.wait_ge(ada0_here[n], 16)
                            step(nc.vector.tensor_scalar(ada_sum[:, 0, n], w, c_act[:, k:k + 1], None, ALU.mult))
                            continue
                        behind(len(pieces) - 1)
                        ins = nc.vector.scalar_tensor_tensor(out=ada_sum[:, 0, n], in0=w, scalar=c_act[:, k:k + 1],
                                                             in1=ada_sum[:, 0, n], op0=ALU.mult, op1=ALU.add)
                        if k == KB - 1 and n == pieces[-1]:
                            ins.then_inc(ada0_sums, 1)
                        else:
                            step(ins)

            def modulation(g):
                dve.wait_ge(ada_psum, g + 1)
                n = 2 * PIECES
                nc.vector.tensor_tensor(mods[:, g * n:g * n + n], MISC[0][:, 0:n], col("ada_b")[:, g * n:g * n + n],
                                        ALU.add).then_inc(mods_ready, 1)

            def gain(i):
                layer, which = i // 2, (SCALE_M, SCALE_F)[i % 2]
                dve.wait_ge(mods_ready, 3 * layer + (1, 3)[i % 2])
                link(nc.vector.scalar_tensor_tensor(out=gains[:, i], in0=mod(layer, which), scalar=1.0,
                                                    in1=col("norm_g")[:, 8 * i:8 * i + 8], op0=ALU.add, op1=ALU.mult))

            def normed(i, gain_col):
                dve.wait_ge(rstd_ready, i + 1)
                for k in range(DT):
                    nc.vector.scalar_tensor_tensor(out=hT[:, k], in0=xT[:, k], scalar=gain_col(k), in1=rstd[:, :],
                                                   op0=ALU.mult, op1=ALU.mult).then_inc(hn_ready, 1)

            def residual(phase, gate, first=0, last=4):
                for n in range(first, last):
                    ps = unit(phase, n)
                    for i in range(2):
                        k = 2 * n + i
                        ins = nc.vector.scalar_tensor_tensor(out=xT[:, k], in0=ps[:, i], scalar=gate(k), in1=xT[:, k],
                                                             op0=ALU.mult, op1=ALU.add)
                    ins.then_inc(x_ready, 1)

            modulation(0)
            gain(0)
            normed(0, lambda k: gains[:, 0, k:k + 1])

            nc.vector.memset(apad[:, :, 0:PAD], 0.0)
            nc.vector.memset(apad[:, :, PAD + T:], 0.0)
            for j in range(2):
                dve.wait_ge(sg_ready, j + 1)
                ps = unit("w_in", 2 * j + 1)
                nc.vector.tensor_tensor(apad[:, 2 * j:2 * j + 2, PAD:PAD + T], ps, sgate, ALU.mult).then_inc(a_ready, 1)
            dve.wait_ge(a_ready, 2)

            def taps(first, last):
                for tap in range(first, last):
                    for k in range(MT):
                        w = col("conv_w", 4 * tap + k)
                        if tap == 0:
                            step(nc.vector.tensor_scalar(conv[:, k], apad[:, k, 0:T], w, col("conv_b", k),
                                                         ALU.mult, ALU.add))
                            continue
                        behind(MT - 1)
                        ins = nc.vector.scalar_tensor_tensor(out=conv[:, k], in0=apad[:, k, tap:tap + T], scalar=w,
                                                             in1=conv[:, k], op0=ALU.mult, op1=ALU.add)
                        if tap == TAPS - 1 and k == MT - 1:
                            ins.then_inc(conv_ready, 1)
                        else:
                            step(ins)

            dve.wait_ge(tables_here, 32)

            def rotate(j):
                dve.wait_ge(qk_copied, j + 1)
                a, b = qk[:, 2 * j:2 * j + 2], qk_swap[:, 2 * j:2 * j + 2]
                nc.vector.tensor_tensor(a, a, table("rope_cos").unsqueeze(1).to_broadcast([P, 2, T]), ALU.mult)
                link(nc.vector.tensor_tensor(b, b, table("rope_sin").unsqueeze(1).to_broadcast([P, 2, T]), ALU.mult))
                nc.vector.tensor_tensor(a, a, b, ALU.add).then_inc(qk_ready, 1)

            taps(0, 14)
            for j in range(4):
                rotate(j)
            taps(14, TAPS)

            def decayed(h):
                dve.wait_ge(score_psum, h + 1)
                if h >= 2:
                    dve.wait_ge(ret_psum, h - 1)
                for j in range(TT):
                    ins = nc.vector.scalar_tensor_tensor(out=score[:, h % 2, j], in0=MISC[h % 2][:, T * j:T * j + T],
                                                         scalar=float(P) ** -0.5,
                                                         in1=decay[:, h, P * (1 - j):P * (1 - j) + T],
                                                         op0=ALU.mult, op1=ALU.mult)
                ins.then_inc(score_ready, 1)

            def gated(h):
                dve.wait_ge(ret_rstd, h + 1)
                dve.wait_ge(g_ready, 2)
                link(nc.vector.tensor_tensor(ret[:, h], ret[:, h], head_rstd[:, h % 2], ALU.mult))
                nc.vector.tensor_tensor(mixT[:, MT + h], ret[:, h], gsilu[:, h], ALU.mult).then_inc(ret_ready, 1)

            for h in range(HEADS):
                decayed(h)
                if h >= 1:
                    gated(h - 1)
            gated(HEADS - 1)

            dve.wait_ge(conv_ready, 1)
            dve.wait_ge(ln_psum, 1)
            link(nc.vector.tensor_scalar(mean[:, 0], STAT[:, 0:T], 1.0 / MIX, None, ALU.mult))
            nc.vector.tensor_tensor(conv, conv, mean.to_broadcast([P, MT, T]), ALU.subtract).then_inc(centred, 1)
            dve.wait_ge(ln_rstd, 1)
            for k in range(MT):
                nc.vector.scalar_tensor_tensor(out=conv[:, k], in0=conv[:, k], scalar=col("cln_g", k), in1=rstd[:, :],
                                               op0=ALU.mult, op1=ALU.mult).then_inc(ln_scaled, 1)
            modulation(1)
            dve.wait_ge(mods_ready, 2)
            residual("w_out", lambda k: mod(0, GATE_M, k))
            modulation(2)
            gain(1)
            normed(1, lambda k: gains[:, 1, k:k + 1])

            def square_unit(base, n):
                dve.wait_ge(hid_relu, base + n + 1)
                a = hid[:, 2 * n:2 * n + 2]
                nc.vector.tensor_tensor(a, a, a, ALU.mult).then_inc(hid_ready, 1)

            def reduce_angle(dst, src, k):
                link(nc.vector.tensor_scalar(k, src, 0.5 / np.pi, SINGLE, ALU.mult, ALU.add))
                link(nc.vector.tensor_scalar(k, k, SINGLE, None, ALU.subtract))
                for n, part in enumerate(TWO_PI):
                    link(nc.vector.scalar_tensor_tensor(out=dst, in0=k, scalar=-part, in1=src if n == 0 else dst,
                                                        op0=ALU.mult, op1=ALU.add))
                return nc.vector.tensor_scalar(dst, dst, PI, -PI, ALU.min, ALU.max)

            def product(out_re, out_im, a, b, tmp, c=None):
                tt = nc.vector.tensor_tensor
                tt(out_re, a[0], b[0], ALU.mult)
                link(tt(tmp, a[1], b[1], ALU.mult))
                link(tt(out_re, out_re, tmp, ALU.subtract))
                tt(out_im, a[0], b[1], ALU.mult)
                link(tt(tmp, a[1], b[0], ALU.mult))
                return tt(out_im, out_im, tmp, ALU.add)

            def s5_steps():
                dve.wait_ge(lam_psum, 1)
                nc.vector.tensor_scalar(s5_lr, MISC[0][:, 0:64], -1e-4, None, ALU.min)
                dve.wait_ge(s5_fun, 1)
                link(nc.vector.tensor_copy(s5_li, MISC[0][:, 64:128]))
                nc.vector.tensor_tensor(s5_th, s5_li, s5_dt, ALU.mult)
                nc.vector.tensor_tensor(s5_a, s5_lr, s5_dt, ALU.mult).then_inc(s5_args, 1)
                dve.wait_ge(s5_args, 1)
                reduce_angle(s5_r, s5_th, s5_k).then_inc(s5_args, 1)

            def s5_discretize():
                tt, ts, stt = nc.vector.tensor_tensor, nc.vector.tensor_scalar, nc.vector.scalar_tensor_tensor
                dve.wait_ge(s5_fun, 3)
                link(tt(s5_cos, s5_cos, s5_cos, ALU.mult))
                link(ts(s5_cos, s5_cos, -2.0, 1.0, ALU.mult, ALU.add))
                tt(s5_abi, s5_mag, s5_sin, ALU.mult)
                link(tt(s5_abr, s5_mag, s5_cos, ALU.mult))
                ts(s5_nr, s5_abr, -1.0, None, ALU.add)
                tt(s5_den, s5_lr, s5_lr, ALU.mult)
                link(tt(s5_t1, s5_li, s5_li, ALU.mult))
                link(tt(s5_den, s5_den, s5_t1, ALU.add))
                nc.vector.reciprocal(s5_rden, s5_den)
                tt(s5_fr, s5_nr, s5_lr, ALU.mult)
                link(tt(s5_t1, s5_abi, s5_li, ALU.mult))
                link(tt(s5_fr, s5_fr, s5_t1, ALU.add))
                tt(s5_fi, s5_abi, s5_lr, ALU.mult)
                link(tt(s5_t2, s5_nr, s5_li, ALU.mult))
                link(tt(s5_fi, s5_fi, s5_t2, ALU.subtract))
                tt(s5_fr, s5_fr, s5_rden, ALU.mult)
                link(tt(s5_fi, s5_fi, s5_rden, ALU.mult))
                nc.vector.memset(powers[:, 0, 0], 1.0)
                nc.vector.memset(powers[:, 1, 0], 0.0)
                nc.vector.tensor_copy(powers[:, 0, 1], s5_abr)
                link(nc.vector.tensor_copy(powers[:, 1, 1], s5_abi))
                base = (s5_abr, s5_abi)
                for n in range(2, L + 1):
                    link(product(powers[:, 0, n], powers[:, 1, n], (powers[:, 0, n - 1], powers[:, 1, n - 1]), base,
                                 s5_t1))
                for ri in range(2):
                    nc.vector.tensor_copy(pow_in[0:64, ri], powers[0:64, ri, 0:L].rearrange("p n g -> p g n")[:, :, ::-1])
                    nc.vector.tensor_copy(pow_in[64:128, ri], powers[64:128, ri, 0:L].rearrange("p n g -> p g n"))
                    nc.vector.tensor_copy(pow_out[0:64, ri], powers[0:64, ri, 1:L + 1].rearrange("p n g -> p g n"))
                    link(nc.vector.tensor_copy(pow_out[64:128, ri],
                                               powers[64:128, ri, 1:L + 1].rearrange("p n g -> p g n")[:, :, ::-1]))
                dve.wait_ge(braw_here, 64)
                shape = [P, GROUPS, GC]
                f = tuple(x.unsqueeze(2).to_broadcast(shape) for x in (s5_fr, s5_fi))
                nc.vector.memset(b_bar[:, :, GROUPS], 0.0)
                link(product(b_bar[:, 0, 0:GROUPS], b_bar[:, 1, 0:GROUPS], f, (b_raw[:, 0], b_raw[:, 1]),
                             s5_tmp.rearrange("p (g c) -> p g c", g=GROUPS)))

            def s5_kernels(m):
                dve.wait_ge(kext_psum, m + 1)
                if m > 0:
                    dve.wait_ge(k_stored, 64 * m)
                else:
                    dve.wait_ge(dq_here, 64)
                edge = (L - 1) * GC
                nc.vector.tensor_copy(kext[:, :, 0:edge], STAT[:, 0:2 * P].rearrange("p (a x) -> p a x", a=2)[:, :, 0:edge])
                link(nc.vector.tensor_copy(kext[:, :, edge:WIN], MISC[2][:, 0:2 * P].rearrange("p (a x) -> p a x", a=2)))
                for a in range(2):
                    d = s5_dq[:, 2 * m + a:2 * m + a + 1]
                    mid = kext[:, a, edge:P]
                    ins = nc.vector.scalar_tensor_tensor(out=mid, in0=table("ident16"), scalar=d, in1=mid, op0=ALU.mult,
                                                         op1=ALU.add)
                ins.then_inc(kext_ready, 1)

            def s5_tile(m):
                if m > 0:
                    s5_kernels(m - 1)
                    dve.wait_ge(we_psum, 4 * m)
                    dve.wait_ge(ca_stored, 16 * m)
                else:
                    dve.wait_ge(crow_psum, 4)
                    dve.wait_ge(c_copied, 4)
                shape = [P, 8, L, GC]
                groups = slice(8 * m, 8 * m + 8)
                tmp = s5_tmp.rearrange("p (g j c) -> p g j c", g=8, j=L)

                def wide(x):
                    return x.rearrange("p g (j c) -> p g j c", j=L)

                p_in = [pow_in[:, ri, groups].unsqueeze(3).to_broadcast(shape) for ri in range(2)]
                b = [b_bar[:, ri, groups].unsqueeze(2).to_broadcast(shape) for ri in range(2)]
                product(wide(we_src[:, 0]), wide(we_src[:, 1]), p_in, b, tmp).then_inc(we_ready, 1)
                p_out = [pow_out[:, ri, groups].unsqueeze(3).to_broadcast(shape) for ri in range(2)]
                c, minus = [s5_c[:, ri, groups].unsqueeze(2).to_broadcast(shape) for ri in range(2)]
                tt = nc.vector.tensor_tensor
                re, im = wide(ca_src[:, 0]), wide(ca_src[:, 1])
                dve.wait_ge(we_ready, m + 1)
                tt(re, p_out[0], c, ALU.mult)
                link(tt(tmp, p_out[1], minus, ALU.mult))
                link(tt(re, re, tmp, ALU.add))
                tt(im, p_out[0], minus, ALU.mult)
                link(tt(tmp, p_out[1], c, ALU.mult))
                tt(im, im, tmp, ALU.subtract).then_inc(ca_ready, 1)

            for n in range(16):
                square_unit(0, n)
                if n == 0:
                    s5_steps()
                if n == 1:
                    s5_discretize()
                if n in S5_AT_FC1:
                    s5_tile(S5_AT_FC1.index(n))
                if n in MODULATION_AT_FC1:
                    modulation(3 + MODULATION_AT_FC1.index(n))
            s5_tile(5)
            gate_f = lambda k: mod(0, GATE_F, k)
            residual("fc2_0", gate_f, 0, 1)
            modulation(4)
            s5_tile(6)
            residual("fc2_0", gate_f, 1, 2)
            s5_tile(7)
            residual("fc2_0", gate_f, 2, 3)
            s5_kernels(7)
            modulation(5)
            gain(2)
            gain(3)
            rshape = [P, GROUPS, NCH]
            link(nc.vector.tensor_scalar(s5_t1, s5_r, float(L), None, ALU.mult))
            link(reduce_angle(s5_t2, s5_t1, s5_k))
            nc.vector.memset(shrink[:, :, 0:1], 0.0)
            link(nc.vector.tensor_tensor(rot_cos, s5_t2.unsqueeze(2).to_broadcast(rshape),
                                         table("steps").unsqueeze(1).to_broadcast(rshape), ALU.mult))
            reduce_angle(rot_cos, rot_cos, rot_k).then_inc(rot_args, 1)
            dve.wait_ge(rot_fun, 1)
            link(nc.vector.tensor_tensor(rot_cos, rot_cos, rot_cos, ALU.mult))
            link(nc.vector.tensor_scalar(rot_cos, rot_cos, -2.0, 1.0, ALU.mult, ALU.add))
            residual("fc2_0", gate_f, 3, 4)

            normed(2, lambda k: gains[:, 2, k:k + 1])
            for kh in range(2):
                dve.wait_ge(s5_rows, 2 * kh + 2)
                for j in range(4):
                    ins = nc.vector.tensor_copy(h_rows[:, 32 * kh:32 * kh + 32, 4 + j],
                                                PS[2 * kh + 1][32 * j:32 * j + 32, :].rearrange("s (g c) -> s g c", c=GC))
                ins.then_inc(rows_dve, 1)
            for b in range(4):
                dve.wait_ge(u_psum, b + 1)
                if b == 0:
                    dve.wait_ge(h_ready, 8 * 3)
                nc.vector.tensor_copy(u_in[:, 16 * b:16 * b + 16].rearrange("p g s -> p (g s)"), PS[b][:, :])\
                    .then_inc(s5_u, 1)
            tt = nc.vector.tensor_tensor
            for part in range(4):
                dve.wait_ge(s5_e, 2 * part + 2)
                gs = slice(16 * part, 16 * part + 16)

                def flat(x):
                    return x.rearrange("p g s -> p (g s)")

                def by_group(x):
                    return x.rearrange("p (g s) -> p g s", g=16)

                cos, sin, keep = flat(rot_cos[:, gs]), flat(rot_sin[:, gs]), flat(shrink[:, gs])
                e_re, e_im = flat(state[:, 0, gs]), flat(state[:, 1, gs])
                t = part_t
                tt(t[0], cos, e_re, ALU.mult)
                link(tt(t[1], sin, e_im, ALU.mult))
                tt(t[0], t[0], t[1], ALU.add)
                tt(t[2], cos, e_im, ALU.mult)
                link(tt(t[3], sin, e_re, ALU.mult))
                link(tt(t[2], t[2], t[3], ALU.subtract))
                nc.vector.tensor_tensor_scan(out=t[1], data0=keep, data1=t[0], initial=0.0, op0=ALU.mult, op1=ALU.add)
                link(nc.vector.tensor_tensor_scan(out=t[3], data0=keep, data1=t[2], initial=0.0, op0=ALU.mult,
                                                  op1=ALU.add))
                for ri in range(2):
                    nc.vector.memset(state[0:64, ri, gs, 0:1], 0.0)
                    nc.vector.memset(state[64:128, ri, gs, NCH - 1:NCH], 0.0)
                    a, b = (t[1], t[3]) if ri == 0 else (t[3], t[1])
                    tt(t[0], cos, a, ALU.mult)
                    link(tt(t[2], sin, b, ALU.mult))
                    op = ALU.subtract if ri == 0 else ALU.add
                    x, y = by_group(t[0]), by_group(t[2])
                    tt(state[0:64, ri, gs, 1:NCH], x[0:64, :, 0:NCH - 1], y[0:64, :, 0:NCH - 1], op)
                    ins = tt(state[64:128, ri, gs, 0:NCH - 1][:, :, ::-1], x[64:128, :, 0:NCH - 1],
                             y[64:128, :, 0:NCH - 1], op)
                    if ri == 0:
                        link(ins)
                ins.then_inc(state_ready, 1)
                dve.wait_ge(state_ready, part + 1)
            for n in range(4):
                dve.wait_ge(z_psum, n + 1)
                nc.vector.tensor_copy(mixT[:, 2 * n:2 * n + 2].rearrange("p k (s j) -> p k s j", j=L),
                                      MISC[n % 2][:, :].rearrange("p (k j s) -> p k s j", k=2, j=L)).then_inc(z_ready, 1)
            lower_to(first_block["glu"] + 1)
            for n in range(4):
                lower_tiles("glu", n, mixT[:, 2 * n:2 * n + 2], sq[:, 2 * n:2 * n + 2])
            for n in range(4):
                lower_to(first_block["glu"] + 2 * n + 2)
                dve.wait_ge(glu_sig, n + 1)
                ps = unit("glu", 2 * n + 1)
                if n >= 1:
                    dve.wait_ge(x_ready, 12 + n)
                tt(glu_prod, ps, glu_gate, ALU.mult).then_inc(glu_mul, 1)
                dve.wait_ge(glu_mul, n + 1)
                for i in range(2):
                    k = 2 * n + i
                    ins = nc.vector.scalar_tensor_tensor(out=xT[:, k], in0=glu_prod[:, i], scalar=mod(1, GATE_M, k),
                                                         in1=xT[:, k], op0=ALU.mult, op1=ALU.add)
                ins.then_inc(x_ready, 1)
            dve.wait_ge(rstd_ready, 4)
            for k in range(DT + 2):
                if k < DT:
                    nc.vector.scalar_tensor_tensor(out=hT[:, k], in0=xT[:, k], scalar=gains[:, 3, k:k + 1],
                                                   in1=rstd[:, :], op0=ALU.mult, op1=ALU.mult).then_inc(hn_ready, 1)
                if k >= 2:
                    j = k - 2
                    dve.wait_ge(a_high, SET_BASE["fc1_1"] + j + 1)
                    nc.vector.scalar_tensor_tensor(out=rounded(hT[:, j]), in0=hT[:, j], scalar=mod(1, SHIFT_F, j),
                                                   in1=rounded(sq[:, j]), op0=ALU.add, op1=ALU.subtract).then_inc(a_low, 1)
            for n in range(17):
                if n < 16:
                    lower_to(first_block["fc1_1"] + n + 2)
                    square_unit(16, n)
                if n >= 1:
                    lower_tiles("fc2_1", n - 1, hid[:, 2 * n - 2:2 * n], hid_high[:, 2 * n - 2:2 * n])
            residual("fc2_1", lambda k: mod(1, GATE_F, k))

            dve.wait_ge(positions_here, 16)
            link(nc.vector.tensor_copy(rope_cos, positions))
            link(nc.vector.tensor_scalar(rope_cos, rope_cos, table("inv_freq"), None, ALU.mult))
            link(reduce_angle(angle, rope_cos, angle_k))
            nc.vector.tensor_copy(angle_k, angle).then_inc(angle_ready, 1)
            dve.wait_ge(rstd_ready, 5)
            for k in range(DT):
                ins = nc.vector.scalar_tensor_tensor(out=xT[:, k], in0=xT[:, k], scalar=col("norm_f", k), in1=rstd[:, :],
                                                     op0=ALU.mult, op1=ALU.mult)
                if k % 2:
                    ins.then_inc(x_ready, 1)
            for n in range(2):
                dve.wait_ge(p_psum, n + 1)
                nc.vector.tensor_copy(p_tiles[:, 2 * n:2 * n + 2], pair(MISC[n])).then_inc(p_ready, 1)
            dve.wait_ge(angle_fun, 1)
            nc.vector.tensor_scalar(rope_sin, rope_sin, table("rot_sign"), None, ALU.mult)
            link(nc.vector.tensor_tensor(rope_cos, rope_cos, rope_cos, ALU.mult))
            link(nc.vector.tensor_scalar(rope_cos, rope_cos, -2.0, 1.0, ALU.mult, ALU.add))

            def plain_norm(i, name, dst, first=0):
                dve.wait_ge(rstd_ready, i + 1)
                for k in range(DT):
                    nc.vector.scalar_tensor_tensor(out=dst[:, k], in0=xT[:, k], scalar=col(name, first + k),
                                                   in1=rstd[:, :], op0=ALU.mult, op1=ALU.mult).then_inc(hn_ready, 1)

            def split_norm(i, name, phase, first=0, before_low=None):
                dve.wait_ge(rstd_ready, i + 1)
                for k in range(DT + 2):
                    if k < DT:
                        nc.vector.scalar_tensor_tensor(out=hT[:, k], in0=xT[:, k], scalar=col(name, first + k),
                                                       in1=rstd[:, :], op0=ALU.mult, op1=ALU.mult).then_inc(hn_ready, 1)
                    if k >= 2:
                        lower_tiles(phase, k - 2, hT[:, k - 2], sq[:, k - 2])

            nc.vector.memset(padded.rearrange("p s (k n) -> p (s k) n", k=2)[:, :, 0:3], 0.0).then_inc(pad_zero, 1)
            dve.wait_ge(dt_w_rounded, 1)
            nc.vector.tensor_tensor(rounded(dt_w), dt_w, rounded(dt_w_high), ALU.subtract).then_inc(dt_w_low, 1)
            split_norm(5, "ssm_norm_w_2", "xbc")

            def convolve(m):
                dve.wait_ge(xbc_copied, m + 1)
                if m >= 2:
                    dve.wait_ge(xbc_ready, m - 1)
                src = padded[:, m % 4].rearrange("p (k n) -> p k n", k=2)
                for tap in range(4):
                    for i in range(2):
                        tile = 16 + 2 * m + i if m < 4 else 2 * (m - 4) + i
                        w = col("ssm_conv_w_2", 24 * tap + tile)
                        dst = convolved[:, m % 2, T * i:T * i + T]
                        if tap == 0:
                            step(nc.vector.tensor_scalar(dst, src[:, i, 0:T], w, None, ALU.mult))
                            continue
                        behind(1)
                        ins = nc.vector.scalar_tensor_tensor(out=dst, in0=src[:, i, tap:tap + T], scalar=w, in1=dst,
                                                             op0=ALU.mult, op1=ALU.add)
                        if tap == 3 and i == 1:
                            ins.then_inc(xbc_conv, 1)
                        else:
                            step(ins)

            def step_sizes():
                tt, ts, stt = nc.vector.tensor_tensor, nc.vector.tensor_scalar, nc.vector.scalar_tensor_tensor
                dve.wait_ge(dt_fun, 1)
                link(ts(dt_s, dt_e, 2.0, None, ALU.add))
                link(nc.vector.reciprocal(dt_s, dt_s))
                link(tt(dt_s, dt_s, dt_e, ALU.mult))
                link(tt(dt_e, dt_s, dt_s, ALU.mult))
                link(ts(dt_p, dt_e, 1.0 / 17, 1.0 / 15, ALU.mult, ALU.add))
                for n in (13, 11, 9, 7, 5, 3, 1):
                    link(tt(dt_p, dt_p, dt_e, ALU.mult))
                    link(ts(dt_p, dt_p, 1.0 / n, None, ALU.add))
                link(tt(dt_p, dt_p, dt_s, ALU.mult))
                link(ts(dt_y, dt_y, 0.0, None, ALU.max))
                for i in range(TT):
                    link(stt(out=dt_y[:, i], in0=dt_p[:, i], scalar=2.0, in1=dt_y[:, i], op0=ALU.mult, op1=ALU.add))
                    ins = stt(out=dta[:, i], in0=dt_y[:, i], scalar=-1.0, in1=a_rows, op0=ALU.mult, op1=ALU.mult)
                ins.then_inc(dta_ready, 1)

            def weigh_by_dt(n):
                dve.wait_ge(xt_psum, n + 1)
                ps = (STAT, MISC[2])[n % 2][:, :].rearrange("p (k t h c) -> p k t h c", k=2, t=TT, h=2)
                for i in range(2):
                    tile = 2 * n + i
                    ins = nc.vector.tensor_tensor(
                        xdt[:, :, P * tile:P * tile + P].rearrange("p t (h c) -> p t h c", h=2), ps[:, i],
                        dt_y[:, :, 2 * tile:2 * tile + 2].unsqueeze(3).to_broadcast([P, TT, 2, SSM_DIM]), ALU.mult)
                ins.then_inc(xdt_ready, 1)

            def segments(t):
                dve.wait_ge(seg_psum, t + 1)
                if t >= 2:
                    dve.wait_ge(y_psum, t - 1)
                for h in range(2):
                    rows = MISC[t % 2][:, T * h:T * h + T]
                    for i, (dst, src) in enumerate(((slice(0, T), slice(0, T)), (slice(T, SEG), slice(P, T)))):
                        ins = nc.vector.tensor_scalar(seg[:, t % 2, h, dst], rows[:, src],
                                                      a_cum[:, i, 2 * t + h:2 * t + h + 1], 0.0, ALU.subtract, ALU.min)
                ins.then_inc(seg_ready, 1)

            for m in range(XBC_UNITS):
                if m == 0:
                    dve.wait_ge(dt_psum, 1)
                    dve.wait_ge(small_here, 16 * 6)
                    ps = MISC[0][:, 0:TT * SSM_HEADS].rearrange("p (t h) -> p t h", t=TT)
                    link(nc.vector.tensor_tensor(dt_y, ps, dt_bias.unsqueeze(1).to_broadcast([P, TT, SSM_HEADS]), ALU.add))
                    link(nc.vector.tensor_scalar(dt_p, dt_y, -1.0, None, ALU.mult))
                    nc.vector.tensor_tensor(dt_s, dt_y, dt_p, ALU.max).then_inc(dt_args, 1)
                convolve(m)
                if m == 0:
                    step_sizes()
                if m == 2:
                    dve.wait_ge(a_cum_psum, 1)
                    nc.vector.tensor_copy(a_cum, MISC[1][:, 0:TT * SSM_HEADS].rearrange("p (t h) -> p t h", t=TT))
                    nc.vector.tensor_copy(a_cum_rows[0:SSM_HEADS, :], MISC[2][0:SSM_HEADS, 0:T]).then_inc(a_cum_ready, 1)
                    dve.wait_ge(a_cum_ready, 1)
                if m in (6, 7):
                    for g in (2 * (m - 6), 2 * (m - 6) + 1):
                        dve.wait_ge(cb_psum, g + 1)
                        nc.vector.tensor_tensor(cb[:, g], MISC[g % 2][:, 0:SEG], table("tri"), ALU.mult)\
                            .then_inc(cb_ready, 1)
                if m >= 6:
                    weigh_by_dt(m - 6)
            def group_normed(g):
                dve.wait_ge(group_rstd_ready, g + 1)
                for t in range(4 * g, 4 * g + 4):
                    nc.vector.scalar_tensor_tensor(out=xs[:, t], in0=xs[:, t], scalar=col("ssm_gnorm_w_2", t),
                                                   in1=group_rstd[:, g % 2], op0=ALU.mult, op1=ALU.mult)\
                        .then_inc(y_ready, 1)

            segments(0)
            segments(1)
            lower_to(first_block["z"] + 1)
            weigh_by_dt(6)
            weigh_by_dt(7)
            for t in range(Z_TILES):
                if t % 2 == 0 and t < Z_TILES - 2:
                    lower_to(first_block["z"] + t // 2 + 2)
                dve.wait_ge(y_psum, t + 1)
                nc.vector.scalar_tensor_tensor(out=xs[:, t], in0=xs[:, t], scalar=d_cols[:, t:t + 1],
                                               in1=(STAT, MISC[2])[t % 2][:, 0:T], op0=ALU.mult, op1=ALU.add)\
                    .then_inc(y_skipped, 1)
                if t + 2 < Z_TILES:
                    segments(t + 2)
                if t in (11, 15):
                    group_normed((t - 11) // 4)
            lower_to(first_block["ssm_out"] + 2)
            group_normed(2)
            for t in range(Z_TILES):
                if t == 8:
                    group_normed(3)
                lower_tiles("ssm_out", t, xs[:, t], y_high[:, t])

            def add_projection(phase):
                for n in range(4):
                    nc.vector.tensor_tensor(xT[:, 2 * n:2 * n + 2], xT[:, 2 * n:2 * n + 2], unit(phase, n), ALU.add)\
                        .then_inc(x_ready, 1)

            add_projection("ssm_out")

            def embedding(layer, norm):
                lower_to(first_block[f"ple_gate_{layer}"] + 1)
                split_norm(norm, "ple_norm_w_2", f"ple_gate_{layer}", 8 * layer)
                for n in range(4):
                    lower_to(first_block[f"ple_gate_{layer}"] + min(n + 2, 4))
                    dve.wait_ge(ple_sig, 4 * layer + n + 1)
                    g = ple_gate[:, n % 2].rearrange("p (k n) -> p k n", k=2)
                    a = ple_prod[:, 2 * n:2 * n + 2]
                    nc.vector.tensor_tensor(a, a, g, ALU.mult).then_inc(ple_mul, 1)
                    dve.wait_ge(ple_mul, 4 * layer + n + 1)
                    nc.vector.tensor_tensor(xT[:, 2 * n:2 * n + 2], xT[:, 2 * n:2 * n + 2], a, ALU.add)\
                        .then_inc(x_ready, 1)

            embedding(0, 6)

            lower_to(first_block["q"] + 1)
            plain_norm(7, "kv_norm_w_2", mixT)
            split_norm(7, "attn_norm_w_2", "q")

            def head_normed(m):
                dve.wait_ge(qk2_rstd, m + 1)
                for i in range(2):
                    a = qk2[:, 2 * m + i]
                    ins = nc.vector.scalar_tensor_tensor(out=a, in0=a, scalar=col("q_norm_w_2" if m else "k_norm_w_2", 0),
                                                         in1=head_rstd2[:, m % 2, T * i:T * i + T], op0=ALU.mult,
                                                         op1=ALU.mult)
                ins.then_inc(qk2_normed, 1)

            def rotate2(m):
                dve.wait_ge(qk2_swapped, m + 1)
                a, b = qk2[:, 2 * m:2 * m + 2], swap2[:, m % 2].rearrange("p (k n) -> p k n", k=2)
                nc.vector.tensor_tensor(a, a, rope_cos.unsqueeze(1).to_broadcast([P, 2, T]), ALU.mult)
                link(nc.vector.tensor_tensor(b, b, rope_sin.unsqueeze(1).to_broadcast([P, 2, T]), ALU.mult))
                nc.vector.tensor_tensor(a, a, b, ALU.add).then_inc(qk2_ready, 1)

            def masked(t):
                dve.wait_ge(s_psum, t + 1)
                if t >= 2:
                    dve.wait_ge(pt_psum, 2 * (t - 1))
                for h in range(2):
                    ins = nc.vector.scalar_tensor_tensor(out=probs[:, t % 2, h], in0=MISC[h][:, 0:SEG], scalar=64 ** -0.5,
                                                         in1=table("window"), op0=ALU.mult, op1=ALU.add)
                ins.then_inc(s_masked, 1)
                dve.wait_ge(s_masked, t + 1)
                for h in range(2):
                    for b, (lo, hi) in enumerate(((0, P), (P, SEG))):
                        ins = nc.vector.tensor_reduce(row_max[:, t, 2 * h + b:2 * h + b + 1], probs[:, t % 2, h, lo:hi],
                                                      AX.X, ALU.max)
                link(ins)
                sink = sinks[:, 2 * t:2 * t + 2].unsqueeze(2).to_broadcast([P, 2, 2])

                def by_head(x):
                    return x[:, t].rearrange("p (h b) -> p h b", h=2)

                link(nc.vector.tensor_tensor(by_head(row_max), by_head(row_max), sink, ALU.max))
                nc.vector.tensor_scalar(neg_max[:, t], row_max[:, t], -1.0, None, ALU.mult)
                nc.vector.tensor_tensor(by_head(sink_arg), sink, by_head(row_max), ALU.subtract).then_inc(s_max, 1)

            def normalised(t):
                dve.wait_ge(s_exp, t + 1)
                link(nc.vector.tensor_tensor(row_sum[:, t], row_sum[:, t], sink_exp[:, t], ALU.add))
                link(nc.vector.reciprocal(row_inv[:, t], row_sum[:, t]))
                for h in range(2):
                    for b, (lo, hi) in enumerate(((0, P), (P, SEG))):
                        i = 2 * h + b
                        a = probs[:, t % 2, h, lo:hi]
                        ins = nc.vector.tensor_scalar(a, a, row_inv[:, t, i:i + 1], None, ALU.mult)
                ins.then_inc(probs_ready, 1)

            def gated_output(t):
                dve.wait_ge(o_psum, t + 1)
                dve.wait_ge(g2_ready, t // 2 + 1)
                nc.vector.tensor_tensor(mixT[:, t],
                                        PS[(first_unit["gate"] + ATT_UNITS.index(("out", t))) % BANKS][:, 0:T], g2[:, t], ALU.mult).then_inc(o_ready, 1)

            for m in range(5):
                lower_to(first_block["q"] + m + 1)
                head_normed(m)
                if m >= 1:
                    rotate2(m - 1)
                if m == 3:
                    masked(0)
            masked(1)
            lower_to(first_block["gate"] + 2)
            for t in range(ATT_TILES):
                if t in (1, 3):
                    lower_to(first_block["gate"] + (t + 1) // 2 + 2)
                normalised(t)
                if t + 2 < ATT_TILES:
                    masked(t + 2)
                if t == 0:
                    rotate2(4)
                if t >= 1:
                    gated_output(t - 1)
                if t >= 4:
                    lower_tiles("attn_out", t - 4, mixT[:, t - 4], att_high[:, t - 4])
            lower_to(first_block["attn_out"] + 1)
            gated_output(ATT_TILES - 1)
            for t in range(4, ATT_TILES):
                lower_tiles("attn_out", t, mixT[:, t], att_high[:, t])
            add_projection("attn_out")
            embedding(1, 8)


N_STACK_LOADS = sum(2 if name in ("k_norm_w_2", "q_norm_w_2") else 1 for rows in STACKS for name, _ in rows)

INPUTS = [
    "x", "c", "norm_g", "ada_w", "ada_b", "w_in", "conv_w", "conv_b", "cln_g", "cln_b", "w_out", "s5_lam_re",
    "s5_lam_im", "s5_log_step", "s5_b_re", "s5_b_im", "s5_c_re", "s5_c_im", "s5_d", "w_glu_a", "w_glu_b", "w_fc1",
    "w_fc2", "norm_f", "p_2", "positions_2", "ssm_norm_w_2", "ssm_in_w_2", "ssm_conv_w_2", "ssm_conv_b_2",
    "ssm_dt_bias_2", "ssm_a_log_2", "ssm_d_2", "ssm_gnorm_w_2", "ssm_out_w_2", "kv_norm_w_2", "kv_w_2",
    "k_norm_w_2", "attn_norm_w_2", "attn_in_w_2", "q_norm_w_2", "attn_sinks_2", "attn_out_w_2", "ple_norm_w_2",
    "ple_gate_w_2", "ple_proj_w_2",
]


def build(nc, inputs):
    arrays, dram = {}, {}
    for name in INPUTS:
        a = np.ascontiguousarray(inputs[name])
        arrays[f"in_{name}"] = a
        dram[name] = nc.dram_tensor(f"in_{name}", a.shape, mybir.dt.from_np(a.dtype), kind="ExternalInput").ap()
    arrays["in_const"] = CONST
    dram["const"] = nc.dram_tensor("in_const", CONST.shape, F32, kind="ExternalInput").ap()
    dram["s5_d_flat"] = dram["s5_d"].rearrange("a n -> (a n)")
    for rows in STACKS:
        for name, count in rows:
            a = dram[name]
            if name in ("k_norm_w_2", "q_norm_w_2"):
                dram[name] = a if len(a.shape) == 2 else a.rearrange("(a n) -> a n", a=1)
                continue
            flat = a if len(a.shape) == 1 else a.rearrange(
                {2: "a b -> (a b)", 3: "a b c -> (a b c)"}[len(a.shape)])
            dram[name] = flat.rearrange("(r n) -> r n", n=P)
    dram["w_in"], dram["w_out"] = dram["w_in"][0], dram["w_out"][0]
    dram["glu_a"], dram["glu_b"] = dram["w_glu_a"][0], dram["w_glu_b"][0]
    for layer in range(2):
        dram[f"fc1_{layer}"], dram[f"fc2_{layer}"] = dram["w_fc1"][layer], dram["w_fc2"][layer]
        dram[f"ple_gate_{layer}"] = dram["ple_gate_w_2"][layer]
        dram[f"ple_proj_{layer}"] = dram["ple_proj_w_2"][layer].rearrange("(k p) n -> p k n", p=P)
    dram["ssm_in"], dram["ssm_out"], dram["kv"] = dram["ssm_in_w_2"][0], dram["ssm_out_w_2"][0], dram["kv_w_2"]
    dram["attn_in"], dram["attn_out"] = dram["attn_in_w_2"][0], dram["attn_out_w_2"][0]
    out = nc.dram_tensor("out", (1, T, D), F32, kind="ExternalOutput").ap()
    program(nc, dram, out)
    return arrays


def kernel(**inputs):
    import concourse.bacc as bacc
    from concourse.bass_utils import run_bass_kernel_spmd

    nc = bacc.Bacc("TRN2", target_bir_lowering=False, num_devices=1)
    arrays = build(nc, inputs)
    r = run_bass_kernel_spmd(nc, [arrays], core_ids=[0])
    return r.results[0]["out"]
```
